# Optimizing a Trainium2 kernel written in Bass

```python
import jax, jax.numpy as jnp
from jax import lax
import numpy as np

D_MODEL = 1024
BATCH = 1
SEQ = 1024
DEPTH = 2

CHUNK = 64
N_MIXERS = 2
N_A_LAYERS = (DEPTH + 1) // 2
N_B_LAYERS = DEPTH // 2
RMS_EPS = 1e-6

A_HEAD_DIM = 128
A_HEADS = D_MODEL // A_HEAD_DIM
A_SUB = 16
A_NSUB = CHUNK // A_SUB

B_HEAD_DIM = 64
B_Q_HEADS = D_MODEL // B_HEAD_DIM
B_KV_HEADS = 2
B_GROUP = B_Q_HEADS // B_KV_HEADS
B_KV_WIDTH = B_KV_HEADS * B_HEAD_DIM
WINDOW = 128
WINDOW_CHUNKS = WINDOW // CHUNK
B_IN_WIDTH = D_MODEL + 2 * B_KV_WIDTH + D_MODEL

kernel_name = "hybrid_hgrn2_swa_sink_alibi_sandwich"

def rmsnorm(x, gain):
    xf = x.astype(jnp.float32)
    y = xf * lax.rsqrt(jnp.mean(xf * xf, axis=-1, keepdims=True) + RMS_EPS)
    return (y * gain.astype(jnp.float32)).astype(x.dtype)

def hgrn_lower_bounds(lb_logits):
    p = jax.nn.softmax(lb_logits.astype(jnp.float32), axis=0)
    return jnp.maximum(jnp.cumsum(p, axis=0) - p[0:1], 0.0)

def hgrn2_mixer(h, w_in, lower_bound, gn_gain, w_out):
    bsz, seq, _ = h.shape
    n_chunks = seq // CHUNK
    proj = h @ w_in
    q_raw, f_raw, i_raw, gate = jnp.split(proj, 4, axis=-1)

    def to_heads(t):
        return t.reshape(bsz, n_chunks, CHUNK, A_HEADS, A_HEAD_DIM).transpose(0, 3, 1, 2, 4).astype(jnp.float32)

    q = jax.nn.silu(to_heads(q_raw))
    f_pre = to_heads(f_raw)
    v = to_heads(i_raw)
    lb = lower_bound.astype(jnp.float32).reshape(A_HEADS, 1, 1, A_HEAD_DIM)
    log_f = jnp.logaddexp(jnp.log(lb), jnp.log1p(-lb) + jax.nn.log_sigmoid(f_pre))
    k = (1.0 - lb) * jax.nn.sigmoid(-f_pre)
    b = jnp.cumsum(log_f, axis=3)

    pos = np.arange(CHUNK)
    starts = np.arange(A_NSUB) * A_SUB
    ref = b[:, :, :, ::A_SUB, :]
    sub_shape = (bsz, A_HEADS, n_chunks, A_NSUB, A_SUB, A_HEAD_DIM)
    q_hat = q.reshape(sub_shape) * jnp.exp(b.reshape(sub_shape) - ref[:, :, :, :, None, :])
    keep = jnp.asarray(pos[None, :] < (starts[:, None] + A_SUB))
    expo = jnp.where(keep[:, :, None], ref[:, :, :, :, None, :] - b[:, :, :, None, :, :], 0.0)
    k_hat = k[:, :, :, None] * jnp.exp(expo)
    scores = jnp.einsum('bhnisd,bhnicd->bhnisc', q_hat, k_hat)
    causal = jnp.asarray((pos[:, None] >= pos[None, :]).reshape(A_NSUB, A_SUB, CHUNK))
    scores = jnp.where(causal, scores, 0.0)
    o_intra = jnp.einsum('bhnisc,bhncv->bhnisv', scores, v).reshape(bsz, A_HEADS, n_chunks, CHUNK, A_HEAD_DIM)

    b_last = b[:, :, :, -1, :]
    k_dec = k * jnp.exp(b_last[:, :, :, None, :] - b)
    u = jnp.einsum('bhncd,bhncv->bhndv', k_dec, v)

    def step(state, inp):
        decay, upd = inp
        return decay[..., None] * state + upd, state

    state0 = jnp.zeros((bsz, A_HEADS, A_HEAD_DIM, A_HEAD_DIM), jnp.float32)
    _, s_prev = lax.scan(step, state0, (jnp.moveaxis(jnp.exp(b_last), 2, 0), jnp.moveaxis(u, 2, 0)))
    s_prev = jnp.moveaxis(s_prev, 0, 2)
    o_inter = jnp.einsum('bhncd,bhndv->bhncv', q * jnp.exp(b), s_prev)
    o = o_inter + o_intra

    o = o * lax.rsqrt(jnp.mean(o * o, axis=-1, keepdims=True) + RMS_EPS)
    o = o * gn_gain.astype(jnp.float32).reshape(A_HEADS, 1, 1, A_HEAD_DIM)
    o = o.transpose(0, 2, 3, 1, 4).reshape(bsz, seq, D_MODEL).astype(h.dtype)
    return (o * jax.nn.silu(gate)) @ w_out

def alibi_slopes():
    h = np.arange(1, B_Q_HEADS + 1, dtype=np.float32)
    return jnp.asarray((2.0 ** (-8.0 * h / B_Q_HEADS)).astype(np.float32).reshape(B_KV_HEADS, B_GROUP))

def swa_sink_mixer(h, w_in, sinks, w_out):
    bsz, seq, _ = h.shape
    n_chunks = seq // CHUNK
    band_len = WINDOW_CHUNKS * CHUNK
    proj = h @ w_in
    q, k, v, gate = jnp.split(proj, [D_MODEL, D_MODEL + B_KV_WIDTH, D_MODEL + 2 * B_KV_WIDTH], axis=-1)
    q = q.reshape(bsz, n_chunks, CHUNK, B_KV_HEADS, B_GROUP, B_HEAD_DIM).astype(jnp.float32)
    k = k.reshape(bsz, n_chunks, CHUNK, B_KV_HEADS, B_HEAD_DIM)
    v = v.reshape(bsz, n_chunks, CHUNK, B_KV_HEADS, B_HEAD_DIM)

    def band(t):
        padded = jnp.pad(t, ((0, 0), (WINDOW_CHUNKS - 1, 0), (0, 0), (0, 0), (0, 0)))
        return jnp.concatenate([padded[:, j:j + n_chunks] for j in range(WINDOW_CHUNKS)], axis=2)

    kb = band(k).astype(jnp.float32)
    vb = band(v)
    logits = jnp.einsum('bnqhgd,bnshd->bnhgqs', q, kb) * (B_HEAD_DIM ** -0.5)
    q_in = np.arange(CHUNK)[:, None]
    s_in = np.arange(band_len)[None, :]
    dist = jnp.asarray(np.abs(q_in + (WINDOW_CHUNKS - 1) * CHUNK - s_in).astype(np.float32))
    logits = logits - alibi_slopes()[:, :, None, None] * dist
    key_chunk = np.arange(n_chunks)[:, None] - (WINDOW_CHUNKS - 1) + np.arange(band_len)[None, :] // CHUNK
    valid = jnp.asarray(key_chunk >= 0)
    logits = jnp.where(valid[None, :, None, None, None, :], logits, -jnp.inf)
    sink = sinks.astype(jnp.float32).reshape(1, 1, B_KV_HEADS, B_GROUP, 1, 1)
    m = jnp.maximum(jnp.max(logits, axis=-1, keepdims=True), sink)
    e = jnp.exp(logits - m)
    p = e / (jnp.sum(e, axis=-1, keepdims=True) + jnp.exp(sink - m))
    out = jnp.einsum('bnhgqs,bnshd->bnqhgd', p.astype(vb.dtype), vb)
    out = out.reshape(bsz, seq, D_MODEL).astype(h.dtype)
    return (out * jax.nn.silu(gate)) @ w_out

def setup_inputs(seed: int = 0) -> dict:
    key = jax.random.key(seed)
    ks = jax.random.split(key, 12)
    s = D_MODEL ** -0.5
    return {
        "x": jax.random.normal(ks[0], (BATCH, SEQ, D_MODEL), jnp.float32),
        "norm_pre": 1.0 + 0.02 * jax.random.normal(ks[1], (DEPTH, D_MODEL), jnp.float32),
        "norm_post": 1.0 + 0.02 * jax.random.normal(ks[2], (DEPTH, D_MODEL), jnp.float32),
        "a_w_in": s * jax.random.normal(ks[3], (N_A_LAYERS, D_MODEL, 4 * D_MODEL), jnp.float32),
        "a_lb_logits": 0.5 * jax.random.normal(ks[4], (N_A_LAYERS, D_MODEL), jnp.float32),
        "a_norm": 1.0 + 0.02 * jax.random.normal(ks[5], (N_A_LAYERS, D_MODEL), jnp.float32),
        "a_w_out": s * jax.random.normal(ks[6], (N_A_LAYERS, D_MODEL, D_MODEL), jnp.float32),
        "b_w_in": s * jax.random.normal(ks[7], (N_B_LAYERS, D_MODEL, B_IN_WIDTH), jnp.float32),
        "b_sinks": 0.5 * jax.random.normal(ks[8], (N_B_LAYERS, B_Q_HEADS), jnp.float32),
        "b_w_out": s * jax.random.normal(ks[9], (N_B_LAYERS, D_MODEL, D_MODEL), jnp.float32),
    }

def reference(x, norm_pre, norm_post, a_w_in, a_lb_logits, a_norm, a_w_out, b_w_in, b_sinks, b_w_out):
    lower_bounds = hgrn_lower_bounds(a_lb_logits)
    for layer in range(DEPTH):
        h = rmsnorm(x, norm_pre[layer])
        j = layer // N_MIXERS
        if layer % N_MIXERS == 0:
            y = hgrn2_mixer(h, a_w_in[j], lower_bounds[j], a_norm[j], a_w_out[j])
        else:
            y = swa_sink_mixer(h, b_w_in[j], b_sinks[j], b_w_out[j])
        x = x + rmsnorm(y, norm_post[layer])
    return x


_drawn_inputs = setup_inputs


def setup_inputs(seed=0):
    import zlib

    import numpy as np

    out = dict(_drawn_inputs(seed))
    spreads = {}
    factors = {'a_norm': 2.851, 'b_sinks': 3.059}
    for name, (base, spread) in spreads.items():
        noise = np.random.default_rng([zlib.crc32(name.encode()), seed]).standard_normal(out[name].shape)
        drawn = base * np.exp(spread * noise) if base else spread * noise
        out[name] = __import__('jax').numpy.asarray(drawn.astype(out[name].dtype))
    for name, factor in factors.items():
        out[name] = (out[name] * factor).astype(out[name].dtype)
    return out
```

```python
from collections import namedtuple

import numpy as np

import concourse.bass as bass
from concourse import mybir

F32 = mybir.dt.float32
F32R = mybir.dt.float32r
I32 = mybir.dt.int32
ALU = mybir.AluOpType
ACT = mybir.ActivationFunctionType
AX_X = mybir.AxisListType.X

P = 128
D = 1024
T = 1024
KB = D // P
TB = T // P
HALF = 512
EPS = 1e-6

CHUNK = 64
NCH = T // CHUNK
NPAIR = NCH // 2
SUB = 16
HEADS = D // P
A_BLOCKS = 4
A_COLUMN = (D, 0, 3 * D, 2 * D)

DH = 64
KV = 2
NJ = 4
B_KV_BLOCKS = 2
GATE_COLUMN = D + 2 * KV * DH
MASKED = -1.0e30

FIRST_A = 0
FIRST_AO = FIRST_A + A_BLOCKS * HEADS
FIRST_B = FIRST_AO + KB
FIRST_BO = FIRST_B + B_KV_BLOCKS + 4 * NJ
BLK_B = A_BLOCKS * HEADS
BLK_END = BLK_B + B_KV_BLOCKS + 4 * NJ


def build(nc, x, norm_pre, norm_post, a_w_in, a_lb_logits, a_norm, a_w_out, b_w_in, b_sinks,
          b_w_out, identity, score_masks, alibi, out, x1_store):
    ds = bass.ds

    at = [(nc.sbuf_base + 31) // 32 * 32]

    def sb(name, shape, dt=F32, offset=None):
        size = int(np.prod(shape[1:])) * 4
        if offset is None:
            offset = at[0]
            at[0] += (size + 31) // 32 * 32
        return nc.alloc_sbuf_tensor_at(name, shape, dt, offset=offset)

    KIB = 1024
    ident = sb("ident", [P, P])
    ones = sb("ones", [P, P])
    masks = sb("masks", [P, 3, P], I32)
    lb_col = sb("lb_col", [P, HEADS])
    lb_tmp = sb("lb_tmp", [P, HEADS])
    log1mlb_col = sb("log1mlb_col", [P, HEADS])
    gn_col = sb("gn_col", [P, HEADS])
    sink = sb("sink", [P, NJ, 2])
    ssq = sb("ssq", [P, 4])
    rms = sb("rms", [P, 4])
    chunk_decay = sb("chunk_decay", [P, NPAIR, 2])
    pair_decay = sb("pair_decay", [P, NPAIR])
    row_max = sb("row_max", [P, 2, 8])
    sink_exp = sb("sink_exp", [P, 2, 8])
    row_sum = sb("row_sum", [P, 2, 8])
    eps_col = sb("eps_col", [P, 1])
    one_col = sb("one_col", [P, 1])
    mixed = sb("mixed", [P, KB, T])
    w_raw = sb("w_raw", [P, 2, KB, P])
    split_hi = sb("split_hi", [P, 2, KB, P], F32R)
    split_lo = sb("split_lo", [P, 2, KB, P], F32R)

    zone1 = at[0]
    zone2 = zone1 + 64 * KIB
    zone_end = zone2 + 80 * KIB
    assert zone_end <= nc.sbuf_usable_end, (zone_end, nc.sbuf_usable_end)

    def zoned(zone):
        off = [zone]

        def take(name, shape, dt=F32):
            t = sb(name, shape, dt, offset=off[0])
            off[0] += int(np.prod(shape[1:])) * 4
            return t
        return take

    z = zoned(zone1)
    hA_hi, hA_lo = z("hA_hi", [P, KB, T], F32R), z("hA_lo", [P, KB, T], F32R)
    z = zoned(zone1)
    woA_hi, woA_lo = z("woA_hi", [P, KB, D], F32R), z("woA_lo", [P, KB, D], F32R)
    z = zoned(zone1)
    q_even, q_odd = (z(n, [P, NCH, 2, CHUNK]) for n in ("q_even", "q_odd"))
    k_raw = z("k_raw", [P, T])
    v_raw = z("v_raw", [P, T])
    k_both = z("k_both", [P, KV, T])
    v_tok = z("v_tok", [P, TB, P])
    v_swap = z("v_swap", [P, TB, P])
    k_band = z("k_band", [P, NCH, P])
    v_band = z("v_band", [P, NCH, DH])
    logits = z("logits", [P, 2, 4, 2, P])
    probs_t = z("probs_t", [P, 4, 2, P])
    z = zoned(zone2 + 4 * KIB * 12)
    x_in = z("x_in", [P, 2, D])
    x_scaled = z("x_scaled", [P, 2, D])
    gain_in = z("gain_in", [P, D])
    z = zoned(zone2)
    k1, k2, k3 = (z(n, [P, NCH, CHUNK]) for n in ("k1", "k2", "k3"))
    q1, q3 = (z(n, [P, NCH, CHUNK]) for n in ("q1", "q3"))
    scores = z("scores", [P, NPAIR, P])
    k_dec_a = z("k_dec_a", [P, NPAIR, CHUNK])
    q_dec_b = z("q_dec_b", [P, NPAIR, CHUNK])
    k_dec = z("k_dec", [P, T])
    q_dec = z("q_dec", [P, T])
    val = z("val", [P, T])
    state = z("state", [P, NPAIR - 1, P])
    z = zoned(zone2 + 4 * KIB * 12)
    tmp1, tmp2, tmp3, rstd = (z(n, [P, T]) for n in ("tmp1", "tmp2", "tmp3", "rstd"))
    silu_q = z("silu_q", [P, T])
    b_cum = z("b_cum", [P, T])
    k_gate = z("k_gate", [P, T])
    scan_keep = z("scan_keep", [P, T])
    z = zoned(zone2)
    hB_hi, hB_lo = z("hB_hi", [P, KB, T], F32R), z("hB_lo", [P, KB, T], F32R)
    z = zoned(zone2)
    woB_hi, woB_lo = z("woB_hi", [P, KB, D], F32R), z("woB_lo", [P, KB, D], F32R)
    z = zoned(zone2 + 64 * KIB)
    gain_post = z("gain_post", [P, D])
    gain_pre = z("gain_pre", [P, D])
    y_norm = z("y_norm", [P, 2, D])
    z = zoned(zone2 + 64 * KIB)
    bias = z("bias", [P, NJ, 4 * P])
    gain_last = z("gain_last", [P, D])
    z = zoned(zone2 + 64 * KIB)
    y_last = z("y_last", [P, 2, D])

    ps = nc.alloc_psum_tensor("ps", [P, 8, HALF], F32)
    proj_ps = [ps[:, 0:2, :], ps[:, 2:4, :]]
    mix_ps = [ps[:, 4:6, :], ps[:, 6:8, :]]

    def flat(ap):
        return ap.rearrange("p a b -> p (a b)")

    names = """
        const_loaded gain_in_loaded gains_loaded bias_loaded gain_last_loaded k_both_loaded resid_stored out_stored
        x_in_loaded0 x_in_loaded1 raw_loaded0 raw_loaded1 resid_loaded0 resid_loaded1
        ones_set zeros_set keep_ones keep_set cols_set
        bound_shifted bound_exped bound_inverse bound_prob bound_ready bound_logged
        in_squared in_logged in_rms_ready in_scaled in_turned in_hi_ready in_lo_ready
        hi_ready lo_ready block_done
        f_abs f_exp f_log f_neg_ready f_neg_exp f_neg_log log_f_ready log_nf_ready k_gate_ready
        log_f_full b_ready silu_q_ready gate_ready val_ready val_turned val_tok_ready
        k_dec_turned k_dec_tok_ready d3_ready e3q_ready e3k_ready q3_ready k3_ready d21_ready e21_ready
        k2_ready k1_ready dq1_ready eq1_ready q1_ready eb_ready dkd_ready ekd_ready decay_ready
        pair_decay_ready q_dec_b_ready q_dec_ready k_dec_a_ready k_dec_ready
        level3_done level2_done level1_done level0_done level3_kept level2_kept level1_kept level0_kept
        update_done state_step o_done o_squared mean_done mean_logged rstd_ready o_scaled mixed_ready
        mix_hi_ready mix_lo_ready out_tile_done y_squared y_logged y_rms y_scaled x1_ready
        x1_squared x1_logged x1_rms h_scaled h_turned h_hi_ready h_lo_ready
        k_raw_ready v_raw_ready v_turned v_tok_ready zeroB_set q_even_ready q_odd_ready
        k_band_ready v_swap_ready v_band_ready logits_done biased edge_masked max_part max_ready shifted exped
        sink_shifted sink_exped sum_part sum_ready inverse_ready probs_ready probs_turned
        probs_t_ready pv_done o_ready
    """.split()
    S = namedtuple("Semaphores", names)(*(nc.alloc_semaphore(n) for n in names))
    raw_loaded = (S.raw_loaded0, S.raw_loaded1)
    x_in_loaded = (S.x_in_loaded0, S.x_in_loaded1)
    resid_loaded = (S.resid_loaded0, S.resid_loaded1)

    def first(value):
        return isinstance(value, int) and value == 0

    def row_tile(dram, t):
        return dram[0, ds(t * P, P), :].rearrange("p (k n) -> p k n", k=KB)

    def mixed_tile(t):
        return mixed[:, :, ds(t * P, P)]

    def gain_row(gains, layer):
        return gains[layer, :].partition_broadcast(P)

    def chunks(buf):
        return buf[:].rearrange("p (n c) -> p n c", c=CHUNK)

    def by_chunk(banks):
        return flat(banks).rearrange("p (n c) -> p n c", c=CHUNK)

    def halves(buf):
        return buf[:].rearrange("p (r e c) -> p r e c", e=2, c=CHUNK)

    def subs(buf):
        return buf[:].rearrange("p (n c) -> p n c", c=SUB)

    mix_flat = [flat(m) for m in mix_ps]

    with nc.Block() as block:

        @block.sync
        def _(sp):
            a_cols = a_w_in[0].rearrange("(k p) n -> p k n", p=P)
            b_cols = b_w_in[0].rearrange("(k p) n -> p k n", p=P)

            def load(slot, source, n):
                if not (isinstance(n, int) and n < 2):
                    sp.wait_ge(raw_loaded[slot], 16)
                    sp.wait_ge(S.lo_ready, n - 1)
                sp.dma_start(w_raw[:, slot], source).then_inc(raw_loaded[slot], 16)

            def a_head(h):
                for j in range(A_BLOCKS):
                    column = h * P + A_COLUMN[j]
                    if not first(h):
                        column = sp.snap(column)
                    load(j % 2, a_cols[:, :, ds(column, P)], h * A_BLOCKS + (FIRST_A + j))

            def out_weights(w, n):
                for k in range(KB):
                    load(k % 2, w[0, k * P:(k + 1) * P, :].rearrange("p (a b) -> p a b", a=KB), n + k)

            a_head(0)
            with sp.Fori(1, HEADS) as h:
                a_head(h)
            out_weights(a_w_out, FIRST_AO)
            load(0, b_cols[:, :, D:D + P], FIRST_B)
            load(1, b_cols[:, :, D + P:D + 2 * P], FIRST_B + 1)
            with sp.Fori(1, NJ + 1) as i:
                for j in range(4):
                    column = i * 2 * P + ((GATE_COLUMN if j < 2 else 0) + (j % 2) * P - 2 * P)
                    load(j % 2, b_cols[:, :, ds(column, P)], i * 4 + (FIRST_B - 2 + j))
            out_weights(b_w_out, FIRST_BO)

        @block.gpsimd
        def _(pool):
            def load_x(t, slot):
                pool.dma_start(x_in[:, slot], x[0, ds(t * P, P), :]).then_inc(x_in_loaded[slot], 16)

            load_x(0, 0)
            load_x(1, 1)
            pool.dma_start(gain_in[:], gain_row(norm_pre, 0)).then_inc(S.gain_in_loaded, 16)
            pool.dma_start(ident[:], identity).then_inc(S.const_loaded, 16)
            pool.dma_start(masks[:], score_masks).then_inc(S.const_loaded, 16)
            with nc.allow_non_contiguous_dma("columns of 1024 numbers"):
                pool.dma_start(lb_tmp[:], a_lb_logits[0].rearrange("(h p) -> p h", p=P))\
                    .then_inc(S.const_loaded, 16)
                pool.dma_start(gn_col[:], a_norm[0].rearrange("(h p) -> p h", p=P))\
                    .then_inc(S.const_loaded, 16)
                for blk in range(2):
                    pool.dma_start(sink[blk * DH:(blk + 1) * DH],
                                   b_sinks[0].rearrange("(j b e) -> b j e", j=NJ, b=2)[blk]
                                   .partition_broadcast(DH)).then_inc(S.const_loaded, 16)
            pool.memset(ones[:], 1.0 / P).then_inc(S.ones_set, 1)
            for t in (k1, k2, q1, scores):
                pool.memset(t[:], 0.0).then_inc(S.zeros_set, 1)
            with pool.Fori(1, TB // 2) as i:
                for slot in range(2):
                    pool.wait_ge(S.in_scaled, i * 2 + (slot - 1))
                    load_x(i * 2 + slot, slot)

            pool.wait_ge(S.mixed_ready, HEADS)
            pool.dma_start(gain_post[:], gain_row(norm_post, 0)).then_inc(S.gains_loaded, 16)
            pool.dma_start(gain_pre[:], gain_row(norm_pre, 1)).then_inc(S.gains_loaded, 16)

            def load_resid(source, layer, t, slot):
                pool.wait_ge(S.mix_lo_ready, t + (TB * layer + 1))
                pool.dma_start(mixed_tile(t), row_tile(source, t)).then_inc(resid_loaded[slot], 16)

            def store(target, layer, t, stored):
                pool.wait_ge(S.x1_ready, t + (TB * layer + 1))
                pool.dma_start(row_tile(target, t), mixed_tile(t)).then_inc(stored, 16)

            for slot in range(2):
                load_resid(x, 0, slot, slot)
            with pool.Fori(1, TB // 2) as i:
                for slot in range(2):
                    load_resid(x, 0, i * 2 + slot, slot)
                    store(x1_store, 0, i * 2 + (slot - 2), S.resid_stored)
            for t in range(TB - 2, TB):
                store(x1_store, 0, t, S.resid_stored)

            pool.wait_ge(S.out_tile_done, TB)
            pool.memset(q_even[:], 0.0).then_inc(S.zeroB_set, 1)
            pool.memset(q_odd[:], 0.0).then_inc(S.zeroB_set, 1)
            pool.memset(k_band[:, 0, :], 0.0).then_inc(S.zeroB_set, 1)
            pool.memset(v_swap[:, 0, :], 0.0).then_inc(S.zeroB_set, 1)
            pool.wait_ge(S.h_turned, TB)
            pool.dma_start(bias[:], alibi).then_inc(S.bias_loaded, 16)
            pool.dma_start(gain_last[:], gain_row(norm_post, 1)).then_inc(S.gain_last_loaded, 16)
            pool.wait_ge(S.k_raw_ready, 1)
            for g in range(KV):
                for half in range(2):
                    pool.dma_start(k_both[half * DH:(half + 1) * DH, g, :], k_raw[g * DH:(g + 1) * DH, :])\
                        .then_inc(S.k_both_loaded, 16)
            pool.wait_ge(S.k_both_loaded, 16 * 4)
            pool.wait_ge(S.v_tok_ready, 1)
            pool.wait_ge(S.zeroB_set, 4)
            pool.tensor_copy(v_swap[0:DH], v_tok[0:DH]).then_inc(S.v_swap_ready, 1)
            pool.wait_ge(S.v_swap_ready, 1)
            pool.tensor_copy(v_swap[DH:P, 1:TB, :], v_tok[DH:P, 0:TB - 1, :]).then_inc(S.v_swap_ready, 1)
            pool.wait_ge(S.v_swap_ready, 2)

            def bands(p):
                g = p // 2
                keys = k_both[:, ds(g, 1), :].rearrange("p a (n c) -> p (a n) c", c=CHUNK)
                if not first(p):
                    pool.wait_ge(S.logits_done, p * 4)
                pool.tensor_copy(k_band[:, 1:NCH:2, 0:CHUNK], keys[:, 0:NCH:2, :])
                pool.tensor_copy(k_band[:, 1:NCH:2, CHUNK:P], keys[:, 1:NCH:2, :])
                pool.tensor_copy(k_band[:, 0:NCH:2, 0:CHUNK], keys[:, 0:NCH:2, :])
                pool.tensor_copy(k_band[:, 2:NCH:2, CHUNK:P], keys[:, 1:NCH - 2:2, :])\
                    .then_inc(S.k_band_ready, 1)
                if not first(p):
                    pool.wait_ge(S.pv_done, p * 4)
                cols = ds(g * DH, DH)
                pool.tensor_copy(v_band[:, 1:NCH:2, :], v_tok[:, :, cols])
                pool.tensor_copy(v_band[:, 0:NCH:2, :], v_swap[:, :, cols]).then_inc(S.v_band_ready, 1)

            bands(0)
            with pool.Fori(1, NJ) as p:
                bands(p)

            pool.wait_ge(S.resid_stored, 16 * TB)
            pool.wait_ge(S.o_ready, 4 * NJ)
            for slot in range(2):
                load_resid(x1_store, 1, slot, slot)
            with pool.Fori(1, TB // 2) as i:
                for slot in range(2):
                    load_resid(x1_store, 1, i * 2 + slot, slot)
                    store(out, 1, i * 2 + (slot - 2), S.out_stored)
            for t in range(TB - 2, TB):
                store(out, 1, t, S.out_stored)
            pool.wait_ge(S.out_stored, 16 * TB)

        @block.tensor
        def _(pe):
            def turn(src, dst):
                for k in range(KB):
                    last = pe.transpose(dst[:, k * P:(k + 1) * P], src[:, k * P:(k + 1) * P], ident[:])
                return last

            def three_pass(dst, w_hi, w_lo, v_hi, v_lo, start, stop):
                pe.matmul(dst, w_hi, v_hi, start=start, stop=False)
                pe.matmul(dst, w_lo, v_hi, start=False, stop=False)
                return pe.matmul(dst, w_hi, v_lo, start=False, stop=stop)

            def project(slot, half, h_hi, h_lo):
                toks = slice(half * HALF, (half + 1) * HALF)
                for k in range(KB):
                    last = three_pass(proj_ps[slot][:, half, :], split_hi[:, slot, k, :], split_lo[:, slot, k, :],
                                      h_hi[:, k, toks], h_lo[:, k, toks], k == 0, k == KB - 1)
                return last

            pe.wait_ge(S.const_loaded, 16 * 6)

            def turn_in(t, slot):
                pe.wait_ge(S.in_scaled, t + 1)
                turn(x_scaled[:, slot], mix_flat[slot]).then_inc(S.in_turned, 1)

            for t in range(2):
                turn_in(t, t)
            with pe.Fori(1, TB // 2) as i:
                for slot in range(2):
                    turn_in(i * 2 + slot, slot)
            pe.wait_ge(S.ones_set, 1)
            pe.wait_ge(S.zeros_set, 4)

            def turn_values(p):
                pe.wait_ge(S.val_ready, p + 1)
                turn(val, mix_flat[0]).then_inc(S.val_turned, 1)

            def turn_keys(p):
                pe.wait_ge(S.k_dec_ready, p + 1)
                turn(k_dec, mix_flat[1]).then_inc(S.k_dec_turned, 1)

            def level(k, q, dst, done):
                for r in range(NPAIR):
                    last = pe.matmul(dst[:, r * P:(r + 1) * P], flat(k[:])[:, r * P:(r + 1) * P],
                                     flat(q[:])[:, r * P:(r + 1) * P], start=True, stop=True)
                last.then_inc(done, 1)

            def level3(p):
                pe.wait_ge(S.q3_ready, p + 1)
                pe.wait_ge(S.k3_ready, p + 1)
                pe.wait_ge(S.val_tok_ready, p + 1)
                level(k3, q3, mix_flat[0], S.level3_done)

            def updates(p):
                pe.wait_ge(S.val_tok_ready, p + 1)
                pe.wait_ge(S.k_dec_tok_ready, p + 1)
                for r in range(NPAIR - 1):
                    cols = slice(r * P, (r + 1) * P)
                    last = pe.matmul(mix_flat[1][:, cols], k_dec[:, cols], val[:, cols], start=True, stop=True)
                last.then_inc(S.update_done, 1)

            def level2(p):
                pe.wait_ge(S.k2_ready, p + 1)
                pe.wait_ge(S.level3_kept, p + 1)
                level(k2, q3, mix_flat[0], S.level2_done)

            def level1(p):
                pe.wait_ge(S.k1_ready, p + 1)
                pe.wait_ge(S.q1_ready, p + 1)
                pe.wait_ge(S.state_step, p * (NPAIR - 1) + (NPAIR - 1))
                level(k1, q1, mix_flat[1], S.level1_done)

            def level0(p):
                pe.wait_ge(S.k_dec_a_ready, p + 1)
                pe.wait_ge(S.q_dec_b_ready, p + 1)
                pe.wait_ge(S.level2_kept, p + 1)
                for r in range(NPAIR):
                    last = pe.matmul(mix_ps[0][0:CHUNK, 0, r * CHUNK:(r + 1) * CHUNK], k_dec_a[:, r, :],
                                     q_dec_b[:, r, :], start=True, stop=True)
                last.then_inc(S.level0_done, 1)

            def outputs(p):
                pe.wait_ge(S.level1_kept, p + 1)
                pe.wait_ge(S.level0_kept, p + 1)
                pe.wait_ge(S.q_dec_ready, p + 1)
                for r in range(NPAIR):
                    cols = slice(r * P, (r + 1) * P)
                    last = pe.matmul(mix_flat[1][:, cols], val[:, cols], scores[:, r, :], start=True, stop=r == 0)
                    if r:
                        last = pe.matmul(mix_flat[1][:, cols], state[:, r - 1, :], q_dec[:, cols],
                                         start=False, stop=True)
                last.then_inc(S.o_done, 1)

            def means(p):
                pe.wait_ge(S.o_squared, p + 1)
                for half in range(2):
                    last = pe.matmul(mix_ps[0][:, half, :], ones[:], rstd[:, half * HALF:(half + 1) * HALF],
                                     start=True, stop=True)
                last.then_inc(S.mean_done, 1)

            def head_projections(h, between):
                free = ((S.gate_ready, 0), (S.val_ready, 0), (S.log_nf_ready, 1), (S.silu_q_ready, 1))
                for j in range(A_BLOCKS):
                    pe.wait_ge(S.lo_ready, h * A_BLOCKS + (j + 1))
                    sem, plus = free[j]
                    if plus or not first(h):
                        pe.wait_ge(sem, h + plus)
                    if j == 2:
                        pe.wait_ge(S.f_abs, h + 1)
                    for half in range(2):
                        if first(h) and j == 0:
                            pe.wait_ge(S.in_lo_ready, TB // 2 * (half + 1))
                        last = project(j % 2, half, hA_hi, hA_lo)
                        if half == 1:
                            last.then_inc(S.block_done, 1)
                        for step in between[2 * j + half]:
                            step(h - 1)

            steps = ((turn_values, turn_keys), (level3, updates), (level2, level1), (level0,), (outputs,),
                     (means,), (), ())
            head_projections(0, ((),) * 8)
            with pe.Fori(1, HEADS) as h:
                head_projections(h, steps)
            for group in steps:
                for step in group:
                    step(HEADS - 1)

            def out_tile(layer, t, slot, weights, free):
                pe.wait_ge(S.mix_lo_ready, t + (TB * layer + 1))
                for sem, value in free:
                    pe.wait_ge(sem, value)
                first_weight = (FIRST_AO, FIRST_BO)[layer]
                w_hi, w_lo = weights
                for half in range(2):
                    cols = slice(half * HALF, (half + 1) * HALF)
                    for k in range(KB):
                        if first(t) and half == 0:
                            pe.wait_ge(S.lo_ready, first_weight + k + 1)
                        last = three_pass(proj_ps[slot][:, half, :], split_hi[:, slot, k, :], split_lo[:, slot, k, :],
                                          w_hi[:, k, cols], w_lo[:, k, cols], k == 0, k == KB - 1)
                last.then_inc(S.out_tile_done, 1)

            def turn_h(t, slot):
                pe.wait_ge(S.h_scaled, t + 1)
                turn(y_norm[:, slot], mix_flat[slot]).then_inc(S.h_turned, 1)

            woA, woB = (woA_hi, woA_lo), (woB_hi, woB_lo)
            out_tile(0, 0, 0, woA, ((S.gate_ready, HEADS),))
            out_tile(0, 1, 1, woA, ((S.val_ready, HEADS),))
            turn_h(0, 0)
            with pe.Fori(1, TB // 2) as i:
                out_tile(0, i * 2, 0, woA, ((S.y_scaled, i * 2 - 1),))
                turn_h(i * 2 - 1, 1)
                out_tile(0, i * 2 + 1, 1, woA, ((S.y_scaled, i * 2),))
                turn_h(i * 2, 0)

            pe.wait_ge(S.lo_ready, FIRST_B + 1)
            pe.wait_ge(S.y_scaled, TB - 1)
            pe.wait_ge(S.h_lo_ready, TB // 2)
            project(0, 0, hB_hi, hB_lo)
            turn_h(TB - 1, 1)
            pe.wait_ge(S.h_lo_ready, TB)
            project(0, 1, hB_hi, hB_lo).then_inc(S.block_done, 1)
            pe.wait_ge(S.lo_ready, FIRST_B + 2)
            pe.wait_ge(S.y_scaled, TB)
            for half in range(2):
                last = project(1, half, hB_hi, hB_lo)
            last.then_inc(S.block_done, 1)
            pe.wait_ge(S.v_raw_ready, 1)

            def logits_of(p, c):
                if c == 0:
                    pe.wait_ge(S.q_even_ready, p * 2 + 2)
                    pe.wait_ge(S.q_odd_ready, p * 2 + 2)
                    pe.wait_ge(S.k_band_ready, p + 1)
                elif c < 3:
                    pe.wait_ge(S.biased, p * 4 + c)
                else:
                    pe.wait_ge(S.o_ready, p * 4 + 1)
                for n in range(4):
                    for e, q in enumerate((q_even, q_odd)):
                        col = (2 * n + e) * P
                        last = pe.matmul(mix_flat[0][:, col:col + P], q[:, 4 * c + n].rearrange("p b q -> p (b q)"),
                                         k_band[:, 4 * c + n, :],
                                         start=True, stop=True)
                last.then_inc(S.logits_done, 1)

            def turn_probs(p, c):
                pe.wait_ge(S.probs_ready, p * 4 + (c + 1))
                src = logits[:, c % 2].rearrange("p n e k -> p (n e k)")
                turn(src, mix_flat[1]).then_inc(S.probs_turned, 1)

            def values_of(p, c):
                pe.wait_ge(S.probs_t_ready, p * 4 + (c + 1))
                if c == 0:
                    pe.wait_ge(S.v_band_ready, p + 1)
                    pe.wait_ge(S.biased, p * 4 + 3)
                elif c == 1:
                    pe.wait_ge(S.biased, p * 4 + 4)
                else:
                    pe.wait_ge(S.o_ready, p * 4 + c)
                for n in range(4):
                    for e in range(2):
                        last = pe.matmul(mix_ps[0][e * DH:(e + 1) * DH, 0, n * P:(n + 1) * P],
                                         v_band[:, 4 * c + n, :], probs_t[:, n, e, :], start=True, stop=True)
                last.then_inc(S.pv_done, 1)

            def turn_v(p):
                turn(v_raw, mix_flat[1]).then_inc(S.v_turned, 1)

            def attn(*steps):
                return tuple((lambda p, f=f, c=c: f(p, c)) for f, c in steps)

            attention = (attn((logits_of, 0)), attn((logits_of, 1)), attn((turn_probs, 0), (logits_of, 2)),
                         attn((values_of, 0), (turn_probs, 1)), attn((logits_of, 3)),
                         attn((values_of, 1), (turn_probs, 2)), attn((values_of, 2), (turn_probs, 3)),
                         attn((values_of, 3)))

            def step_projections(i, between):
                for j in range(4):
                    pe.wait_ge(S.lo_ready, i * 4 + (FIRST_B + 3 + j))
                    if j < 2:
                        if first(i):
                            pe.wait_ge((S.k_raw_ready, S.v_raw_ready)[j], 1)
                        else:
                            pe.wait_ge(S.q_even_ready, i * 2 + (j - 1))
                            pe.wait_ge(S.q_odd_ready, i * 2 + (j - 1))
                    else:
                        pe.wait_ge(S.gate_ready, i * 2 + (HEADS + j - 1))
                    for half in range(2):
                        last = project(j % 2, half, hB_hi, hB_lo)
                        if half == 1:
                            last.then_inc(S.block_done, 1)
                        for step in between[2 * j + half]:
                            step(i - 1)

            step_projections(0, ((turn_v,),) + ((),) * 7)
            with pe.Fori(1, NJ) as i:
                step_projections(i, attention)
            for group in attention:
                for step in group:
                    step(NJ - 1)

            out_tile(1, 0, 0, woB, ((S.q_even_ready, 2 * NJ - 1), (S.q_odd_ready, 2 * NJ - 1)))
            out_tile(1, 1, 1, woB, ((S.q_even_ready, 2 * NJ), (S.q_odd_ready, 2 * NJ)))
            with pe.Fori(1, TB // 2) as i:
                out_tile(1, i * 2, 0, woB, ((S.y_scaled, i * 2 + (TB - 1)),))
                out_tile(1, i * 2 + 1, 1, woB, ((S.y_scaled, i * 2 + TB),))

        @block.scalar
        def _(act):
            def inverse_rms(source, junk, col, squared, logged, ready, n, loaded):
                act.wait_ge(S.cols_set, 2)
                for sem, value in loaded:
                    act.wait_ge(sem, value)
                nc.scalar.activation(junk, source, ACT.Square, accum_out=ssq[:, col:col + 1]).then_inc(squared, 1)
                act.wait_ge(squared, n)
                nc.scalar.activation(rms[:, col:col + 1], ssq[:, col:col + 1], ACT.Ln, scale=1.0 / D,
                                     bias=eps_col[:]).then_inc(logged, 1)
                act.wait_ge(logged, n)
                nc.scalar.activation(rms[:, col:col + 1], rms[:, col:col + 1], ACT.Exp, scale=-0.5)\
                    .then_inc(ready, 1)

            def split_block(n, slot, free):
                act.wait_ge(raw_loaded[slot], (n - slot) * 8 + 16)
                if free is not None:
                    act.wait_ge(*free)
                nc.scalar.copy(split_hi[:, slot], w_raw[:, slot]).then_inc(S.hi_ready, 1)

            def split_out_weights(n, k, w_hi):
                act.wait_ge(raw_loaded[k % 2], (n + k - k % 2) * 8 + 16)
                nc.scalar.copy(w_hi[:, k, :], flat(w_raw[:, k % 2])).then_inc(S.hi_ready, 1)

            act.wait_ge(S.bound_shifted, 1)
            nc.scalar.activation(lb_tmp[:], lb_tmp[:], ACT.Exp).then_inc(S.bound_exped, 1)
            act.wait_ge(S.bound_ready, 1)
            act.wait_ge(S.cols_set, 2)
            nc.scalar.activation(log1mlb_col[:], lb_col[:], ACT.Ln, scale=-1.0, bias=one_col[:])\
                .then_inc(S.bound_logged, 1)

            def norm_in(t, slot):
                loaded = [(x_in_loaded[slot], (t - slot) * 8 + 16)]
                if not (isinstance(t, int) and t < 2):
                    loaded.append((S.in_turned, t - 1))
                inverse_rms(x_in[:, slot], x_scaled[:, slot], slot, S.in_squared, S.in_logged, S.in_rms_ready,
                            t + 1, loaded)

            def high_in(t, slot):
                act.wait_ge(S.in_turned, t + 1)
                nc.scalar.copy(hA_hi[:, :, ds(t * P, P)], mix_flat[slot].rearrange("p (k n) -> p k n", k=KB))\
                    .then_inc(S.in_hi_ready, 1)

            norm_in(0, 0)
            split_block(0, 0, None)
            norm_in(1, 1)
            high_in(0, 0)
            with act.Fori(1, TB // 2) as i:
                norm_in(i * 2, 0)
                high_in(i * 2 - 1, 1)
                norm_in(i * 2 + 1, 1)
                high_in(i * 2, 0)
            high_in(TB - 1, 1)

            def value_buffer(p):
                act.wait_ge(S.block_done, p * A_BLOCKS + A_BLOCKS)
                nc.scalar.copy(val[:], flat(proj_ps[1])).then_inc(S.val_ready, 1)

            def values_by_token(p):
                act.wait_ge(S.val_turned, p + 1)
                nc.scalar.copy(val[:], mix_flat[0]).then_inc(S.val_tok_ready, 1)

            def keys_by_token(p):
                act.wait_ge(S.k_dec_turned, p + 1)
                nc.scalar.copy(k_dec[:], mix_flat[1]).then_inc(S.k_dec_tok_ready, 1)

            def forget_gate(h):
                act.wait_ge(S.block_done, h * A_BLOCKS + 1)
                if not first(h):
                    act.wait_ge(S.q1_ready, h)
                nc.scalar.activation(tmp1[:], flat(proj_ps[0]), ACT.Abs).then_inc(S.f_abs, 1)
                act.wait_ge(S.f_abs, h + 1)
                nc.scalar.activation(tmp1[:], tmp1[:], ACT.Exp, scale=-1.0).then_inc(S.f_exp, 1)
                act.wait_ge(S.f_exp, h + 1)
                nc.scalar.activation(tmp1[:], tmp1[:], ACT.Ln, bias=one_col[:]).then_inc(S.f_log, 1)
                act.wait_ge(S.f_neg_ready, h + 1)
                nc.scalar.activation(tmp3[:], tmp3[:], ACT.Exp).then_inc(S.f_neg_exp, 1)
                act.wait_ge(S.f_neg_exp, h + 1)
                nc.scalar.activation(tmp3[:], tmp3[:], ACT.Ln, scale=lb_col[:, ds(h, 1)], bias=one_col[:])\
                    .then_inc(S.f_neg_log, 1)
                act.wait_ge(S.log_nf_ready, h + 1)
                if not first(h):
                    act.wait_ge(S.k_dec_ready, h)
                nc.scalar.activation(k_gate[:], tmp2[:], ACT.Exp, bias=log1mlb_col[:, ds(h, 1)])\
                    .then_inc(S.k_gate_ready, 1)

            def silu_query(h):
                act.wait_ge(S.block_done, h * A_BLOCKS + 2)
                if not first(h):
                    act.wait_ge(S.q_dec_ready, h)
                nc.scalar.activation(silu_q[:], flat(proj_ps[1]), ACT.Silu).then_inc(S.silu_q_ready, 1)

            def silu_gate(h):
                act.wait_ge(S.block_done, h * A_BLOCKS + 3)
                nc.scalar.activation(mixed[:, ds(h, 1), :].rearrange("p a n -> p (a n)"), flat(proj_ps[0]),
                                     ACT.Silu).then_inc(S.gate_ready, 1)

            def decays_near(h):
                act.wait_ge(S.d3_ready, h + 1)
                act.wait_ge(S.k_gate_ready, h + 1)
                nc.scalar.activation(tmp2[:], tmp1[:], ACT.Exp).then_inc(S.e3q_ready, 1)
                nc.scalar.activation(tmp1[:], tmp1[:], ACT.Exp, scale=-1.0).then_inc(S.e3k_ready, 1)
                act.wait_ge(S.d21_ready, h + 1)
                nc.scalar.activation(tmp3[:], tmp3[:], ACT.Exp).then_inc(S.e21_ready, 1)

            def decays_far(h):
                act.wait_ge(S.b_ready, h + 1)
                if not first(h):
                    act.wait_ge(S.k_dec_ready, h)
                nc.scalar.activation(chunk_decay[:], halves(b_cum)[:, :, :, CHUNK - 1], ACT.Exp)\
                    .then_inc(S.decay_ready, 1)
                act.wait_ge(S.q3_ready, h + 1)
                nc.scalar.activation(tmp2[:], b_cum[:], ACT.Exp).then_inc(S.eb_ready, 1)
                act.wait_ge(S.dq1_ready, h + 1)
                nc.scalar.activation(tmp1[:, 0:HALF], tmp1[:, 0:HALF], ACT.Exp).then_inc(S.eq1_ready, 1)
                act.wait_ge(S.dkd_ready, h + 1)
                nc.scalar.activation(tmp3[:], tmp3[:], ACT.Exp).then_inc(S.ekd_ready, 1)

            def keep_level0(p):
                act.wait_ge(S.level1_kept, p + 1)
                act.wait_ge(S.level0_done, p + 1)
                nc.scalar.copy(scores[0:CHUNK, :, CHUNK:P],
                               mix_ps[0][0:CHUNK, 0, :].rearrange("p (r c) -> p r c", c=CHUNK))\
                    .then_inc(S.level0_kept, 1)

            def square_output(p):
                act.wait_ge(S.o_done, p + 1)
                nc.scalar.activation(rstd[:], mix_flat[1], ACT.Square).then_inc(S.o_squared, 1)

            def inverse_head_rms(p):
                act.wait_ge(S.mean_done, p + 1)
                nc.scalar.activation(rstd[:], mix_flat[0], ACT.Ln, bias=eps_col[:]).then_inc(S.mean_logged, 1)
                act.wait_ge(S.mean_logged, p + 1)
                nc.scalar.activation(rstd[:], rstd[:], ACT.Exp, scale=-0.5).then_inc(S.rstd_ready, 1)

            def head(h, previous, following):
                def next_block(j):
                    n = h * A_BLOCKS + j
                    split_block(n, j % 2, (S.block_done, n - 1) if not (first(h) and j < 2) else None)

                next_block(1)
                if previous:
                    value_buffer(h - 1)
                    values_by_token(h - 1)
                    keys_by_token(h - 1)
                next_block(2)
                forget_gate(h)
                next_block(3)
                if previous:
                    keep_level0(h - 1)
                silu_query(h)
                if previous:
                    square_output(h - 1)
                decays_near(h)
                if previous:
                    inverse_head_rms(h - 1)
                if following:
                    next_block(4)
                silu_gate(h)
                decays_far(h)

            head(0, False, True)
            with act.Fori(1, HEADS - 1) as h:
                head(h, True, True)
            head(HEADS - 1, True, False)
            last = HEADS - 1
            value_buffer(last)
            act.wait_ge(S.block_done, BLK_B)
            for k, step in enumerate((values_by_token, keys_by_token, None, None, keep_level0, square_output,
                                      inverse_head_rms, None)):
                split_out_weights(FIRST_AO, k, woA_hi)
                if step:
                    step(last)

            def split_mixed(layer, t, slot, free):
                for sem, value in free:
                    act.wait_ge(sem, value)
                nc.scalar.copy(split_hi[:, slot], mixed_tile(t)).then_inc(S.mix_hi_ready, 1)

            def norm_y(layer, t, slot, buffer):
                loaded = [(S.out_tile_done, t + (TB * layer + 1))]
                if not (isinstance(t, int) and t < 2):
                    loaded.append((S.h_turned, t - 1) if layer == 0 else (S.x1_ready, t + (TB - 1)))
                inverse_rms(flat(proj_ps[slot]), buffer[:, slot], slot, S.y_squared, S.y_logged, S.y_rms,
                            t + (TB * layer + 1), loaded)

            def high_h(t, slot):
                act.wait_ge(S.h_turned, t + 1)
                nc.scalar.copy(hB_hi[:, :, ds(t * P, P)], mix_flat[slot].rearrange("p (k n) -> p k n", k=KB))\
                    .then_inc(S.h_hi_ready, 1)

            def norm_x1(t, slot):
                inverse_rms(mixed_tile(t), y_norm[:, slot].rearrange("p (k n) -> p k n", k=KB), 2 + slot,
                            S.x1_squared, S.x1_logged, S.x1_rms, t + 1, [(S.x1_ready, t + 1)])

            split_mixed(0, 0, 0, ((S.mixed_ready, HEADS),))
            split_mixed(0, 1, 1, ())
            norm_y(0, 0, 0, y_norm)
            norm_x1(0, 0)
            split_mixed(0, 2, 0, ((S.out_tile_done, 1),))
            norm_y(0, 1, 1, y_norm)
            high_h(0, 0)
            norm_x1(1, 1)
            with act.Fori(1, TB // 2 - 1) as i:
                for slot in range(2):
                    t = i * 2 + slot
                    split_mixed(0, t + 1, 1 - slot, ((S.out_tile_done, t),))
                    norm_y(0, t, slot, y_norm)
                    high_h(t - 1, 1 - slot)
                    norm_x1(t, slot)
            for t in (TB - 2, TB - 1):
                slot = t % 2
                if t + 1 < TB:
                    split_mixed(0, t + 1, 1 - slot, ((S.out_tile_done, t),))
                else:
                    split_block(FIRST_B, 0, (S.out_tile_done, TB - 1))
                norm_y(0, t, slot, y_norm)
                high_h(t - 1, 1 - slot)
                norm_x1(t, slot)
            high_h(TB - 1, 1)

            split_block(FIRST_B + 1, 1, (S.out_tile_done, TB))
            split_block(FIRST_B + 2, 0, (S.block_done, BLK_B + 1))
            nc.scalar.copy(k_raw[:], flat(proj_ps[0])).then_inc(S.k_raw_ready, 1)
            split_block(FIRST_B + 3, 1, (S.block_done, BLK_B + 2))
            nc.scalar.copy(v_raw[:], flat(proj_ps[1])).then_inc(S.v_raw_ready, 1)

            def next_blk(i, j):
                split_block(i * 4 + (FIRST_B + 2 + j), j % 2, (S.block_done, i * 4 + (BLK_B + j + 1)))

            def gate(i, blk):
                act.wait_ge(S.block_done, i * 4 + (BLK_B + 3 + blk))
                act.wait_ge(S.resid_stored, 16 * TB) if first(i) and blk == 0 else None
                nc.scalar.activation(mixed[:, ds(i * 2 + blk, 1), :].rearrange("p a n -> p (a n)"),
                                     flat(proj_ps[blk]), ACT.Silu).then_inc(S.gate_ready, 1)

            def even_queries(i, blk):
                act.wait_ge(S.zeroB_set, 4)
                act.wait_ge(S.block_done, i * 4 + (BLK_B + 5 + blk))
                if blk == 0 and not first(i):
                    act.wait_ge(S.logits_done, i * 4)
                nc.scalar.activation(q_even[0:DH, :, blk, :], by_chunk(proj_ps[blk])[0:DH], ACT.Copy, scale=DH ** -0.5)\
                    .then_inc(S.q_even_ready, 1)

            def exp_logits(p, c):
                act.wait_ge(S.sink_shifted, p * 4 + (c + 1))
                nc.scalar.activation(sink_exp[:, c % 2], sink_exp[:, c % 2], ACT.Exp).then_inc(S.sink_exped, 1)
                act.wait_ge(S.shifted, p * 4 + (c + 1))
                nc.scalar.activation(logits[:, c % 2], logits[:, c % 2], ACT.Exp).then_inc(S.exped, 1)

            def probs_by_key(p, c):
                act.wait_ge(S.probs_turned, p * 4 + (c + 1))
                nc.scalar.copy(probs_t[:].rearrange("p n e k -> p (n e k)"), mix_flat[1])\
                    .then_inc(S.probs_t_ready, 1)

            def attend(*steps):
                def run(i):
                    for f, c in steps:
                        f(i - 1, c)
                return run

            attention = (attend((exp_logits, 0)), attend((exp_logits, 1), (probs_by_key, 0)),
                         attend((exp_logits, 2), (probs_by_key, 1), (exp_logits, 3)),
                         attend((probs_by_key, 2), (probs_by_key, 3)))

            def step(i, previous, following):
                if previous:
                    next_blk(i, 1)
                    even_queries(i - 1, 1)
                    attention[0](i)
                next_blk(i, 2)
                gate(i, 0)
                if previous:
                    attention[1](i)
                next_blk(i, 3)
                gate(i, 1)
                if previous:
                    attention[2](i)
                if following:
                    next_blk(i, 4)
                even_queries(i, 0)
                if previous:
                    attention[3](i)

            def values_by_token_b():
                act.wait_ge(S.v_turned, 1)
                nc.scalar.copy(v_tok[:].rearrange("p t d -> p (t d)"), mix_flat[1]).then_inc(S.v_tok_ready, 1)

            values_by_token_b()
            step(0, False, True)
            with act.Fori(1, NJ - 1) as i:
                step(i, True, True)
            step(NJ - 1, True, False)
            even_queries(NJ - 1, 1)
            for j in range(4):
                for k in (2 * j, 2 * j + 1):
                    split_out_weights(FIRST_BO, k, woB_hi)
                attention[j](NJ)

            split_mixed(1, 0, 0, ((S.o_ready, 4 * NJ),))
            split_mixed(1, 1, 1, ())
            norm_y(1, 0, 0, y_last)
            with act.Fori(1, TB // 2) as i:
                split_mixed(1, i * 2, 0, ((S.out_tile_done, i * 2 + (TB - 1)),))
                norm_y(1, i * 2 - 1, 1, y_last)
                split_mixed(1, i * 2 + 1, 1, ((S.out_tile_done, i * 2 + TB),))
                norm_y(1, i * 2, 0, y_last)
            norm_y(1, TB - 1, 1, y_last)

        @block.vector
        def _(dve):
            v = nc.vector

            def split_block(n, slot):
                dve.wait_ge(S.hi_ready, n + 1)
                v.tensor_tensor(split_lo[:, slot], w_raw[:, slot], split_hi[:, slot].bitcast(F32), ALU.subtract)\
                    .then_inc(S.lo_ready, 1)

            def split_out_weights(n, k, w_hi, w_lo):
                dve.wait_ge(S.hi_ready, n + k + 1)
                v.tensor_tensor(w_lo[:, k, :], flat(w_raw[:, k % 2]), w_hi[:, k, :].bitcast(F32), ALU.subtract)\
                    .then_inc(S.lo_ready, 1)

            v.memset(eps_col[:], EPS).then_inc(S.cols_set, 1)
            v.memset(one_col[:], 1.0).then_inc(S.cols_set, 1)
            v.memset(scan_keep[:], 1.0).then_inc(S.keep_ones, 1)
            dve.wait_ge(S.keep_ones, 1)
            v.memset(chunks(scan_keep)[:, :, 0:1], 0.0).then_inc(S.keep_set, 1)
            dve.wait_ge(S.const_loaded, 16 * 6)
            v.tensor_tensor(lb_tmp[:], lb_tmp[:], lb_tmp[:], ALU.subtract).then_inc(S.bound_shifted, 1)
            dve.wait_ge(S.bound_exped, 1)
            v.reciprocal(lb_col[:], lb_tmp[:]).then_inc(S.bound_inverse, 1)
            dve.wait_ge(S.bound_inverse, 1)
            v.tensor_tensor(lb_tmp[:], lb_tmp[:], lb_col[:], ALU.mult).then_inc(S.bound_prob, 1)
            dve.wait_ge(S.bound_prob, 1)
            v.tensor_tensor(lb_col[:], lb_tmp[:], lb_tmp[:], ALU.subtract).then_inc(S.bound_prob, 1)
            dve.wait_ge(S.bound_prob, 2)
            v.tensor_scalar(lb_col[:], lb_col[:], 0.0, None, ALU.max).then_inc(S.bound_ready, 1)

            dve.wait_ge(S.gain_in_loaded, 16)

            def scale_in(t, slot):
                dve.wait_ge(S.in_rms_ready, t + 1)
                v.scalar_tensor_tensor(x_scaled[:, slot], x_in[:, slot], rms[:, slot:slot + 1], gain_in[:],
                                       ALU.mult, ALU.mult).then_inc(S.in_scaled, 1)

            def low_in(t, slot):
                dve.wait_ge(S.in_hi_ready, t + 1)
                cols = ds(t * P, P)
                v.tensor_tensor(hA_lo[:, :, cols], mix_flat[slot].rearrange("p (k n) -> p k n", k=KB),
                                hA_hi[:, :, cols].bitcast(F32), ALU.subtract).then_inc(S.in_lo_ready, 1)

            scale_in(0, 0)
            split_block(0, 0)
            scale_in(1, 1)
            low_in(0, 0)
            with dve.Fori(1, TB // 2) as i:
                scale_in(i * 2, 0)
                low_in(i * 2 - 1, 1)
                scale_in(i * 2 + 1, 1)
                low_in(i * 2, 0)
            low_in(TB - 1, 1)
            dve.wait_ge(S.zeros_set, 4)

            def keep(n, bank, done, kept, p):
                dve.wait_ge(S.zeros_set, 4)
                if n == 2:
                    dve.wait_ge(S.level2_kept, p + 1)
                dve.wait_ge(done, p + 1)
                mask = masks[:, n:n + 1, :].broadcast_to([P, NPAIR, P])
                v.copy_predicated(scores[:], mask, mix_flat[bank].rearrange("p (r c) -> p r c", c=P))\
                    .then_inc(kept, 1)

            def states(p):
                dve.wait_ge(S.update_done, p + 1)
                for r in range(NPAIR - 1):
                    update = mix_flat[1][:, r * P:(r + 1) * P]
                    if r == 0:
                        v.tensor_copy(state[:, 0, :], update).then_inc(S.state_step, 1)
                    else:
                        dve.wait_ge(S.state_step, p * (NPAIR - 1) + r)
                        v.scalar_tensor_tensor(state[:, r, :], state[:, r - 1, :], pair_decay[:, r:r + 1], update,
                                               ALU.mult, ALU.add).then_inc(S.state_step, 1)

            def forget_gate(h):
                f = flat(proj_ps[0])
                dve.wait_ge(S.block_done, h * A_BLOCKS + 1)
                dve.wait_ge(S.f_abs, h + 1)
                v.tensor_scalar(tmp3[:], f, -1.0, 40.0, ALU.mult, ALU.min).then_inc(S.f_neg_ready, 1)
                dve.wait_ge(S.f_log, h + 1)
                v.scalar_tensor_tensor(b_cum[:], f, 0.0, tmp1[:], ALU.min, ALU.subtract)\
                    .then_inc(S.log_f_ready, 1)
                dve.wait_ge(S.log_f_ready, h + 1)
                v.tensor_tensor(tmp2[:], b_cum[:], f, ALU.subtract).then_inc(S.log_nf_ready, 1)

            def cumulate(h):
                dve.wait_ge(S.f_neg_log, h + 1)
                v.tensor_tensor(b_cum[:], b_cum[:], tmp3[:], ALU.add).then_inc(S.log_f_full, 1)
                dve.wait_ge(S.log_f_full, h + 1)
                v.tensor_tensor_scan(b_cum[:], scan_keep[:], b_cum[:], 0.0, ALU.mult, ALU.add)\
                    .then_inc(S.b_ready, 1)

            b_subs, b_chunks, b_halves = subs(b_cum), chunks(b_cum), halves(b_cum)
            b_quads = b_cum[:].rearrange("p (n s c) -> p n s c", s=2, c=SUB)
            HC = CHUNK // 2

            def distances(h):
                dve.wait_ge(S.b_ready, h + 1)
                v.tensor_tensor(subs(tmp1), b_subs, b_subs[:, :, 0:1].broadcast_to([P, T // SUB, SUB]),
                                ALU.subtract).then_inc(S.d3_ready, 1)
                v.tensor_tensor(tmp3[:, 0:HALF].rearrange("p (n c) -> p n c", c=SUB),
                                b_quads[:, :, 1, 0:1].broadcast_to([P, T // SUB // 2, SUB]), b_quads[:, :, 0, :],
                                ALU.subtract)
                v.tensor_tensor(tmp3[:, HALF:T].rearrange("p (n c) -> p n c", c=HC),
                                b_chunks[:, :, HC:HC + 1].broadcast_to([P, NCH, HC]), b_chunks[:, :, 0:HC],
                                ALU.subtract).then_inc(S.d21_ready, 1)

            def near_operands(h):
                dve.wait_ge(S.silu_q_ready, h + 1)
                dve.wait_ge(S.e3q_ready, h + 1)
                if not first(h):
                    dve.wait_ge(S.level2_done, h)
                v.tensor_tensor(flat(q3[:]), silu_q[:], tmp2[:], ALU.mult).then_inc(S.q3_ready, 1)
                dve.wait_ge(S.e3k_ready, h + 1)
                v.tensor_tensor(flat(k3[:]), k_gate[:], tmp1[:], ALU.mult).then_inc(S.k3_ready, 1)
                dve.wait_ge(S.k3_ready, h + 1)
                v.tensor_tensor(tmp1[:, 0:HALF].rearrange("p (n c) -> p n c", c=HC), b_chunks[:, :, HC:CHUNK],
                                b_chunks[:, :, HC:HC + 1].broadcast_to([P, NCH, HC]), ALU.subtract)\
                    .then_inc(S.dq1_ready, 1)
                dve.wait_ge(S.e21_ready, h + 1)
                even = "p (n s c) -> p n s c"
                v.tensor_tensor(flat(k2[:]).rearrange(even, s=2, c=SUB)[:, :, 0, :],
                                k_gate[:].rearrange(even, s=2, c=SUB)[:, :, 0, :],
                                tmp3[:, 0:HALF].rearrange("p (n c) -> p n c", c=SUB), ALU.mult)\
                    .then_inc(S.k2_ready, 1)
                if not first(h):
                    dve.wait_ge(S.level1_done, h)
                v.tensor_tensor(k1[:, :, 0:HC], chunks(k_gate)[:, :, 0:HC],
                                tmp3[:, HALF:T].rearrange("p (n c) -> p n c", c=HC), ALU.mult)\
                    .then_inc(S.k1_ready, 1)
                dve.wait_ge(S.k1_ready, h + 1)
                v.tensor_tensor(chunks(tmp3), b_chunks[:, :, CHUNK - 1:CHUNK].broadcast_to([P, NCH, CHUNK]), b_chunks,
                                ALU.subtract).then_inc(S.dkd_ready, 1)

            def far_operands(h):
                dve.wait_ge(S.eq1_ready, h + 1)
                v.tensor_tensor(q1[:, :, HC:CHUNK], chunks(silu_q)[:, :, HC:CHUNK],
                                tmp1[:, 0:HALF].rearrange("p (n c) -> p n c", c=HC), ALU.mult)\
                    .then_inc(S.q1_ready, 1)
                dve.wait_ge(S.decay_ready, h + 1)
                v.tensor_tensor(pair_decay[:], chunk_decay[:, :, 0], chunk_decay[:, :, 1], ALU.mult)\
                    .then_inc(S.pair_decay_ready, 1)
                dve.wait_ge(S.eb_ready, h + 1)
                if not first(h):
                    dve.wait_ge(S.level0_done, h)
                sq, eb, kg, ekd = halves(silu_q), halves(tmp2), halves(k_gate), halves(tmp3)
                v.tensor_tensor(q_dec_b[:], sq[:, :, 1, :], eb[:, :, 1, :], ALU.mult).then_inc(S.q_dec_b_ready, 1)
                dve.wait_ge(S.ekd_ready, h + 1)
                v.tensor_tensor(k_dec_a[:], kg[:, :, 0, :], ekd[:, :, 0, :], ALU.mult).then_inc(S.k_dec_a_ready, 1)
                if not first(h):
                    dve.wait_ge(S.o_done, h)
                v.tensor_tensor(halves(q_dec)[:, :, 0, :], sq[:, :, 0, :], eb[:, :, 0, :], ALU.mult)
                dve.wait_ge(S.q_dec_b_ready, h + 1)
                v.tensor_tensor(halves(q_dec)[:, :, 1, :], q_dec_b[:],
                                chunk_decay[:, :, 0:1].broadcast_to([P, NPAIR, CHUNK]), ALU.mult)\
                    .then_inc(S.q_dec_ready, 1)
                v.tensor_tensor(halves(k_dec)[:, :, 1, :], kg[:, :, 1, :], ekd[:, :, 1, :], ALU.mult)
                dve.wait_ge(S.k_dec_a_ready, h + 1)
                v.tensor_tensor(halves(k_dec)[:, :, 0, :], k_dec_a[:],
                                chunk_decay[:, :, 1:2].broadcast_to([P, NPAIR, CHUNK]), ALU.mult)\
                    .then_inc(S.k_dec_ready, 1)

            def norm_and_gate(p):
                dve.wait_ge(S.rstd_ready, p + 1)
                v.tensor_tensor(rstd[:], mix_flat[1], rstd[:], ALU.mult).then_inc(S.o_scaled, 1)
                dve.wait_ge(S.o_scaled, p + 1)
                dve.wait_ge(S.gate_ready, p + 1)
                row = mixed[:, ds(p, 1), :].rearrange("p a n -> p (a n)")
                v.scalar_tensor_tensor(row, rstd[:], gn_col[:, ds(p, 1)], row, ALU.mult, ALU.mult)\
                    .then_inc(S.mixed_ready, 1)

            def head(h, previous, following):
                n = h * A_BLOCKS
                split_block(n + 1, 1)
                if previous:
                    keep(0, 0, S.level3_done, S.level3_kept, h - 1)
                    states(h - 1)
                split_block(n + 2, 0)
                forget_gate(h)
                if previous:
                    keep(1, 0, S.level2_done, S.level2_kept, h - 1)
                    keep(2, 1, S.level1_done, S.level1_kept, h - 1)
                cumulate(h)
                split_block(n + 3, 1)
                distances(h)
                near_operands(h)
                if previous:
                    norm_and_gate(h - 1)
                if following:
                    split_block(n + 4, 0)
                far_operands(h)

            head(0, False, True)
            with dve.Fori(1, HEADS - 1) as h:
                head(h, True, True)
            head(HEADS - 1, True, False)
            last = HEADS - 1
            for k in range(2):
                split_out_weights(FIRST_AO, k, woA_hi, woA_lo)
            keep(0, 0, S.level3_done, S.level3_kept, last)
            states(last)
            keep(1, 0, S.level2_done, S.level2_kept, last)
            for k in range(2, 5):
                split_out_weights(FIRST_AO, k, woA_hi, woA_lo)
            keep(2, 1, S.level1_done, S.level1_kept, last)
            for k in range(5, 7):
                split_out_weights(FIRST_AO, k, woA_hi, woA_lo)
            norm_and_gate(last)
            split_out_weights(FIRST_AO, 7, woA_hi, woA_lo)

            def split_mixed(layer, t, slot):
                dve.wait_ge(S.mix_hi_ready, t + (TB * layer + 1))
                v.tensor_tensor(split_lo[:, slot], mixed_tile(t), split_hi[:, slot].bitcast(F32), ALU.subtract)\
                    .then_inc(S.mix_lo_ready, 1)

            def add_y(layer, t, slot, buffer, gain):
                n = t + (TB * layer + 1)
                dve.wait_ge(S.y_rms, n)
                v.scalar_tensor_tensor(buffer[:, slot], flat(proj_ps[slot]), rms[:, slot:slot + 1], gain[:],
                                       ALU.mult, ALU.mult).then_inc(S.y_scaled, 1)
                dve.wait_ge(S.y_scaled, n)
                dve.wait_ge(resid_loaded[slot], (t - slot) * 8 + (64 * layer + 16))
                v.tensor_tensor(mixed_tile(t), buffer[:, slot].rearrange("p (k n) -> p k n", k=KB), mixed_tile(t),
                                ALU.add).then_inc(S.x1_ready, 1)

            def low_h(t, slot):
                dve.wait_ge(S.h_hi_ready, t + 1)
                cols = ds(t * P, P)
                v.tensor_tensor(hB_lo[:, :, cols], mix_flat[slot].rearrange("p (k n) -> p k n", k=KB),
                                hB_hi[:, :, cols].bitcast(F32), ALU.subtract).then_inc(S.h_lo_ready, 1)

            def scale_h(t, slot):
                dve.wait_ge(S.x1_rms, t + 1)
                v.scalar_tensor_tensor(y_norm[:, slot].rearrange("p (k n) -> p k n", k=KB), mixed_tile(t),
                                       rms[:, 2 + slot:3 + slot], gain_pre[:].rearrange("p (k n) -> p k n", k=KB),
                                       ALU.mult, ALU.mult).then_inc(S.h_scaled, 1)

            split_mixed(0, 0, 0)
            split_mixed(0, 1, 1)
            dve.wait_ge(S.gains_loaded, 32)
            add_y(0, 0, 0, y_norm, gain_post)
            scale_h(0, 0)
            split_mixed(0, 2, 0)
            add_y(0, 1, 1, y_norm, gain_post)
            low_h(0, 0)
            scale_h(1, 1)
            with dve.Fori(1, TB // 2 - 1) as i:
                for slot in range(2):
                    t = i * 2 + slot
                    split_mixed(0, t + 1, 1 - slot)
                    add_y(0, t, slot, y_norm, gain_post)
                    low_h(t - 1, 1 - slot)
                    scale_h(t, slot)
            for t in (TB - 2, TB - 1):
                slot = t % 2
                if t + 1 < TB:
                    split_mixed(0, t + 1, 1 - slot)
                else:
                    split_block(FIRST_B, 0)
                add_y(0, t, slot, y_norm, gain_post)
                low_h(t - 1, 1 - slot)
                scale_h(t, slot)
            low_h(TB - 1, 1)

            split_block(FIRST_B + 1, 1)
            split_block(FIRST_B + 2, 0)
            split_block(FIRST_B + 3, 1)
            dve.wait_ge(S.bias_loaded, 16)

            def odd_queries(i, blk):
                dve.wait_ge(S.zeroB_set, 4)
                dve.wait_ge(S.block_done, i * 4 + (BLK_B + 5 + blk))
                if blk == 0 and not first(i):
                    dve.wait_ge(S.logits_done, i * 4)
                v.tensor_scalar(q_odd[DH:P, :, blk, :], by_chunk(proj_ps[blk])[DH:P], DH ** -0.5, None, ALU.mult)\
                    .then_inc(S.q_odd_ready, 1)

            def shift(p, c):
                n, buf = p * 4 + (c + 1), c % 2
                dve.wait_ge(S.logits_done, n)
                lg = logits[:, buf].rearrange("p (r n) e k -> p r (n e k)", r=2)
                table = bias[:, ds(p, 1), :].broadcast_to([P, 2, 4 * P])
                v.tensor_tensor(lg, mix_flat[0].rearrange("p (r m) -> p r m", r=2), table, ALU.add)\
                    .then_inc(S.biased, 1)
                dve.wait_ge(S.biased, n)
                if c == 0:
                    v.memset(logits[:, buf, 0, :, CHUNK:P], MASKED).then_inc(S.edge_masked, 1)
                    dve.wait_ge(S.edge_masked, p + 1)
                by_row = logits[:, buf].rearrange("p n e k -> p (n e) k")
                v.tensor_reduce(row_max[:, buf], by_row, AX_X, ALU.max).then_inc(S.max_part, 1)
                dve.wait_ge(S.max_part, n)
                rows = row_max[:, buf].rearrange("p (n e) -> p n e", e=2)
                sinks = sink[:, ds(p, 1), :].broadcast_to([P, 4, 2])
                v.tensor_tensor(rows, rows, sinks, ALU.max).then_inc(S.max_ready, 1)
                dve.wait_ge(S.max_ready, n)
                v.tensor_tensor(sink_exp[:, buf].rearrange("p (n e) -> p n e", e=2), sinks, rows, ALU.subtract)\
                    .then_inc(S.sink_shifted, 1)
                v.tensor_tensor(by_row, by_row, row_max[:, buf].unsqueeze(2).broadcast_to([P, 8, P]), ALU.subtract)\
                    .then_inc(S.shifted, 1)

            def normalise(p, c):
                n, buf = p * 4 + (c + 1), c % 2
                by_row = logits[:, buf].rearrange("p n e k -> p (n e) k")
                dve.wait_ge(S.exped, n)
                v.tensor_reduce(row_sum[:, buf], by_row, AX_X, ALU.add).then_inc(S.sum_part, 1)
                dve.wait_ge(S.sum_part, n)
                dve.wait_ge(S.sink_exped, n)
                v.tensor_tensor(row_sum[:, buf], row_sum[:, buf], sink_exp[:, buf], ALU.add).then_inc(S.sum_ready, 1)
                dve.wait_ge(S.sum_ready, n)
                v.reciprocal(row_sum[:, buf], row_sum[:, buf]).then_inc(S.inverse_ready, 1)
                dve.wait_ge(S.inverse_ready, n)
                v.tensor_tensor(by_row, by_row, row_sum[:, buf].unsqueeze(2).broadcast_to([P, 8, P]), ALU.mult)\
                    .then_inc(S.probs_ready, 1)

            def gate_output(p, c):
                dve.wait_ge(S.pv_done, p * 4 + (c + 1))
                dve.wait_ge(S.gate_ready, p * 2 + (HEADS + 2))
                for blk in range(2):
                    dst = mixed[:, ds(p * 2 + blk, 1), 4 * CHUNK * c:4 * CHUNK * (c + 1)]\
                        .rearrange("p a (n q) -> p (a n) q", q=CHUNK)
                    src = mix_ps[0][:, 0, :].rearrange("p (n b q) -> p n b q", b=2, q=CHUNK)[:, :, blk, :]
                    last = v.tensor_tensor(dst, src, dst, ALU.mult)
                last.then_inc(S.o_ready, 1)

            def attend(*steps):
                def run(i):
                    for f, c in steps:
                        f(i - 1, c)
                return run

            attention = (attend((shift, 0)), attend((shift, 1), (normalise, 0)),
                         attend((shift, 2), (normalise, 1), (gate_output, 0), (shift, 3)),
                         attend((normalise, 2), (gate_output, 1), (normalise, 3), (gate_output, 2),
                                (gate_output, 3)))

            def step(i, previous, following):
                n = i * 4 + (FIRST_B + 2)
                if previous:
                    split_block(n + 1, 1)
                    odd_queries(i - 1, 1)
                    attention[0](i)
                split_block(n + 2, 0)
                if previous:
                    attention[1](i)
                split_block(n + 3, 1)
                if previous:
                    attention[2](i)
                if following:
                    split_block(n + 4, 0)
                odd_queries(i, 0)
                if previous:
                    attention[3](i)

            step(0, False, True)
            with dve.Fori(1, NJ - 1) as i:
                step(i, True, True)
            step(NJ - 1, True, False)
            odd_queries(NJ - 1, 1)
            for j in range(4):
                for k in (2 * j, 2 * j + 1):
                    split_out_weights(FIRST_BO, k, woB_hi, woB_lo)
                attention[j](NJ)

            dve.wait_ge(S.gain_last_loaded, 16)
            split_mixed(1, 0, 0)
            split_mixed(1, 1, 1)
            add_y(1, 0, 0, y_last, gain_last)
            with dve.Fori(1, TB // 2) as i:
                split_mixed(1, i * 2, 0)
                add_y(1, i * 2 - 1, 1, y_last, gain_last)
                split_mixed(1, i * 2 + 1, 1)
                add_y(1, i * 2, 0, y_last, gain_last)
            add_y(1, TB - 1, 1, y_last, gain_last)


def shape_constants():
    c = np.arange(P)[:, None]
    q = np.arange(P)[None, :]
    same = c // CHUNK == q // CHUNK
    c_sub, q_sub = c % CHUNK // SUB, q % CHUNK // SUB
    near = same & (c_sub == q_sub) & (c <= q)
    middle = same & (q_sub % 2 == 1) & (c_sub == q_sub - 1)
    far = same & (q_sub >= 2) & (c_sub < 2)
    score_masks = np.stack([near, middle, far], axis=1).astype(np.int32)
    heads = KV * 8
    slopes = (2.0 ** (-8.0 * np.arange(1, heads + 1, dtype=np.float32) / heads)).astype(np.float32)
    alibi = np.zeros((2, CHUNK, NJ, 2, 2, 2, CHUNK), np.float32)
    query = np.arange(CHUNK)[:, None]
    key = np.arange(CHUNK)[None, :]
    for odd_chunk in range(2):
        for half in range(2):
            own = half == odd_chunk
            dist = np.abs(query + (0 if own else CHUNK) - key).astype(np.float32)
            for blk in range(2):
                for j in range(NJ):
                    for e in range(2):
                        alibi[blk, :, j, odd_chunk, e, half, :] = -slopes[4 * j + 2 * blk + e] * dist
    return np.eye(P, dtype=np.float32), score_masks, alibi.reshape(P, NJ, 4 * P)


def kernel(**inputs):
    import concourse.bacc as bacc
    from concourse.bass_utils import run_bass_kernel_spmd

    nc = bacc.Bacc("TRN2", target_bir_lowering=False, num_devices=1)
    names = ("x", "norm_pre", "norm_post", "a_w_in", "a_lb_logits", "a_norm", "a_w_out", "b_w_in", "b_sinks",
             "b_w_out")
    arrays = {n: np.ascontiguousarray(inputs[n]) for n in names}
    arrays["identity"], arrays["score_masks"], arrays["alibi"] = shape_constants()
    handles = [nc.dram_tensor(f"in_{n}", a.shape, mybir.dt.from_np(a.dtype), kind="ExternalInput").ap()
               for n, a in arrays.items()]
    out = nc.dram_tensor("out", (1, T, D), F32, kind="ExternalOutput").ap()
    x1_store = nc.dram_tensor("x1_store", (1, T, D), F32).ap()
    build(nc, *handles, out, x1_store)
    result = run_bass_kernel_spmd(nc, [{f"in_{n}": a for n, a in arrays.items()}], core_ids=[0])
    return result.results[0]["out"]
```

```python
from collections import namedtuple

import numpy as np

import concourse.bass as bass
from concourse import mybir

F32 = mybir.dt.float32
F32R = mybir.dt.float32r
I32 = mybir.dt.int32
ALU = mybir.AluOpType
ACT = mybir.ActivationFunctionType
AX_X = mybir.AxisListType.X

P = 128
D = 1024
T = 1024
KB = D // P
X_SLOTS = 4
TB = T // P
HALF = 512
EPS = 1e-6

CHUNK = 64
NCH = T // CHUNK
NPAIR = NCH // 2
SUB = 16
HEADS = D // P
A_BLOCKS = 4
A_COLUMN = (D, 0, 3 * D, 2 * D)

DH = 64
KV = 2
NJ = 4
B_KV_BLOCKS = 2
GATE_COLUMN = D + 2 * KV * DH
MASKED = -1.0e30

FIRST_A = 0
FIRST_AO = FIRST_A + A_BLOCKS * HEADS
FIRST_B = FIRST_AO + KB
FIRST_BO = FIRST_B + B_KV_BLOCKS + 4 * NJ
BLK_B = A_BLOCKS * HEADS
BLK_END = BLK_B + B_KV_BLOCKS + 4 * NJ


def build(nc, x, norm_pre, norm_post, a_w_in, a_lb_logits, a_norm, a_w_out, b_w_in, b_sinks,
          b_w_out, identity, score_masks, alibi, out, x1_store):
    ds = bass.ds

    at = [(nc.sbuf_base + 31) // 32 * 32]

    def sb(name, shape, dt=F32, offset=None):
        size = int(np.prod(shape[1:])) * 4
        if offset is None:
            offset = at[0]
            at[0] += (size + 31) // 32 * 32
        return nc.alloc_sbuf_tensor_at(name, shape, dt, offset=offset)

    KIB = 1024
    ident = sb("ident", [P, P])
    ones = sb("ones", [P, P])
    masks = sb("masks", [P, 3, P], I32)
    lb_col = sb("lb_col", [P, HEADS])
    lb_tmp = sb("lb_tmp", [P, HEADS])
    log1mlb_col = sb("log1mlb_col", [P, HEADS])
    gn_col = sb("gn_col", [P, HEADS])
    sink = sb("sink", [P, NJ, 2])
    ssq = sb("ssq", [P, 4])
    rms = sb("rms", [P, 4])
    chunk_decay = sb("chunk_decay", [P, NPAIR, 2])
    pair_decay = sb("pair_decay", [P, NPAIR])
    neg_max = sb("neg_max", [P, 2, 8])
    sink_exp = sb("sink_exp", [P, 2, 8])
    row_sum = sb("row_sum", [P, 2, 8])
    eps_col = sb("eps_col", [P, 1])
    one_col = sb("one_col", [P, 1])
    mixed = sb("mixed", [P, KB, T])
    w_raw = sb("w_raw", [P, 2, KB, P])
    split_hi = sb("split_hi", [P, 2, KB, P], F32R)
    split_lo = sb("split_lo", [P, 2, KB, P], F32R)

    zone1 = at[0]
    zone2 = zone1 + 64 * KIB
    zone_end = zone2 + 80 * KIB
    assert zone_end <= nc.sbuf_usable_end, (zone_end, nc.sbuf_usable_end)

    def zoned(zone):
        off = [zone]

        def take(name, shape, dt=F32):
            t = sb(name, shape, dt, offset=off[0])
            off[0] += int(np.prod(shape[1:])) * 4
            return t
        return take

    z = zoned(zone1)
    hA_hi, hA_lo = z("hA_hi", [P, KB, T], F32R), z("hA_lo", [P, KB, T], F32R)
    z = zoned(zone1)
    woA_hi, woA_lo = z("woA_hi", [P, KB, D], F32R), z("woA_lo", [P, KB, D], F32R)
    z = zoned(zone1)
    q_even, q_odd = (z(n, [P, NCH, 2, CHUNK]) for n in ("q_even", "q_odd"))
    y_last = sb("y_last", [P, 2, D], offset=zone1 + 16 * KIB)
    k_raw = z("k_raw", [P, T])
    v_raw = z("v_raw", [P, T])
    k_both = z("k_both", [P, KV, T])
    v_tok = z("v_tok", [P, TB, P])
    v_swap = z("v_swap", [P, TB, P])
    k_band = z("k_band", [P, NCH, P])
    v_band = z("v_band", [P, NCH, DH])
    logits = z("logits", [P, 2, 4, 2, P])
    probs_t = z("probs_t", [P, 4, 2, P])
    z = zoned(zone2 + 4 * KIB * 12)
    x_in = z("x_in", [P, X_SLOTS, D])
    x_scaled = z("x_scaled", [P, 2, D])
    gain_in = z("gain_in", [P, D])
    z = zoned(zone2)
    k1, k2, k3 = (z(n, [P, NCH, CHUNK]) for n in ("k1", "k2", "k3"))
    q1, q3 = (z(n, [P, NCH, CHUNK]) for n in ("q1", "q3"))
    scores = z("scores", [P, NPAIR, P])
    k_dec_a = z("k_dec_a", [P, NPAIR, CHUNK])
    q_dec_b = z("q_dec_b", [P, NPAIR, CHUNK])
    k_dec = z("k_dec", [P, T])
    q_dec = z("q_dec", [P, T])
    val = z("val", [P, T])
    state = z("state", [P, NPAIR - 1, P])
    z = zoned(zone2 + 4 * KIB * 12)
    tmp1, tmp2, tmp3, rstd = (z(n, [P, T]) for n in ("tmp1", "tmp2", "tmp3", "rstd"))
    silu_q = z("silu_q", [P, T])
    b_cum = z("b_cum", [P, T])
    k_gate = z("k_gate", [P, T])
    scan_keep = z("scan_keep", [P, T])
    z = zoned(zone2)
    hB_hi, hB_lo = z("hB_hi", [P, KB, T], F32R), z("hB_lo", [P, KB, T], F32R)
    z = zoned(zone2)
    woB_hi, woB_lo = z("woB_hi", [P, KB, D], F32R), z("woB_lo", [P, KB, D], F32R)
    z = zoned(zone2 + 64 * KIB)
    gain_post = z("gain_post", [P, D])
    gain_pre = z("gain_pre", [P, D])
    y_norm = z("y_norm", [P, 2, D])
    z = zoned(zone2 + 64 * KIB)
    bias = z("bias", [P, NJ, 4 * P])
    gain_last = z("gain_last", [P, D])

    ps = nc.alloc_psum_tensor("ps", [P, 8, HALF], F32)
    proj_ps = [ps[:, 0:2, :], ps[:, 2:4, :]]
    mix_ps = [ps[:, 4:6, :], ps[:, 6:8, :]]

    def flat(ap):
        return ap.rearrange("p a b -> p (a b)")

    names = """
        ident_loaded const_loaded gain_in_loaded gains_loaded bias_loaded gain_last_loaded k_both_loaded resid_stored out_stored
        x_in_loaded0 x_in_loaded1 x_in_loaded2 x_in_loaded3 x_in_loaded4 x_in_loaded5 x_in_loaded6
        x_in_loaded7 raw_loaded0 raw_loaded1 resid_loaded0 resid_loaded1
        ones_set zeros_set keep_ones keep_set cols_set
        bound_shifted bound_exped bound_inverse bound_prob bound_ready bound_logged
        in_squared in_logged in_rms_ready in_scaled in_turned in_hi_ready in_lo_ready
        hi_ready lo_ready odd_lo_ready block_done last_half
        f_abs f_exp f_log f_neg_ready f_neg_exp f_neg_log log_f_ready log_nf_ready k_gate_ready
        log_f_full b_ready silu_q_ready gate_ready val_ready val_turned val_tok_ready
        k_dec_turned k_dec_tok_ready d3_ready e3q_ready e3k_ready q3_ready k3_ready d21_ready e21_ready
        k2_ready k1_ready dq1_ready eq1_ready q1_ready eb_ready dkd_ready ekd_ready decay_ready
        pair_decay_ready q_dec_b_ready q_dec_ready k_dec_a_ready k_dec_ready
        level3_done level2_done level1_done level0_done level3_kept level2_kept level1_kept level0_kept
        update_done state_step o_done o_squared mean_done mean_logged rstd_ready o_scaled mixed_ready
        mix_hi_ready mix_lo_ready out_tile_done y_squared y_logged y_rms y_scaled x1_ready
        x1_squared x1_logged x1_rms h_scaled h_turned h_hi_ready h_lo_ready
        k_raw_ready v_raw_ready v_turned v_tok_ready zeroB_set q_even_ready q_odd_ready
        k_band_ready v_swap_ready v_band_ready sinks_negated logits_done biased edge_masked max_part max_ready sink_shifted
        exped sum_ready inverse_ready probs_ready probs_turned
        probs_t_ready pv_done o_ready
    """.split()
    S = namedtuple("Semaphores", names)(*(nc.alloc_semaphore(n) for n in names))
    raw_loaded = (S.raw_loaded0, S.raw_loaded1)
    x_in_loaded = (S.x_in_loaded0, S.x_in_loaded1, S.x_in_loaded2, S.x_in_loaded3, S.x_in_loaded4, S.x_in_loaded5,
                   S.x_in_loaded6, S.x_in_loaded7)
    resid_loaded = (S.resid_loaded0, S.resid_loaded1)

    def low_b(m):
        return (S.odd_lo_ready, m // 2 + 1) if m % 2 else (S.lo_ready, FIRST_BO + m // 2 + 1)

    def out_part(w, m):
        half, k = m // 4, m % 4 * 2
        return w[:, k:k + 2, half * HALF:(half + 1) * HALF]

    def raw_part(m):
        return w_raw[:, m % 2].rearrange("p a b -> p (a b)").rearrange("p (a b) -> p a b", a=2)

    def first(value):
        return isinstance(value, int) and value == 0

    def row_tile(dram, t):
        return dram[0, ds(t * P, P), :].rearrange("p (k n) -> p k n", k=KB)

    def mixed_tile(t):
        return mixed[:, :, ds(t * P, P)]

    def gain_row(gains, layer):
        return gains[layer, :].partition_broadcast(P)

    def chunks(buf):
        return buf[:].rearrange("p (n c) -> p n c", c=CHUNK)

    def by_chunk(banks):
        return flat(banks).rearrange("p (n c) -> p n c", c=CHUNK)

    def halves(buf):
        return buf[:].rearrange("p (r e c) -> p r e c", e=2, c=CHUNK)

    def subs(buf):
        return buf[:].rearrange("p (n c) -> p n c", c=SUB)

    mix_flat = [flat(m) for m in mix_ps]

    with nc.Block() as block:

        @block.sync
        def _(sp):
            a_cols = a_w_in[0].rearrange("(k p) n -> p k n", p=P)
            b_cols = b_w_in[0].rearrange("(k p) n -> p k n", p=P)

            def load(slot, source, n):
                if not (isinstance(n, int) and n < 2):
                    sp.wait_ge(raw_loaded[slot], 16)
                    sp.wait_ge(S.lo_ready, n - 1)
                sp.dma_start(w_raw[:, slot], source).then_inc(raw_loaded[slot], 16)

            def a_head(h, first_block=0):
                for j in range(first_block, A_BLOCKS):
                    column = h * P + A_COLUMN[j]
                    if not first(h):
                        column = sp.snap(column)
                    load(j % 2, a_cols[:, :, ds(column, P)], h * A_BLOCKS + (FIRST_A + j))

            def out_weights(w, n, split):
                for m in range(KB):
                    half, k = m // 4, m % 4 * 2
                    if m < 2:
                        sp.wait_ge(S.lo_ready, n + m - 1)
                    else:
                        sp.wait_ge(*split(m - 2))
                    sp.dma_start(raw_part(m),
                                 w[0, k * P:(k + 2) * P, half * HALF:(half + 1) * HALF]
                                 .rearrange("(a p) n -> p a n", p=P)).then_inc(raw_loaded[m % 2], 16)

            def load_x(t):
                sp.dma_start(x_in[:, t], x[0, t * P:(t + 1) * P, :]).then_inc(x_in_loaded[t], 16)

            load_x(0)
            sp.dma_start(gain_in[:], gain_row(norm_pre, 0)).then_inc(S.gain_in_loaded, 16)
            load_x(1)
            load(0, a_cols[:, :, ds(A_COLUMN[0], P)], FIRST_A)
            load_x(2)
            load(1, a_cols[:, :, ds(A_COLUMN[1], P)], FIRST_A + 1)
            load_x(3)
            a_head(0, 2)
            with sp.Fori(1, HEADS) as h:
                a_head(h)
            out_weights(a_w_out, FIRST_AO, lambda m: (S.lo_ready, FIRST_AO + m + 1))
            load(0, b_cols[:, :, D:D + P], FIRST_B)
            load(1, b_cols[:, :, D + P:D + 2 * P], FIRST_B + 1)
            with sp.Fori(1, NJ + 1) as i:
                for j in range(4):
                    column = i * 2 * P + ((GATE_COLUMN if j < 2 else 0) + (j % 2) * P - 2 * P)
                    load(j % 2, b_cols[:, :, ds(column, P)], i * 4 + (FIRST_B - 2 + j))
            out_weights(b_w_out, FIRST_BO, low_b)

        @block.gpsimd
        def _(pool):
            pool.dma_start(ident[:], identity).then_inc(S.ident_loaded, 16)
            pool.dma_start(masks[:], score_masks).then_inc(S.const_loaded, 16)
            with nc.allow_non_contiguous_dma("columns of 1024 numbers"):
                pool.dma_start(lb_tmp[:], a_lb_logits[0].rearrange("(h p) -> p h", p=P))\
                    .then_inc(S.const_loaded, 16)
                pool.dma_start(gn_col[:], a_norm[0].rearrange("(h p) -> p h", p=P))\
                    .then_inc(S.const_loaded, 16)
                for blk in range(2):
                    pool.dma_start(sink[blk * DH:(blk + 1) * DH],
                                   b_sinks[0].rearrange("(j b e) -> b j e", j=NJ, b=2)[blk]
                                   .partition_broadcast(DH)).then_inc(S.const_loaded, 16)
            for t in range(X_SLOTS, TB):
                pool.wait_ge(S.in_scaled, t - X_SLOTS + 1)
                pool.dma_start(x_in[:, t % X_SLOTS], x[0, t * P:(t + 1) * P, :]).then_inc(x_in_loaded[t], 16)
            pool.memset(ones[:], 1.0 / P).then_inc(S.ones_set, 1)
            for t in (k1, k2, q1, scores):
                pool.memset(t[:], 0.0).then_inc(S.zeros_set, 1)

            pool.wait_ge(S.mixed_ready, HEADS)
            pool.dma_start(gain_post[:], gain_row(norm_post, 0)).then_inc(S.gains_loaded, 16)
            pool.dma_start(gain_pre[:], gain_row(norm_pre, 1)).then_inc(S.gains_loaded, 16)

            def load_resid(source, layer, t, slot):
                pool.wait_ge(S.mix_lo_ready, t + (TB * layer + 1))
                pool.dma_start(mixed_tile(t), row_tile(source, t)).then_inc(resid_loaded[slot], 16)

            def store(target, layer, t, stored):
                pool.wait_ge(S.x1_ready, t + (TB * layer + 1))
                pool.dma_start(row_tile(target, t), mixed_tile(t)).then_inc(stored, 16)

            for slot in range(2):
                load_resid(x, 0, slot, slot)
            with pool.Fori(1, TB // 2) as i:
                for slot in range(2):
                    load_resid(x, 0, i * 2 + slot, slot)
                    store(x1_store, 0, i * 2 + (slot - 2), S.resid_stored)
            for t in range(TB - 2, TB):
                store(x1_store, 0, t, S.resid_stored)

            pool.wait_ge(S.out_tile_done, TB)
            pool.memset(q_even[:], 0.0).then_inc(S.zeroB_set, 1)
            pool.memset(q_odd[:], 0.0).then_inc(S.zeroB_set, 1)
            pool.memset(k_band[:, 0, :], 0.0).then_inc(S.zeroB_set, 1)
            pool.memset(v_swap[:, 0, :], 0.0).then_inc(S.zeroB_set, 1)
            pool.wait_ge(S.h_turned, TB)
            pool.dma_start(bias[:], alibi).then_inc(S.bias_loaded, 16)
            pool.dma_start(gain_last[:], gain_row(norm_post, 1)).then_inc(S.gain_last_loaded, 16)
            pool.wait_ge(S.k_raw_ready, 1)
            for g in range(KV):
                for half in range(2):
                    pool.dma_start(k_both[half * DH:(half + 1) * DH, g, :], k_raw[g * DH:(g + 1) * DH, :])\
                        .then_inc(S.k_both_loaded, 16)
            pool.wait_ge(S.k_both_loaded, 16 * 4)
            pool.wait_ge(S.v_tok_ready, 1)
            pool.wait_ge(S.zeroB_set, 4)
            pool.tensor_copy(v_swap[0:DH], v_tok[0:DH]).then_inc(S.v_swap_ready, 1)
            pool.wait_ge(S.v_swap_ready, 1)
            pool.tensor_copy(v_swap[DH:P, 1:TB, :], v_tok[DH:P, 0:TB - 1, :]).then_inc(S.v_swap_ready, 1)
            pool.wait_ge(S.v_swap_ready, 2)

            def bands(g):
                keys = k_both[:, g].rearrange("p (n c) -> p n c", c=CHUNK)
                if g:
                    pool.wait_ge(S.logits_done, g * 8)
                pool.tensor_copy(k_band[:, 1:NCH:2, 0:CHUNK], keys[:, 0:NCH:2, :])
                pool.tensor_copy(k_band[:, 1:NCH:2, CHUNK:P], keys[:, 1:NCH:2, :])
                pool.tensor_copy(k_band[:, 0:NCH:2, 0:CHUNK], keys[:, 0:NCH:2, :])
                pool.tensor_copy(k_band[:, 2:NCH:2, CHUNK:P], keys[:, 1:NCH - 2:2, :])\
                    .then_inc(S.k_band_ready, 2)
                if g:
                    pool.wait_ge(S.pv_done, g * 8)
                cols = slice(g * DH, (g + 1) * DH)
                pool.tensor_copy(v_band[:, 1:NCH:2, :], v_tok[:, :, cols])
                pool.tensor_copy(v_band[:, 0:NCH:2, :], v_swap[:, :, cols]).then_inc(S.v_band_ready, 2)

            for g in range(KV):
                bands(g)

            for m in range(1, KB, 2):
                pool.wait_ge(S.hi_ready, FIRST_BO + m + 1)
                pool.tensor_tensor(out_part(woB_lo, m), raw_part(m), out_part(woB_hi, m).bitcast(F32), ALU.subtract)\
                    .then_inc(S.odd_lo_ready, 1)

            pool.wait_ge(S.resid_stored, 16 * TB)
            for slot in range(2):
                load_resid(x1_store, 1, slot, slot)
            with pool.Fori(1, TB // 2) as i:
                for slot in range(2):
                    load_resid(x1_store, 1, i * 2 + slot, slot)
                    store(out, 1, i * 2 + (slot - 2), S.out_stored)
            for t in range(TB - 2, TB):
                store(out, 1, t, S.out_stored)
            pool.wait_ge(S.out_stored, 16 * TB)

        @block.tensor
        def _(pe):
            def turn(src, dst):
                for k in range(KB):
                    last = pe.transpose(dst[:, k * P:(k + 1) * P], src[:, k * P:(k + 1) * P], ident[:])
                return last

            def three_pass(dst, w_hi, w_lo, v_hi, v_lo, start, stop):
                pe.matmul(dst, w_hi, v_hi, start=start, stop=False)
                pe.matmul(dst, w_lo, v_hi, start=False, stop=False)
                return pe.matmul(dst, w_hi, v_lo, start=False, stop=stop)

            def project(slot, half, h_hi, h_lo, rows=range(KB)):
                toks = slice(half * HALF, (half + 1) * HALF)
                for k in rows:
                    last = three_pass(proj_ps[slot][:, half, :], split_hi[:, slot, k, :], split_lo[:, slot, k, :],
                                      h_hi[:, k, toks], h_lo[:, k, toks], k == 0, k == KB - 1)
                return last

            pe.wait_ge(S.ident_loaded, 16)

            def turn_in(t):
                pe.wait_ge(S.in_scaled, t + 1)
                turn(x_scaled[:, t % 2], mix_flat[t % 2]).then_inc(S.in_turned, 1)

            for t in range(TB // 2 + 1):
                turn_in(t)
            for j in range(2):
                pe.wait_ge(S.lo_ready, j + 1)
                pe.wait_ge(S.in_lo_ready, TB // 2)
                project(j, 0, hA_hi, hA_lo)
                for t in ((TB // 2 + 1, TB // 2 + 2), (TB - 1,))[j]:
                    turn_in(t)
            pe.wait_ge(S.in_lo_ready, TB)
            for j in range(2):
                project(j, 1, hA_hi, hA_lo).then_inc(S.block_done, 1)
            pe.wait_ge(S.ones_set, 1)
            pe.wait_ge(S.zeros_set, 4)

            def turn_values(p):
                pe.wait_ge(S.val_ready, p + 1)
                turn(val, mix_flat[0]).then_inc(S.val_turned, 1)

            def turn_keys(p):
                pe.wait_ge(S.k_dec_ready, p + 1)
                turn(k_dec, mix_flat[1]).then_inc(S.k_dec_turned, 1)

            def level(k, q, dst, done):
                for r in range(NPAIR):
                    last = pe.matmul(dst[:, r * P:(r + 1) * P], flat(k[:])[:, r * P:(r + 1) * P],
                                     flat(q[:])[:, r * P:(r + 1) * P], start=True, stop=True)
                last.then_inc(done, 1)

            def level3(p):
                pe.wait_ge(S.q3_ready, p + 1)
                pe.wait_ge(S.k3_ready, p + 1)
                pe.wait_ge(S.val_tok_ready, p + 1)
                level(k3, q3, mix_flat[0], S.level3_done)

            def updates(p):
                pe.wait_ge(S.val_tok_ready, p + 1)
                pe.wait_ge(S.k_dec_tok_ready, p + 1)
                for r in range(NPAIR - 1):
                    cols = slice(r * P, (r + 1) * P)
                    last = pe.matmul(mix_flat[1][:, cols], k_dec[:, cols], val[:, cols], start=True, stop=True)
                last.then_inc(S.update_done, 1)

            def level2(p):
                pe.wait_ge(S.k2_ready, p + 1)
                pe.wait_ge(S.level3_kept, p + 1)
                level(k2, q3, mix_flat[0], S.level2_done)

            def level1(p):
                pe.wait_ge(S.k1_ready, p + 1)
                pe.wait_ge(S.q1_ready, p + 1)
                pe.wait_ge(S.state_step, p * (NPAIR - 1) + (NPAIR - 1))
                level(k1, q1, mix_flat[1], S.level1_done)

            def level0(p):
                pe.wait_ge(S.k_dec_a_ready, p + 1)
                pe.wait_ge(S.q_dec_b_ready, p + 1)
                pe.wait_ge(S.level2_kept, p + 1)
                for r in range(NPAIR):
                    last = pe.matmul(mix_ps[0][0:CHUNK, 0, r * CHUNK:(r + 1) * CHUNK], k_dec_a[:, r, :],
                                     q_dec_b[:, r, :], start=True, stop=True)
                last.then_inc(S.level0_done, 1)

            def outputs(p):
                pe.wait_ge(S.level1_kept, p + 1)
                pe.wait_ge(S.level0_kept, p + 1)
                pe.wait_ge(S.q_dec_ready, p + 1)
                for r in range(NPAIR):
                    cols = slice(r * P, (r + 1) * P)
                    last = pe.matmul(mix_flat[1][:, cols], val[:, cols], scores[:, r, :], start=True, stop=r == 0)
                    if r:
                        last = pe.matmul(mix_flat[1][:, cols], state[:, r - 1, :], q_dec[:, cols],
                                         start=False, stop=True)
                last.then_inc(S.o_done, 1)

            def means(p):
                pe.wait_ge(S.o_squared, p + 1)
                for half in range(2):
                    last = pe.matmul(mix_ps[0][:, half, :], ones[:], rstd[:, half * HALF:(half + 1) * HALF],
                                     start=True, stop=True)
                last.then_inc(S.mean_done, 1)

            def head_projections(h, between, first_block=0):
                free = ((S.gate_ready, 0), (S.val_ready, 0), (S.log_nf_ready, 1), (S.silu_q_ready, 1))
                for j in range(first_block, A_BLOCKS):
                    pe.wait_ge(S.lo_ready, h * A_BLOCKS + (j + 1))
                    sem, plus = free[j]
                    if plus or not first(h):
                        pe.wait_ge(sem, h + plus)
                    if j == 2:
                        pe.wait_ge(S.f_abs, h + 1)
                    for half in range(2):
                        last = project(j % 2, half, hA_hi, hA_lo)
                        if half == 1:
                            last.then_inc(S.block_done, 1)
                        elif j == A_BLOCKS - 1:
                            last.then_inc(S.last_half, 1)
                        for step in between[2 * j + half]:
                            step(h - 1)

            steps = ((turn_values, turn_keys), (level3, updates), (level2, level1), (level0,), (outputs,),
                     (means,), (), ())
            head_projections(0, ((),) * 8, 2)
            with pe.Fori(1, HEADS) as h:
                head_projections(h, steps)
            for group in steps:
                for step in group:
                    step(HEADS - 1)

            def out_tile(layer, t, slot, weights, free, between=((), ())):
                pe.wait_ge(S.mix_lo_ready, t + (TB * layer + 1))
                for sem, value in free:
                    pe.wait_ge(sem, value)
                w_hi, w_lo = weights
                for half in range(2):
                    cols = slice(half * HALF, (half + 1) * HALF)
                    for k in range(KB):
                        if first(t) and k % 2 == 0:
                            m = half * 4 + k // 2
                            pe.wait_ge(*(low_b(m) if layer else (S.lo_ready, FIRST_AO + m + 1)))
                        last = three_pass(proj_ps[slot][:, half, :], split_hi[:, slot, k, :], split_lo[:, slot, k, :],
                                          w_hi[:, k, cols], w_lo[:, k, cols], k == 0, k == KB - 1)
                    if half:
                        last.then_inc(S.out_tile_done, 1)
                    for step in between[half]:
                        step(NJ - 1)

            def turn_h(t, slot):
                pe.wait_ge(S.h_scaled, t + 1)
                turn(y_norm[:, slot], mix_flat[slot]).then_inc(S.h_turned, 1)

            woA, woB = (woA_hi, woA_lo), (woB_hi, woB_lo)
            out_tile(0, 0, 0, woA, ((S.gate_ready, HEADS),))
            out_tile(0, 1, 1, woA, ((S.val_ready, HEADS),))
            turn_h(0, 0)
            with pe.Fori(1, TB // 2) as i:
                out_tile(0, i * 2, 0, woA, ((S.y_scaled, i * 2 - 1),))
                turn_h(i * 2 - 1, 1)
                out_tile(0, i * 2 + 1, 1, woA, ((S.y_scaled, i * 2),))
                turn_h(i * 2, 0)

            pe.wait_ge(S.lo_ready, FIRST_B + 1)
            pe.wait_ge(S.y_scaled, TB - 1)
            pe.wait_ge(S.h_lo_ready, TB // 2)
            project(0, 0, hB_hi, hB_lo)
            turn_h(TB - 1, 1)
            pe.wait_ge(S.h_lo_ready, TB)
            project(0, 1, hB_hi, hB_lo).then_inc(S.block_done, 1)
            pe.wait_ge(S.lo_ready, FIRST_B + 2)
            pe.wait_ge(S.y_scaled, TB)
            for half in range(2):
                last = project(1, half, hB_hi, hB_lo)
            last.then_inc(S.block_done, 1)
            pe.wait_ge(S.v_raw_ready, 1)

            def logits_of(p, c):
                if c == 0:
                    pe.wait_ge(S.q_even_ready, p * 2 + 2)
                    pe.wait_ge(S.q_odd_ready, p * 2 + 2)
                    pe.wait_ge(S.k_band_ready, p + 1)
                else:
                    pe.wait_ge(S.biased, p * 4 + c)
                for n in range(4):
                    for e, q in enumerate((q_even, q_odd)):
                        col = (2 * n + e) * P
                        last = pe.matmul(mix_flat[0][:, col:col + P], q[:, 4 * c + n].rearrange("p b q -> p (b q)"),
                                         k_band[:, 4 * c + n, :],
                                         start=True, stop=True)
                last.then_inc(S.logits_done, 1)

            def turn_probs(p, c):
                pe.wait_ge(S.probs_ready, p * 4 + (c + 1))
                if c:
                    pe.wait_ge(S.o_ready, p * 4 + c)
                src = logits[:, c % 2].rearrange("p n e k -> p (n e k)")
                turn(src, mix_flat[1]).then_inc(S.probs_turned, 1)

            def values_of(p, c):
                pe.wait_ge(S.probs_t_ready, p * 4 + (c + 1))
                if c == 0:
                    pe.wait_ge(S.v_band_ready, p + 1)
                for n in range(4):
                    for e in range(2):
                        last = pe.matmul(mix_ps[1][e * DH:(e + 1) * DH, 0, n * P:(n + 1) * P],
                                         v_band[:, 4 * c + n, :], probs_t[:, n, e, :], start=True, stop=True)
                last.then_inc(S.pv_done, 1)

            def turn_v(p):
                turn(v_raw, mix_flat[1]).then_inc(S.v_turned, 1)

            def attn(*steps):
                return tuple((lambda p, f=f, c=c: f(p, c)) for f, c in steps)

            L, Tr, V = logits_of, turn_probs, values_of
            attention = ((), attn((L, 0)), (), attn((L, 1)), (), attn((Tr, 0), (L, 2)), attn((V, 0)), (),
                         attn((Tr, 1), (L, 3)), attn((V, 1)), (), attn((Tr, 2)), attn((V, 2)), (), attn((Tr, 3)),
                         attn((V, 3)))

            def step_projections(i, between):
                for j in range(4):
                    pe.wait_ge(S.lo_ready, i * 4 + (FIRST_B + 3 + j))
                    if j < 2:
                        if first(i):
                            pe.wait_ge((S.k_raw_ready, S.v_raw_ready)[j], 1)
                        else:
                            pe.wait_ge(S.q_even_ready, i * 2 + (j - 1))
                            pe.wait_ge(S.q_odd_ready, i * 2 + (j - 1))
                    else:
                        pe.wait_ge(S.gate_ready, i * 2 + (HEADS + j - 1))
                    for quarter in range(4):
                        rows = range(quarter % 2 * (KB // 2), (quarter % 2 + 1) * (KB // 2))
                        last = project(j % 2, quarter // 2, hB_hi, hB_lo, rows)
                        if quarter == 3:
                            last.then_inc(S.block_done, 1)
                        elif quarter == 1 and j == 3:
                            last.then_inc(S.last_half, 1)
                        for step in between[4 * j + quarter]:
                            step(i - 1)

            step_projections(0, ((turn_v,),) + ((),) * 15)
            with pe.Fori(1, NJ) as i:
                step_projections(i, attention)

            for step in attn((L, 0), (L, 1), (Tr, 0), (L, 2), (V, 0), (Tr, 1), (L, 3), (V, 1)):
                step(NJ - 1)

            out_tile(1, 0, 0, woB, ((S.q_even_ready, 2 * NJ - 1), (S.q_odd_ready, 2 * NJ - 1)),
                     (attn((Tr, 2)), attn((V, 2))))
            out_tile(1, 1, 1, woB, ((S.q_even_ready, 2 * NJ), (S.q_odd_ready, 2 * NJ)),
                     (attn((Tr, 3)), attn((V, 3))))
            with pe.Fori(1, TB // 2) as i:
                out_tile(1, i * 2, 0, woB, ((S.y_scaled, i * 2 + (TB - 1)),))
                out_tile(1, i * 2 + 1, 1, woB, ((S.y_scaled, i * 2 + TB),))

        @block.scalar
        def _(act):
            def exp_and_log():
                nc.scalar.preload_act_table_set("natural_log_exp_and_others")

            def inverse_rms(source, junk, col, squared, logged, ready, n, loaded):
                act.wait_ge(S.cols_set, 2)
                for sem, value in loaded:
                    act.wait_ge(sem, value)
                nc.scalar.activation(junk, source, ACT.Square, accum_out=ssq[:, col:col + 1]).then_inc(squared, 1)
                act.wait_ge(squared, n)
                nc.scalar.activation(rms[:, col:col + 1], ssq[:, col:col + 1], ACT.Ln, scale=1.0 / D,
                                     bias=eps_col[:]).then_inc(logged, 1)
                act.wait_ge(logged, n)
                nc.scalar.activation(rms[:, col:col + 1], rms[:, col:col + 1], ACT.Exp, scale=-0.5)\
                    .then_inc(ready, 1)

            def split_block(n, slot, free):
                act.wait_ge(raw_loaded[slot], (n - slot) * 8 + 16)
                if free is not None:
                    act.wait_ge(*free)
                nc.scalar.copy(split_hi[:, slot], w_raw[:, slot]).then_inc(S.hi_ready, 1)

            def split_out_weights(layer, m, w_hi):
                n = (FIRST_AO, FIRST_BO)[layer]
                act.wait_ge(raw_loaded[m % 2], (n + m - m % 2) * 8 + 16)
                if m == 0:
                    act.wait_ge(S.last_half, (HEADS, HEADS + NJ)[layer])
                elif m == KB // 2:
                    act.wait_ge(S.block_done, (BLK_B, BLK_END)[layer])
                nc.scalar.copy(out_part(w_hi, m), raw_part(m)).then_inc(S.hi_ready, 1)

            def norm_in(t):
                loaded = [(x_in_loaded[t], 16)]
                if t >= 2:
                    loaded.append((S.in_turned, t - 1))
                inverse_rms(x_in[:, t % X_SLOTS], x_scaled[:, t % 2], t % 2, S.in_squared, S.in_logged,
                            S.in_rms_ready, t + 1, loaded)

            def high_in(t):
                act.wait_ge(S.in_turned, t + 1)
                nc.scalar.copy(hA_hi[:, :, ds(t * P, P)], mix_flat[t % 2].rearrange("p (k n) -> p k n", k=KB))\
                    .then_inc(S.in_hi_ready, 1)

            exp_and_log()
            for t in range(TB):
                norm_in(t)
                if t in (1, 3):
                    split_block(t // 2, t // 2, None)
                if t:
                    high_in(t - 1)
            high_in(TB - 1)

            act.wait_ge(S.bound_shifted, 1)
            nc.scalar.activation(lb_tmp[:], lb_tmp[:], ACT.Exp).then_inc(S.bound_exped, 1)
            act.wait_ge(S.bound_ready, 1)
            act.wait_ge(S.cols_set, 2)
            nc.scalar.activation(log1mlb_col[:], lb_col[:], ACT.Ln, scale=-1.0, bias=one_col[:])\
                .then_inc(S.bound_logged, 1)

            def value_buffer(p):
                act.wait_ge(S.block_done, p * A_BLOCKS + A_BLOCKS)
                nc.scalar.copy(val[:], flat(proj_ps[1])).then_inc(S.val_ready, 1)

            def values_by_token(p):
                act.wait_ge(S.val_turned, p + 1)
                nc.scalar.copy(val[:], mix_flat[0]).then_inc(S.val_tok_ready, 1)

            def keys_by_token(p):
                act.wait_ge(S.k_dec_turned, p + 1)
                nc.scalar.copy(k_dec[:], mix_flat[1]).then_inc(S.k_dec_tok_ready, 1)

            def forget_gate(h):
                act.wait_ge(S.block_done, h * A_BLOCKS + 1)
                if not first(h):
                    act.wait_ge(S.q1_ready, h)
                nc.scalar.activation(tmp1[:], flat(proj_ps[0]), ACT.Abs).then_inc(S.f_abs, 1)
                act.wait_ge(S.f_abs, h + 1)
                nc.scalar.activation(tmp1[:], tmp1[:], ACT.Exp, scale=-1.0).then_inc(S.f_exp, 1)
                act.wait_ge(S.f_exp, h + 1)
                nc.scalar.activation(tmp1[:], tmp1[:], ACT.Ln, bias=one_col[:]).then_inc(S.f_log, 1)
                act.wait_ge(S.f_neg_ready, h + 1)
                nc.scalar.activation(tmp3[:], tmp3[:], ACT.Exp).then_inc(S.f_neg_exp, 1)
                act.wait_ge(S.f_neg_exp, h + 1)
                nc.scalar.activation(tmp3[:], tmp3[:], ACT.Ln, scale=lb_col[:, ds(h, 1)], bias=one_col[:])\
                    .then_inc(S.f_neg_log, 1)
                act.wait_ge(S.log_nf_ready, h + 1)
                if not first(h):
                    act.wait_ge(S.k_dec_ready, h)
                nc.scalar.activation(k_gate[:], tmp2[:], ACT.Exp, bias=log1mlb_col[:, ds(h, 1)])\
                    .then_inc(S.k_gate_ready, 1)

            def silu_query(h):
                act.wait_ge(S.block_done, h * A_BLOCKS + 2)
                if not first(h):
                    act.wait_ge(S.q_dec_ready, h)
                nc.scalar.activation(silu_q[:], flat(proj_ps[1]), ACT.Silu).then_inc(S.silu_q_ready, 1)

            def silu_gate(h):
                act.wait_ge(S.block_done, h * A_BLOCKS + 3)
                nc.scalar.activation(mixed[:, ds(h, 1), :].rearrange("p a n -> p (a n)"), flat(proj_ps[0]),
                                     ACT.Silu).then_inc(S.gate_ready, 1)

            def decays_near(h):
                act.wait_ge(S.d3_ready, h + 1)
                act.wait_ge(S.k_gate_ready, h + 1)
                nc.scalar.activation(tmp2[:], tmp1[:], ACT.Exp).then_inc(S.e3q_ready, 1)
                nc.scalar.activation(tmp1[:], tmp1[:], ACT.Exp, scale=-1.0).then_inc(S.e3k_ready, 1)
                act.wait_ge(S.d21_ready, h + 1)
                nc.scalar.activation(tmp3[:], tmp3[:], ACT.Exp).then_inc(S.e21_ready, 1)

            def decays_far(h):
                act.wait_ge(S.b_ready, h + 1)
                if not first(h):
                    act.wait_ge(S.k_dec_ready, h)
                nc.scalar.activation(chunk_decay[:], halves(b_cum)[:, :, :, CHUNK - 1], ACT.Exp)\
                    .then_inc(S.decay_ready, 1)
                act.wait_ge(S.q3_ready, h + 1)
                nc.scalar.activation(tmp2[:], b_cum[:], ACT.Exp).then_inc(S.eb_ready, 1)
                act.wait_ge(S.dq1_ready, h + 1)
                nc.scalar.activation(tmp1[:, 0:HALF], tmp1[:, 0:HALF], ACT.Exp).then_inc(S.eq1_ready, 1)
                act.wait_ge(S.dkd_ready, h + 1)
                nc.scalar.activation(tmp3[:], tmp3[:], ACT.Exp).then_inc(S.ekd_ready, 1)

            def keep_level0(p):
                act.wait_ge(S.level1_kept, p + 1)
                act.wait_ge(S.level0_done, p + 1)
                nc.scalar.copy(scores[0:CHUNK, :, CHUNK:P],
                               mix_ps[0][0:CHUNK, 0, :].rearrange("p (r c) -> p r c", c=CHUNK))\
                    .then_inc(S.level0_kept, 1)

            def square_output(p):
                act.wait_ge(S.o_done, p + 1)
                nc.scalar.activation(rstd[:], mix_flat[1], ACT.Square).then_inc(S.o_squared, 1)

            def inverse_head_rms(p):
                act.wait_ge(S.mean_done, p + 1)
                nc.scalar.activation(rstd[:], mix_flat[0], ACT.Ln, bias=eps_col[:]).then_inc(S.mean_logged, 1)
                act.wait_ge(S.mean_logged, p + 1)
                nc.scalar.activation(rstd[:], rstd[:], ACT.Exp, scale=-0.5).then_inc(S.rstd_ready, 1)

            def head(h, previous, following):
                def next_block(j):
                    n = h * A_BLOCKS + j
                    split_block(n, j % 2, (S.block_done, n - 1) if not (first(h) and j < 2) else None)

                if previous:
                    next_block(1)
                    value_buffer(h - 1)
                    values_by_token(h - 1)
                    keys_by_token(h - 1)
                next_block(2)
                forget_gate(h)
                next_block(3)
                if previous:
                    keep_level0(h - 1)
                silu_query(h)
                exp_and_log()
                if previous:
                    square_output(h - 1)
                decays_near(h)
                if previous:
                    inverse_head_rms(h - 1)
                if following:
                    next_block(4)
                silu_gate(h)
                exp_and_log()
                decays_far(h)

            head(0, False, True)
            with act.Fori(1, HEADS - 1) as h:
                head(h, True, True)
            head(HEADS - 1, True, False)
            last = HEADS - 1
            value_buffer(last)
            for k, step in enumerate((values_by_token, keys_by_token, None, None, keep_level0, square_output,
                                      inverse_head_rms, None)):
                split_out_weights(0, k, woA_hi)
                if step:
                    step(last)

            def split_mixed(layer, t, slot, free):
                for sem, value in free:
                    act.wait_ge(sem, value)
                nc.scalar.copy(split_hi[:, slot], mixed_tile(t)).then_inc(S.mix_hi_ready, 1)

            def norm_y(layer, t, slot, buffer):
                loaded = [(S.out_tile_done, t + (TB * layer + 1))]
                if not (isinstance(t, int) and t < 2):
                    loaded.append((S.h_turned, t - 1) if layer == 0 else (S.x1_ready, t + (TB - 1)))
                inverse_rms(flat(proj_ps[slot]), buffer[:, slot], slot, S.y_squared, S.y_logged, S.y_rms,
                            t + (TB * layer + 1), loaded)

            def high_h(t, slot):
                act.wait_ge(S.h_turned, t + 1)
                nc.scalar.copy(hB_hi[:, :, ds(t * P, P)], mix_flat[slot].rearrange("p (k n) -> p k n", k=KB))\
                    .then_inc(S.h_hi_ready, 1)

            def norm_x1(t, slot):
                inverse_rms(mixed_tile(t), y_norm[:, slot].rearrange("p (k n) -> p k n", k=KB), 2 + slot,
                            S.x1_squared, S.x1_logged, S.x1_rms, t + 1, [(S.x1_ready, t + 1)])

            split_mixed(0, 0, 0, ((S.mixed_ready, HEADS),))
            split_mixed(0, 1, 1, ())
            norm_y(0, 0, 0, y_norm)
            norm_x1(0, 0)
            split_mixed(0, 2, 0, ((S.out_tile_done, 1),))
            norm_y(0, 1, 1, y_norm)
            high_h(0, 0)
            norm_x1(1, 1)
            with act.Fori(1, TB // 2 - 1) as i:
                for slot in range(2):
                    t = i * 2 + slot
                    split_mixed(0, t + 1, 1 - slot, ((S.out_tile_done, t),))
                    norm_y(0, t, slot, y_norm)
                    high_h(t - 1, 1 - slot)
                    norm_x1(t, slot)
            for t in (TB - 2, TB - 1):
                slot = t % 2
                if t + 1 < TB:
                    split_mixed(0, t + 1, 1 - slot, ((S.out_tile_done, t),))
                else:
                    split_block(FIRST_B, 0, (S.out_tile_done, TB - 1))
                norm_y(0, t, slot, y_norm)
                high_h(t - 1, 1 - slot)
                norm_x1(t, slot)
            high_h(TB - 1, 1)

            split_block(FIRST_B + 1, 1, (S.out_tile_done, TB))
            split_block(FIRST_B + 2, 0, (S.block_done, BLK_B + 1))
            nc.scalar.copy(k_raw[:], flat(proj_ps[0])).then_inc(S.k_raw_ready, 1)
            split_block(FIRST_B + 3, 1, (S.block_done, BLK_B + 2))
            nc.scalar.copy(v_raw[:], flat(proj_ps[1])).then_inc(S.v_raw_ready, 1)

            def next_blk(i, j):
                split_block(i * 4 + (FIRST_B + 2 + j), j % 2, (S.block_done, i * 4 + (BLK_B + j + 1)))

            def gate(i, blk):
                act.wait_ge(S.block_done, i * 4 + (BLK_B + 3 + blk))
                act.wait_ge(S.resid_stored, 16 * TB) if first(i) and blk == 0 else None
                nc.scalar.activation(mixed[:, ds(i * 2 + blk, 1), :].rearrange("p a n -> p (a n)"),
                                     flat(proj_ps[blk]), ACT.Silu).then_inc(S.gate_ready, 1)

            def even_queries(i, blk):
                act.wait_ge(S.zeroB_set, 4)
                act.wait_ge(S.block_done, i * 4 + (BLK_B + 5 + blk))
                if blk == 0 and not first(i):
                    act.wait_ge(S.logits_done, i * 4)
                nc.scalar.activation(q_even[0:DH, :, blk, :], by_chunk(proj_ps[blk])[0:DH], ACT.Copy, scale=DH ** -0.5)\
                    .then_inc(S.q_even_ready, 1)

            def exp_logits(p, c):
                act.wait_ge(S.sink_shifted, p * 4 + (c + 1))
                buf = c % 2
                nc.scalar.activation(sink_exp[:, buf], sink_exp[:, buf], ACT.Exp)
                for n in range(4):
                    for e in range(2):
                        row = n * 2 + e
                        last = nc.scalar.activation(logits[:, buf, n, e, :], logits[:, buf, n, e, :], ACT.Exp,
                                                    bias=neg_max[:, buf, row:row + 1],
                                                    accum_out=row_sum[:, buf, row:row + 1])
                last.then_inc(S.exped, 1)

            def probs_by_key(p, c):
                act.wait_ge(S.probs_turned, p * 4 + (c + 1))
                nc.scalar.copy(probs_t[:].rearrange("p n e k -> p (n e k)"), mix_flat[1])\
                    .then_inc(S.probs_t_ready, 1)

            X, C = exp_logits, probs_by_key

            def step(i, previous, following):
                attend = (lambda *steps: [f(i - 1, c) for f, c in steps]) if previous else (lambda *steps: None)
                if previous:
                    next_blk(i, 1)
                    even_queries(i - 1, 1)
                attend((X, 0))
                next_blk(i, 2)
                attend((X, 1))
                gate(i, 0)
                exp_and_log()
                attend((C, 0), (X, 2))
                next_blk(i, 3)
                gate(i, 1)
                exp_and_log()
                attend((C, 1), (X, 3), (C, 2))
                if following:
                    next_blk(i, 4)
                even_queries(i, 0)
                attend((C, 3))

            def values_by_token_b():
                act.wait_ge(S.v_turned, 1)
                nc.scalar.copy(v_tok[:].rearrange("p t d -> p (t d)"), mix_flat[1]).then_inc(S.v_tok_ready, 1)

            values_by_token_b()
            step(0, False, True)
            with act.Fori(1, NJ - 1) as i:
                step(i, True, True)
            step(NJ - 1, True, False)
            even_queries(NJ - 1, 1)
            last = NJ - 1

            def weights(*ms):
                for m in ms:
                    split_out_weights(1, m, woB_hi)

            weights(0, 1)
            exp_logits(last, 0)
            weights(2, 3)
            exp_logits(last, 1)
            probs_by_key(last, 0)
            exp_logits(last, 2)
            weights(4, 5)
            probs_by_key(last, 1)

            split_mixed(1, 0, 0, ((S.o_ready, 4 * NJ - 3),))
            weights(6, 7)
            split_mixed(1, 1, 1, ())
            exp_logits(last, 3)
            probs_by_key(last, 2)
            norm_y(1, 0, 0, y_last)
            split_mixed(1, 2, 0, ((S.out_tile_done, TB + 1), (S.o_ready, 4 * NJ - 2)))
            probs_by_key(last, 3)
            norm_y(1, 1, 1, y_last)
            split_mixed(1, 3, 1, ((S.out_tile_done, TB + 2),))
            norm_y(1, 2, 0, y_last)
            act.wait_ge(S.o_ready, 4 * NJ)
            with act.Fori(2, TB // 2) as i:
                split_mixed(1, i * 2, 0, ((S.out_tile_done, i * 2 + (TB - 1)),))
                norm_y(1, i * 2 - 1, 1, y_last)
                split_mixed(1, i * 2 + 1, 1, ((S.out_tile_done, i * 2 + TB),))
                norm_y(1, i * 2, 0, y_last)
            norm_y(1, TB - 1, 1, y_last)

        @block.vector
        def _(dve):
            v = nc.vector

            def split_block(n, slot):
                dve.wait_ge(S.hi_ready, n + 1)
                v.tensor_tensor(split_lo[:, slot], w_raw[:, slot], split_hi[:, slot].bitcast(F32), ALU.subtract)\
                    .then_inc(S.lo_ready, 1)

            def split_out_weights(layer, m, w_hi, w_lo):
                dve.wait_ge(S.hi_ready, (FIRST_AO, FIRST_BO)[layer] + m + 1)
                v.tensor_tensor(out_part(w_lo, m), raw_part(m), out_part(w_hi, m).bitcast(F32), ALU.subtract)\
                    .then_inc(S.lo_ready, 1)

            v.memset(eps_col[:], EPS).then_inc(S.cols_set, 1)
            v.memset(one_col[:], 1.0).then_inc(S.cols_set, 1)
            v.memset(scan_keep[:], 1.0).then_inc(S.keep_ones, 1)
            dve.wait_ge(S.keep_ones, 1)
            v.memset(chunks(scan_keep)[:, :, 0:1], 0.0).then_inc(S.keep_set, 1)

            dve.wait_ge(S.gain_in_loaded, 16)

            def scale_in(t):
                slot = t % 2
                dve.wait_ge(S.in_rms_ready, t + 1)
                v.scalar_tensor_tensor(x_scaled[:, slot], x_in[:, t % X_SLOTS], rms[:, slot:slot + 1], gain_in[:],
                                       ALU.mult, ALU.mult).then_inc(S.in_scaled, 1)

            def low_in(t):
                dve.wait_ge(S.in_hi_ready, t + 1)
                cols = slice(t * P, (t + 1) * P)
                v.tensor_tensor(hA_lo[:, :, cols], mix_flat[t % 2].rearrange("p (k n) -> p k n", k=KB),
                                hA_hi[:, :, cols].bitcast(F32), ALU.subtract).then_inc(S.in_lo_ready, 1)

            for t in range(TB):
                scale_in(t)
                if t in (1, 3):
                    split_block(t // 2, t // 2)
                if t:
                    low_in(t - 1)
            low_in(TB - 1)
            dve.wait_ge(S.const_loaded, 16 * 5)
            v.tensor_tensor(lb_tmp[:], lb_tmp[:], lb_tmp[:], ALU.subtract).then_inc(S.bound_shifted, 1)
            dve.wait_ge(S.bound_exped, 1)
            v.reciprocal(lb_col[:], lb_tmp[:]).then_inc(S.bound_inverse, 1)
            dve.wait_ge(S.bound_inverse, 1)
            v.tensor_tensor(lb_tmp[:], lb_tmp[:], lb_col[:], ALU.mult).then_inc(S.bound_prob, 1)
            dve.wait_ge(S.bound_prob, 1)
            v.tensor_tensor(lb_col[:], lb_tmp[:], lb_tmp[:], ALU.subtract).then_inc(S.bound_prob, 1)
            dve.wait_ge(S.bound_prob, 2)
            v.tensor_scalar(lb_col[:], lb_col[:], 0.0, None, ALU.max).then_inc(S.bound_ready, 1)
            v.tensor_scalar(sink[:], sink[:], -1.0, None, ALU.mult).then_inc(S.sinks_negated, 1)

            dve.wait_ge(S.zeros_set, 4)

            def keep(n, bank, done, kept, p):
                dve.wait_ge(S.zeros_set, 4)
                if n == 2:
                    dve.wait_ge(S.level2_kept, p + 1)
                dve.wait_ge(done, p + 1)
                mask = masks[:, n:n + 1, :].broadcast_to([P, NPAIR, P])
                v.copy_predicated(scores[:], mask, mix_flat[bank].rearrange("p (r c) -> p r c", c=P))\
                    .then_inc(kept, 1)

            def states(p):
                dve.wait_ge(S.update_done, p + 1)
                for r in range(NPAIR - 1):
                    update = mix_flat[1][:, r * P:(r + 1) * P]
                    if r == 0:
                        v.tensor_copy(state[:, 0, :], update).then_inc(S.state_step, 1)
                    else:
                        dve.wait_ge(S.state_step, p * (NPAIR - 1) + r)
                        v.scalar_tensor_tensor(state[:, r, :], state[:, r - 1, :], pair_decay[:, r:r + 1], update,
                                               ALU.mult, ALU.add).then_inc(S.state_step, 1)

            def forget_gate(h):
                f = flat(proj_ps[0])
                dve.wait_ge(S.block_done, h * A_BLOCKS + 1)
                dve.wait_ge(S.f_abs, h + 1)
                v.tensor_scalar(tmp3[:], f, -1.0, 40.0, ALU.mult, ALU.min).then_inc(S.f_neg_ready, 1)
                dve.wait_ge(S.f_log, h + 1)
                v.scalar_tensor_tensor(b_cum[:], f, 0.0, tmp1[:], ALU.min, ALU.subtract)\
                    .then_inc(S.log_f_ready, 1)
                dve.wait_ge(S.log_f_ready, h + 1)
                v.tensor_tensor(tmp2[:], b_cum[:], f, ALU.subtract).then_inc(S.log_nf_ready, 1)

            def cumulate(h):
                dve.wait_ge(S.f_neg_log, h + 1)
                v.tensor_tensor(b_cum[:], b_cum[:], tmp3[:], ALU.add).then_inc(S.log_f_full, 1)
                dve.wait_ge(S.log_f_full, h + 1)
                v.tensor_tensor_scan(b_cum[:], scan_keep[:], b_cum[:], 0.0, ALU.mult, ALU.add)\
                    .then_inc(S.b_ready, 1)

            b_subs, b_chunks, b_halves = subs(b_cum), chunks(b_cum), halves(b_cum)
            b_quads = b_cum[:].rearrange("p (n s c) -> p n s c", s=2, c=SUB)
            HC = CHUNK // 2

            def distances(h):
                dve.wait_ge(S.b_ready, h + 1)
                v.tensor_tensor(subs(tmp1), b_subs, b_subs[:, :, 0:1].broadcast_to([P, T // SUB, SUB]),
                                ALU.subtract).then_inc(S.d3_ready, 1)
                v.tensor_tensor(tmp3[:, 0:HALF].rearrange("p (n c) -> p n c", c=SUB),
                                b_quads[:, :, 1, 0:1].broadcast_to([P, T // SUB // 2, SUB]), b_quads[:, :, 0, :],
                                ALU.subtract)
                v.tensor_tensor(tmp3[:, HALF:T].rearrange("p (n c) -> p n c", c=HC),
                                b_chunks[:, :, HC:HC + 1].broadcast_to([P, NCH, HC]), b_chunks[:, :, 0:HC],
                                ALU.subtract).then_inc(S.d21_ready, 1)

            def near_operands(h):
                dve.wait_ge(S.silu_q_ready, h + 1)
                dve.wait_ge(S.e3q_ready, h + 1)
                if not first(h):
                    dve.wait_ge(S.level2_done, h)
                v.tensor_tensor(flat(q3[:]), silu_q[:], tmp2[:], ALU.mult).then_inc(S.q3_ready, 1)
                dve.wait_ge(S.e3k_ready, h + 1)
                v.tensor_tensor(flat(k3[:]), k_gate[:], tmp1[:], ALU.mult).then_inc(S.k3_ready, 1)
                dve.wait_ge(S.k3_ready, h + 1)
                v.tensor_tensor(tmp1[:, 0:HALF].rearrange("p (n c) -> p n c", c=HC), b_chunks[:, :, HC:CHUNK],
                                b_chunks[:, :, HC:HC + 1].broadcast_to([P, NCH, HC]), ALU.subtract)\
                    .then_inc(S.dq1_ready, 1)
                dve.wait_ge(S.e21_ready, h + 1)
                even = "p (n s c) -> p n s c"
                v.tensor_tensor(flat(k2[:]).rearrange(even, s=2, c=SUB)[:, :, 0, :],
                                k_gate[:].rearrange(even, s=2, c=SUB)[:, :, 0, :],
                                tmp3[:, 0:HALF].rearrange("p (n c) -> p n c", c=SUB), ALU.mult)\
                    .then_inc(S.k2_ready, 1)
                if not first(h):
                    dve.wait_ge(S.level1_done, h)
                v.tensor_tensor(k1[:, :, 0:HC], chunks(k_gate)[:, :, 0:HC],
                                tmp3[:, HALF:T].rearrange("p (n c) -> p n c", c=HC), ALU.mult)\
                    .then_inc(S.k1_ready, 1)
                dve.wait_ge(S.k1_ready, h + 1)
                v.tensor_tensor(chunks(tmp3), b_chunks[:, :, CHUNK - 1:CHUNK].broadcast_to([P, NCH, CHUNK]), b_chunks,
                                ALU.subtract).then_inc(S.dkd_ready, 1)

            def far_operands(h):
                dve.wait_ge(S.eq1_ready, h + 1)
                v.tensor_tensor(q1[:, :, HC:CHUNK], chunks(silu_q)[:, :, HC:CHUNK],
                                tmp1[:, 0:HALF].rearrange("p (n c) -> p n c", c=HC), ALU.mult)\
                    .then_inc(S.q1_ready, 1)
                dve.wait_ge(S.decay_ready, h + 1)
                v.tensor_tensor(pair_decay[:], chunk_decay[:, :, 0], chunk_decay[:, :, 1], ALU.mult)\
                    .then_inc(S.pair_decay_ready, 1)
                dve.wait_ge(S.eb_ready, h + 1)
                if not first(h):
                    dve.wait_ge(S.level0_done, h)
                sq, eb, kg, ekd = halves(silu_q), halves(tmp2), halves(k_gate), halves(tmp3)
                v.tensor_tensor(q_dec_b[:], sq[:, :, 1, :], eb[:, :, 1, :], ALU.mult).then_inc(S.q_dec_b_ready, 1)
                dve.wait_ge(S.ekd_ready, h + 1)
                v.tensor_tensor(k_dec_a[:], kg[:, :, 0, :], ekd[:, :, 0, :], ALU.mult).then_inc(S.k_dec_a_ready, 1)
                if not first(h):
                    dve.wait_ge(S.o_done, h)
                v.tensor_tensor(halves(q_dec)[:, :, 0, :], sq[:, :, 0, :], eb[:, :, 0, :], ALU.mult)
                dve.wait_ge(S.q_dec_b_ready, h + 1)
                v.tensor_tensor(halves(q_dec)[:, :, 1, :], q_dec_b[:],
                                chunk_decay[:, :, 0:1].broadcast_to([P, NPAIR, CHUNK]), ALU.mult)\
                    .then_inc(S.q_dec_ready, 1)
                v.tensor_tensor(halves(k_dec)[:, :, 1, :], kg[:, :, 1, :], ekd[:, :, 1, :], ALU.mult)
                dve.wait_ge(S.k_dec_a_ready, h + 1)
                v.tensor_tensor(halves(k_dec)[:, :, 0, :], k_dec_a[:],
                                chunk_decay[:, :, 1:2].broadcast_to([P, NPAIR, CHUNK]), ALU.mult)\
                    .then_inc(S.k_dec_ready, 1)

            def norm_and_gate(p):
                dve.wait_ge(S.rstd_ready, p + 1)
                v.tensor_tensor(rstd[:], mix_flat[1], rstd[:], ALU.mult).then_inc(S.o_scaled, 1)
                dve.wait_ge(S.o_scaled, p + 1)
                dve.wait_ge(S.gate_ready, p + 1)
                row = mixed[:, ds(p, 1), :].rearrange("p a n -> p (a n)")
                v.scalar_tensor_tensor(row, rstd[:], gn_col[:, ds(p, 1)], row, ALU.mult, ALU.mult)\
                    .then_inc(S.mixed_ready, 1)

            def head(h, previous, following):
                n = h * A_BLOCKS
                if previous:
                    split_block(n + 1, 1)
                    keep(0, 0, S.level3_done, S.level3_kept, h - 1)
                    states(h - 1)
                split_block(n + 2, 0)
                forget_gate(h)
                if previous:
                    keep(1, 0, S.level2_done, S.level2_kept, h - 1)
                    keep(2, 1, S.level1_done, S.level1_kept, h - 1)
                cumulate(h)
                split_block(n + 3, 1)
                distances(h)
                near_operands(h)
                if previous:
                    norm_and_gate(h - 1)
                if following:
                    split_block(n + 4, 0)
                far_operands(h)

            head(0, False, True)
            with dve.Fori(1, HEADS - 1) as h:
                head(h, True, True)
            head(HEADS - 1, True, False)
            last = HEADS - 1
            for k in range(2):
                split_out_weights(0, k, woA_hi, woA_lo)
            keep(0, 0, S.level3_done, S.level3_kept, last)
            states(last)
            keep(1, 0, S.level2_done, S.level2_kept, last)
            for k in range(2, 5):
                split_out_weights(0, k, woA_hi, woA_lo)
            keep(2, 1, S.level1_done, S.level1_kept, last)
            for k in range(5, 7):
                split_out_weights(0, k, woA_hi, woA_lo)
            norm_and_gate(last)
            split_out_weights(0, 7, woA_hi, woA_lo)

            def split_mixed(layer, t, slot):
                dve.wait_ge(S.mix_hi_ready, t + (TB * layer + 1))
                v.tensor_tensor(split_lo[:, slot], mixed_tile(t), split_hi[:, slot].bitcast(F32), ALU.subtract)\
                    .then_inc(S.mix_lo_ready, 1)

            def add_y(layer, t, slot, buffer, gain):
                n = t + (TB * layer + 1)
                dve.wait_ge(S.y_rms, n)
                v.scalar_tensor_tensor(buffer[:, slot], flat(proj_ps[slot]), rms[:, slot:slot + 1], gain[:],
                                       ALU.mult, ALU.mult).then_inc(S.y_scaled, 1)
                dve.wait_ge(S.y_scaled, n)
                dve.wait_ge(resid_loaded[slot], (t - slot) * 8 + (64 * layer + 16))
                v.tensor_tensor(mixed_tile(t), buffer[:, slot].rearrange("p (k n) -> p k n", k=KB), mixed_tile(t),
                                ALU.add).then_inc(S.x1_ready, 1)

            def low_h(t, slot):
                dve.wait_ge(S.h_hi_ready, t + 1)
                cols = ds(t * P, P)
                v.tensor_tensor(hB_lo[:, :, cols], mix_flat[slot].rearrange("p (k n) -> p k n", k=KB),
                                hB_hi[:, :, cols].bitcast(F32), ALU.subtract).then_inc(S.h_lo_ready, 1)

            def scale_h(t, slot):
                dve.wait_ge(S.x1_rms, t + 1)
                v.scalar_tensor_tensor(y_norm[:, slot].rearrange("p (k n) -> p k n", k=KB), mixed_tile(t),
                                       rms[:, 2 + slot:3 + slot], gain_pre[:].rearrange("p (k n) -> p k n", k=KB),
                                       ALU.mult, ALU.mult).then_inc(S.h_scaled, 1)

            split_mixed(0, 0, 0)
            split_mixed(0, 1, 1)
            dve.wait_ge(S.gains_loaded, 32)
            add_y(0, 0, 0, y_norm, gain_post)
            scale_h(0, 0)
            split_mixed(0, 2, 0)
            add_y(0, 1, 1, y_norm, gain_post)
            low_h(0, 0)
            scale_h(1, 1)
            with dve.Fori(1, TB // 2 - 1) as i:
                for slot in range(2):
                    t = i * 2 + slot
                    split_mixed(0, t + 1, 1 - slot)
                    add_y(0, t, slot, y_norm, gain_post)
                    low_h(t - 1, 1 - slot)
                    scale_h(t, slot)
            for t in (TB - 2, TB - 1):
                slot = t % 2
                if t + 1 < TB:
                    split_mixed(0, t + 1, 1 - slot)
                else:
                    split_block(FIRST_B, 0)
                add_y(0, t, slot, y_norm, gain_post)
                low_h(t - 1, 1 - slot)
                scale_h(t, slot)
            low_h(TB - 1, 1)

            split_block(FIRST_B + 1, 1)
            split_block(FIRST_B + 2, 0)
            split_block(FIRST_B + 3, 1)
            dve.wait_ge(S.bias_loaded, 16)
            dve.wait_ge(S.sinks_negated, 1)

            def odd_queries(i, blk):
                dve.wait_ge(S.zeroB_set, 4)
                dve.wait_ge(S.block_done, i * 4 + (BLK_B + 5 + blk))
                if blk == 0 and not first(i):
                    dve.wait_ge(S.logits_done, i * 4)
                v.tensor_scalar(q_odd[DH:P, :, blk, :], by_chunk(proj_ps[blk])[DH:P], DH ** -0.5, None, ALU.mult)\
                    .then_inc(S.q_odd_ready, 1)

            def shift(p, c):
                n, buf = p * 4 + (c + 1), c % 2
                dve.wait_ge(S.logits_done, n)
                lg = logits[:, buf].rearrange("p (r n) e k -> p r (n e k)", r=2)
                table = bias[:, ds(p, 1), :].broadcast_to([P, 2, 4 * P])
                v.tensor_tensor(lg, mix_flat[0].rearrange("p (r m) -> p r m", r=2), table, ALU.add)\
                    .then_inc(S.biased, 1)
                dve.wait_ge(S.biased, n)
                if c == 0:
                    v.memset(logits[:, buf, 0, :, CHUNK:P], MASKED).then_inc(S.edge_masked, 1)
                    dve.wait_ge(S.edge_masked, p + 1)
                by_row = logits[:, buf].rearrange("p n e k -> p (n e) k")
                v.tensor_reduce(neg_max[:, buf], by_row, AX_X, ALU.max).then_inc(S.max_part, 1)
                dve.wait_ge(S.max_part, n)
                rows = neg_max[:, buf].rearrange("p (n e) -> p n e", e=2)
                neg_sinks = sink[:, ds(p, 1), :].broadcast_to([P, 4, 2])
                v.scalar_tensor_tensor(rows, rows, -1.0, neg_sinks, ALU.mult, ALU.min).then_inc(S.max_ready, 1)
                dve.wait_ge(S.max_ready, n)
                v.tensor_tensor(sink_exp[:, buf].rearrange("p (n e) -> p n e", e=2), rows, neg_sinks, ALU.subtract)\
                    .then_inc(S.sink_shifted, 1)

            def normalise(p, c):
                n, buf = p * 4 + (c + 1), c % 2
                by_row = logits[:, buf].rearrange("p n e k -> p (n e) k")
                dve.wait_ge(S.exped, n)
                v.tensor_tensor(row_sum[:, buf], row_sum[:, buf], sink_exp[:, buf], ALU.add).then_inc(S.sum_ready, 1)
                dve.wait_ge(S.sum_ready, n)
                v.reciprocal(row_sum[:, buf], row_sum[:, buf]).then_inc(S.inverse_ready, 1)
                dve.wait_ge(S.inverse_ready, n)
                v.tensor_tensor(by_row, by_row, row_sum[:, buf].unsqueeze(2).broadcast_to([P, 8, P]), ALU.mult)\
                    .then_inc(S.probs_ready, 1)

            def gate_output(p, c):
                dve.wait_ge(S.pv_done, p * 4 + (c + 1))
                dve.wait_ge(S.gate_ready, p * 2 + (HEADS + 2))
                for blk in range(2):
                    dst = mixed[:, ds(p * 2 + blk, 1), 4 * CHUNK * c:4 * CHUNK * (c + 1)]\
                        .rearrange("p a (n q) -> p (a n) q", q=CHUNK)
                    src = mix_ps[1][:, 0, :].rearrange("p (n b q) -> p n b q", b=2, q=CHUNK)[:, :, blk, :]
                    last = v.tensor_tensor(dst, src, dst, ALU.mult)
                last.then_inc(S.o_ready, 1)

            M, N, G = shift, normalise, gate_output

            def step(i, previous, following):
                attend = (lambda *steps: [f(i - 1, c) for f, c in steps]) if previous else (lambda *steps: None)
                n = i * 4 + (FIRST_B + 2)
                if previous:
                    split_block(n + 1, 1)
                    odd_queries(i - 1, 1)
                attend((M, 0), (M, 1))
                split_block(n + 2, 0)
                attend((N, 0), (M, 2), (N, 1), (G, 0))
                split_block(n + 3, 1)
                attend((M, 3), (G, 1), (N, 2), (N, 3), (G, 2))
                if following:
                    split_block(n + 4, 0)
                odd_queries(i, 0)
                attend((G, 3))

            step(0, False, True)
            with dve.Fori(1, NJ - 1) as i:
                step(i, True, True)
            step(NJ - 1, True, False)
            odd_queries(NJ - 1, 1)
            last = NJ - 1

            def weights(m):
                split_out_weights(1, m, woB_hi, woB_lo)

            weights(0)
            shift(last, 0)
            weights(2)
            shift(last, 1)
            normalise(last, 0)
            shift(last, 2)
            normalise(last, 1)
            gate_output(last, 0)
            weights(4)
            gate_output(last, 1)

            split_mixed(1, 0, 0)
            weights(6)
            split_mixed(1, 1, 1)
            shift(last, 3)
            normalise(last, 2)
            normalise(last, 3)
            gate_output(last, 2)
            dve.wait_ge(S.gain_last_loaded, 16)
            add_y(1, 0, 0, y_last, gain_last)
            split_mixed(1, 2, 0)
            gate_output(last, 3)
            add_y(1, 1, 1, y_last, gain_last)
            split_mixed(1, 3, 1)
            add_y(1, 2, 0, y_last, gain_last)
            with dve.Fori(2, TB // 2) as i:
                split_mixed(1, i * 2, 0)
                add_y(1, i * 2 - 1, 1, y_last, gain_last)
                split_mixed(1, i * 2 + 1, 1)
                add_y(1, i * 2, 0, y_last, gain_last)
            add_y(1, TB - 1, 1, y_last, gain_last)


def shape_constants():
    c = np.arange(P)[:, None]
    q = np.arange(P)[None, :]
    same = c // CHUNK == q // CHUNK
    c_sub, q_sub = c % CHUNK // SUB, q % CHUNK // SUB
    near = same & (c_sub == q_sub) & (c <= q)
    middle = same & (q_sub % 2 == 1) & (c_sub == q_sub - 1)
    far = same & (q_sub >= 2) & (c_sub < 2)
    score_masks = np.stack([near, middle, far], axis=1).astype(np.int32)
    heads = KV * 8
    slopes = (2.0 ** (-8.0 * np.arange(1, heads + 1, dtype=np.float32) / heads)).astype(np.float32)
    alibi = np.zeros((2, CHUNK, NJ, 2, 2, 2, CHUNK), np.float32)
    query = np.arange(CHUNK)[:, None]
    key = np.arange(CHUNK)[None, :]
    for odd_chunk in range(2):
        for half in range(2):
            own = half == odd_chunk
            dist = np.abs(query + (0 if own else CHUNK) - key).astype(np.float32)
            for blk in range(2):
                for j in range(NJ):
                    for e in range(2):
                        alibi[blk, :, j, odd_chunk, e, half, :] = -slopes[4 * j + 2 * blk + e] * dist
    return np.eye(P, dtype=np.float32), score_masks, alibi.reshape(P, NJ, 4 * P)


def kernel(**inputs):
    import concourse.bacc as bacc
    from concourse.bass_utils import run_bass_kernel_spmd

    nc = bacc.Bacc("TRN2", target_bir_lowering=False, num_devices=1)
    names = ("x", "norm_pre", "norm_post", "a_w_in", "a_lb_logits", "a_norm", "a_w_out", "b_w_in", "b_sinks",
             "b_w_out")
    arrays = {n: np.ascontiguousarray(inputs[n]) for n in names}
    arrays["identity"], arrays["score_masks"], arrays["alibi"] = shape_constants()
    handles = [nc.dram_tensor(f"in_{n}", a.shape, mybir.dt.from_np(a.dtype), kind="ExternalInput").ap()
               for n, a in arrays.items()]
    out = nc.dram_tensor("out", (1, T, D), F32, kind="ExternalOutput").ap()
    x1_store = nc.dram_tensor("x1_store", (1, T, D), F32).ap()
    build(nc, *handles, out, x1_store)
    result = run_bass_kernel_spmd(nc, [{f"in_{n}": a for n, a in arrays.items()}], core_ids=[0])
    return result.results[0]["out"]
```

```python
from collections import namedtuple

import numpy as np

import concourse.bass as bass
from concourse import mybir

F32 = mybir.dt.float32
F32R = mybir.dt.float32r
I32 = mybir.dt.int32
ALU = mybir.AluOpType
ACT = mybir.ActivationFunctionType
AX_X = mybir.AxisListType.X

P = 128
D = 1024
T = 1024
KB = D // P
X_SLOTS = 4
TB = T // P
HALF = 512
EPS = 1e-6

CHUNK = 64
HC = CHUNK // 2
NCH = T // CHUNK
NPAIR = NCH // 2
SUB = 16
HEADS = D // P
A_BLOCKS = 4
A_COLUMN = (D, 0, 3 * D, 2 * D)

DH = 64
KV = 2
NJ = 4
B_KV_BLOCKS = 2
GATE_COLUMN = D + 2 * KV * DH
MASKED = -1.0e30

FIRST_A = 0
FIRST_B = FIRST_A + A_BLOCKS * HEADS
EARLY = (HEADS - 1, 2 * (NJ - 1))
BLK_B = A_BLOCKS * HEADS
BLK_END = BLK_B + B_KV_BLOCKS + 4 * NJ


def build(nc, x, norm_pre, norm_post, a_w_in, a_lb_logits, a_norm, a_w_out, b_w_in, b_sinks,
          b_w_out, identity, score_masks, alibi, out, x1_store):
    ds = bass.ds

    at = [(nc.sbuf_base + 31) // 32 * 32]

    def sb(name, shape, dt=F32, offset=None):
        size = int(np.prod(shape[1:])) * 4
        if offset is None:
            offset = at[0]
            at[0] += (size + 31) // 32 * 32
        return nc.alloc_sbuf_tensor_at(name, shape, dt, offset=offset)

    KIB = 1024
    ident = sb("ident", [P, P])
    ones = sb("ones", [P, P], F32R)
    masks = sb("masks", [P, 2, P], I32)
    lb_col = sb("lb_col", [P, HEADS])
    lb_tmp = sb("lb_tmp", [P, HEADS])
    log1mlb_col = sb("log1mlb_col", [P, HEADS])
    gn_col = sb("gn_col", [P, HEADS])
    sink = sb("sink", [P, NJ, 2])
    ssq = sb("ssq", [P, 4])
    rms = sb("rms", [P, 4])
    chunk_decay = sb("chunk_decay", [P, NPAIR, 2])
    pair_decay = sb("pair_decay", [P, NPAIR])
    neg_max = sb("neg_max", [P, 2, 8])
    sink_exp = sb("sink_exp", [P, 2, 8])
    row_sum = sb("row_sum", [P, 2, 8])
    eps_col = sb("eps_col", [P, 1])
    one_col = sb("one_col", [P, 1])
    mixed = sb("mixed", [P, KB, T])
    w_raw = sb("w_raw", [P, 2, KB, P])
    split_hi = sb("split_hi", [P, 2, KB, P], F32R)
    split_lo = sb("split_lo", [P, 2, KB, P], F32R)

    zone1 = at[0]
    zone2 = zone1 + 64 * KIB
    zone_end = zone2 + 80 * KIB
    assert zone_end <= nc.sbuf_usable_end, (zone_end, nc.sbuf_usable_end)

    def zoned(zone):
        off = [zone]

        def take(name, shape, dt=F32):
            t = sb(name, shape, dt, offset=off[0])
            off[0] += int(np.prod(shape[1:])) * 4
            return t
        return take

    z = zoned(zone1)
    hA_hi, hA_lo = z("hA_hi", [P, KB, T], F32R), z("hA_lo", [P, KB, T], F32R)
    z = zoned(zone1)
    woA_hi, woA_lo = z("woA_hi", [P, KB, D], F32R), z("woA_lo", [P, KB, D], F32R)
    woA_raw = sb("woA_raw", [P, KB, D], offset=zone1 + 32 * KIB)
    z = zoned(zone1)
    q_even, q_odd = (z(n, [P, NCH, 2, CHUNK]) for n in ("q_even", "q_odd"))
    y_last = sb("y_last", [P, 2, D], offset=zone1 + 16 * KIB)
    k_raw = z("k_raw", [P, T])
    v_raw = z("v_raw", [P, T])
    k_both = z("k_both", [P, KV, T])
    v_tok = z("v_tok", [P, TB, P])
    v_swap = z("v_swap", [P, TB, P])
    k_band = z("k_band", [P, NCH, P])
    v_band = z("v_band", [P, NCH, DH])
    logits = z("logits", [P, 2, 4, 2, P])
    probs_t = z("probs_t", [P, 4, 2, P])
    z = zoned(zone2 + 4 * KIB * 12)
    x_in = z("x_in", [P, X_SLOTS, D])
    x_scaled = z("x_scaled", [P, 2, D])
    gain_in = z("gain_in", [P, D])
    z = zoned(zone2)
    k2, k3, q3 = (z(n, [P, NCH, CHUNK]) for n in ("k2", "k3", "q3"))
    k1, q1 = (z(n, [P, NCH, HC]) for n in ("k1", "q1"))
    scores = z("scores", [P, NPAIR, P])
    k_dec_a = z("k_dec_a", [P, NPAIR, CHUNK])
    q_dec_b = z("q_dec_b", [P, NPAIR, CHUNK])
    k_dec = z("k_dec", [P, T])
    q_dec = z("q_dec", [P, T])
    val = z("val", [P, T])
    state = z("state", [P, NPAIR - 1, P])
    square_lo = sb("square_lo", [P, T], F32R, offset=zone2 + 6 * 4 * KIB)
    square_hi = sb("square_hi", [P, T], F32R, offset=zone2 + 7 * 4 * KIB)
    z = zoned(zone2 + 4 * KIB * 12)
    tmp1, tmp2, tmp3, rstd = (z(n, [P, T]) for n in ("tmp1", "tmp2", "tmp3", "rstd"))
    silu_q = z("silu_q", [P, T])
    b_cum = z("b_cum", [P, T])
    k_gate = z("k_gate", [P, T])
    scan_keep = z("scan_keep", [P, T])
    z = zoned(zone2)
    hB_hi, hB_lo = z("hB_hi", [P, KB, T], F32R), z("hB_lo", [P, KB, T], F32R)
    z = zoned(zone2)
    woB_hi, woB_lo = z("woB_hi", [P, KB, D], F32R), z("woB_lo", [P, KB, D], F32R)
    woB_raw = sb("woB_raw", [P, KB, D], offset=zone2 + 32 * KIB)
    z = zoned(zone2 + 64 * KIB)
    gain_post = z("gain_post", [P, D])
    gain_pre = z("gain_pre", [P, D])
    y_norm = z("y_norm", [P, 2, D])
    z = zoned(zone2 + 64 * KIB)
    bias = z("bias", [P, NJ, 4 * P])
    gain_last = z("gain_last", [P, D])

    ps = nc.alloc_psum_tensor("ps", [P, 8, HALF], F32)
    proj_ps = [ps[:, 0:2, :], ps[:, 2:4, :]]
    mix_ps = [ps[:, 4:6, :], ps[:, 6:8, :]]

    def flat(ap):
        return ap.rearrange("p a b -> p (a b)")

    names = """
        ident_loaded const_loaded gain_in_loaded gains_loaded bias_loaded gain_last_loaded k_both_loaded
        resid_stored out_stored last_stored
        x_in_loaded0 x_in_loaded1 x_in_loaded2 x_in_loaded3 x_in_loaded4 x_in_loaded5 x_in_loaded6
        x_in_loaded7 raw_loaded0 raw_loaded1 resid_loaded0 resid_loaded1
        ones_set zeros_set keep_ones keep_set cols_set
        bound_shifted bound_exped bound_inverse bound_prob bound_ready bound_logged
        in_squared in_logged in_rms_ready in_scaled in_turned in_hi_ready in_lo_ready
        hi_ready lo_ready block_done last_half out_w_hi out_w_even_lo out_w_odd_lo
        out_w_loaded0 out_w_loaded1 out_w_loaded2 out_w_loaded3 out_w_loaded4 out_w_loaded5 out_w_loaded6 out_w_loaded7
        f_abs f_exp f_log f_neg_ready f_neg_exp f_neg_log log_f_ready log_nf_ready k_gate_ready
        log_f_full b_ready silu_q_ready gate_ready val_ready val_turned val_tok_ready
        k_dec_turned k_dec_tok_ready d3_ready e3q_ready e3k_ready q3_ready k3_ready d21_ready e21_ready
        k2_ready k1_ready dq1_ready eq1_ready q1_ready eb_ready dkd_ready ekd_ready decay_ready
        pair_decay_ready q_dec_b_ready q_dec_ready k_dec_a_ready k_dec_ready
        level3_done level2_done level1_done level0_done level3_kept level2_kept level1_kept level0_kept
        update_done state_step o_done o_squared square_hi_ready square_lo_ready mean_done mean_logged
        rstd_ready o_scaled mixed_ready
        early_hi_ready early_lo_ready mix_hi_ready mix_lo_ready out_tile_done y_squared y_logged y_rms y_scaled x1_ready
        x1_squared x1_logged x1_rms h_scaled h_turned h_hi_ready h_lo_ready
        k_raw_ready v_raw_ready v_turned v_tok_ready zeroB_set q_even_ready q_odd_ready
        k_band_ready v_swap_ready v_band_ready sinks_negated logits_done biased edge_masked max_part
        max_ready sink_shifted exped sum_ready inverse_ready probs_ready probs_turned
        probs_t_ready pv_done o_ready
    """.split()
    S = namedtuple("Semaphores", names)(*(nc.alloc_semaphore(n) for n in names))
    raw_loaded = (S.raw_loaded0, S.raw_loaded1)
    x_in_loaded = (S.x_in_loaded0, S.x_in_loaded1, S.x_in_loaded2, S.x_in_loaded3, S.x_in_loaded4, S.x_in_loaded5,
                   S.x_in_loaded6, S.x_in_loaded7)
    out_w_loaded = (S.out_w_loaded0, S.out_w_loaded1, S.out_w_loaded2, S.out_w_loaded3,
                    S.out_w_loaded4, S.out_w_loaded5, S.out_w_loaded6, S.out_w_loaded7)
    resid_loaded = (S.resid_loaded0, S.resid_loaded1)

    def low_part(layer, m):
        return (S.out_w_odd_lo if m % 2 else S.out_w_even_lo), 4 * layer + m // 2 + 1

    def out_part(w, m):
        half, k = m // 4, m % 4 * 2
        return w[:, k:k + 2, half * HALF:(half + 1) * HALF]

    def first(value):
        return isinstance(value, int) and value == 0

    def row_tile(dram, t):
        return dram[0, ds(t * P, P), :].rearrange("p (k n) -> p k n", k=KB)

    def mixed_tile(t):
        return mixed[:, :, ds(t * P, P)]

    def gain_row(gains, layer):
        return gains[layer, :].partition_broadcast(P)

    def chunks(buf):
        return buf[:].rearrange("p (n c) -> p n c", c=CHUNK)

    def by_chunk(banks):
        return flat(banks).rearrange("p (n c) -> p n c", c=CHUNK)

    def halves(buf):
        return buf[:].rearrange("p (r e c) -> p r e c", e=2, c=CHUNK)

    def subs(buf):
        return buf[:].rearrange("p (n c) -> p n c", c=SUB)

    mix_flat = [flat(m) for m in mix_ps]

    with nc.Block() as block:

        @block.sync
        def _(sp):
            a_cols = a_w_in[0].rearrange("(k p) n -> p k n", p=P)
            b_cols = b_w_in[0].rearrange("(k p) n -> p k n", p=P)

            def load(slot, source, n):
                if not (isinstance(n, int) and n < 2):
                    sp.wait_ge(raw_loaded[slot], 16)
                    sp.wait_ge(S.lo_ready, n - 1)
                sp.dma_start(w_raw[:, slot], source).then_inc(raw_loaded[slot], 16)

            def a_head(h, first_block=0):
                for j in range(first_block, A_BLOCKS):
                    column = h * P + A_COLUMN[j]
                    if not first(h):
                        column = sp.snap(column)
                    load(j % 2, a_cols[:, :, ds(column, P)], h * A_BLOCKS + (FIRST_A + j))

            def out_weights(layer, w, w_raw_place):
                for m in range(KB):
                    half, k = m // 4, m % 4 * 2
                    if m == 0:
                        sp.wait_ge(S.last_half, (HEADS, HEADS + NJ)[layer])
                    elif half and k == 0:
                        sp.wait_ge(S.block_done, (BLK_B, BLK_END)[layer])
                    sp.dma_start(out_part(w_raw_place, m),
                                 w[0, k * P:(k + 2) * P, half * HALF:(half + 1) * HALF]
                                 .rearrange("(a p) n -> p a n", p=P)).then_inc(out_w_loaded[m], 16)

            def load_x(t):
                sp.dma_start(x_in[:, t], x[0, t * P:(t + 1) * P, :]).then_inc(x_in_loaded[t], 16)

            load_x(0)
            sp.dma_start(gain_in[:], gain_row(norm_pre, 0)).then_inc(S.gain_in_loaded, 16)
            load_x(1)
            load(0, a_cols[:, :, ds(A_COLUMN[0], P)], FIRST_A)
            load_x(2)
            load(1, a_cols[:, :, ds(A_COLUMN[1], P)], FIRST_A + 1)
            load_x(3)
            a_head(0, 2)
            with sp.Fori(1, HEADS) as h:
                a_head(h)
            out_weights(0, a_w_out, woA_raw)
            load(0, b_cols[:, :, D:D + P], FIRST_B)
            load(1, b_cols[:, :, D + P:D + 2 * P], FIRST_B + 1)
            with sp.Fori(1, NJ + 1) as i:
                for j in range(4):
                    column = i * 2 * P + ((GATE_COLUMN if j < 2 else 0) + (j % 2) * P - 2 * P)
                    load(j % 2, b_cols[:, :, ds(column, P)], i * 4 + (FIRST_B - 2 + j))
            out_weights(1, b_w_out, woB_raw)

            tokens = slice((TB - 1) * P, T)
            for half in range(2):
                k = slice(half * KB // 2, (half + 1) * KB // 2)
                sp.wait_ge(S.x1_ready, 2 * TB + half)
                sp.dma_start(row_tile(out, TB - 1)[:, k], mixed[:, k, tokens]).then_inc(S.last_stored, 16)
            sp.wait_ge(S.last_stored, 32)

        @block.gpsimd
        def _(pool):
            pool.dma_start(ident[:], identity).then_inc(S.ident_loaded, 16)
            pool.dma_start(masks[:], score_masks).then_inc(S.const_loaded, 16)
            with nc.allow_non_contiguous_dma("columns of 1024 numbers"):
                pool.dma_start(lb_tmp[:], a_lb_logits[0].rearrange("(h p) -> p h", p=P))\
                    .then_inc(S.const_loaded, 16)
                pool.dma_start(gn_col[:], a_norm[0].rearrange("(h p) -> p h", p=P))\
                    .then_inc(S.const_loaded, 16)
                for blk in range(2):
                    pool.dma_start(sink[blk * DH:(blk + 1) * DH],
                                   b_sinks[0].rearrange("(j b e) -> b j e", j=NJ, b=2)[blk]
                                   .partition_broadcast(DH)).then_inc(S.const_loaded, 16)
            for t in range(X_SLOTS, TB):
                pool.wait_ge(S.in_scaled, t - X_SLOTS + 1)
                pool.dma_start(x_in[:, t % X_SLOTS], x[0, t * P:(t + 1) * P, :]).then_inc(x_in_loaded[t], 16)
            pool.memset(ones[:].bitcast(F32), 1.0 / P).then_inc(S.ones_set, 1)
            for t in (k2, scores):
                pool.memset(t[:], 0.0).then_inc(S.zeros_set, 1)

            def low_weights(layer, raw, w_hi, w_lo):
                for m in range(0, KB, 2):
                    pool.wait_ge(S.out_w_hi, KB * layer + m + 1)
                    pool.tensor_tensor(out_part(w_lo, m), out_part(raw, m), out_part(w_hi, m).bitcast(F32),
                                       ALU.subtract).then_inc(S.out_w_even_lo, 1)

            low_weights(0, woA_raw, woA_hi, woA_lo)
            pool.wait_ge(S.mixed_ready, HEADS)
            pool.dma_start(gain_post[:], gain_row(norm_post, 0)).then_inc(S.gains_loaded, 16)
            pool.dma_start(gain_pre[:], gain_row(norm_pre, 1)).then_inc(S.gains_loaded, 16)

            def load_resid(source, layer, t, slot):
                pool.wait_ge(S.mix_lo_ready, t + (TB * layer + 1))
                if not (isinstance(t, int) and t + layer < 2):
                    pool.wait_ge(resid_loaded[slot], (t - slot) * 8 + 64 * layer)
                pool.dma_start(mixed_tile(t), row_tile(source, t)).then_inc(resid_loaded[slot], 16)

            def store(target, layer, t, stored):
                pool.wait_ge(S.x1_ready, t + (TB * layer + 1))
                pool.dma_start(row_tile(target, t), mixed_tile(t)).then_inc(stored, 16)

            for slot in range(2):
                load_resid(x, 0, slot, slot)
            with pool.Fori(1, TB // 2) as i:
                for slot in range(2):
                    load_resid(x, 0, i * 2 + slot, slot)
                    store(x1_store, 0, i * 2 + (slot - 2), S.resid_stored)
            for t in range(TB - 2, TB):
                store(x1_store, 0, t, S.resid_stored)

            pool.wait_ge(S.out_tile_done, TB)
            pool.memset(q_even[:], 0.0).then_inc(S.zeroB_set, 1)
            pool.memset(q_odd[:], 0.0).then_inc(S.zeroB_set, 1)
            pool.memset(k_band[:, 0, :], 0.0).then_inc(S.zeroB_set, 1)
            pool.memset(v_swap[:, 0, :], 0.0).then_inc(S.zeroB_set, 1)
            pool.wait_ge(S.h_turned, TB)
            pool.dma_start(bias[:], alibi).then_inc(S.bias_loaded, 16)
            pool.dma_start(gain_last[:], gain_row(norm_post, 1)).then_inc(S.gain_last_loaded, 16)
            pool.wait_ge(S.k_raw_ready, 1)
            for g in range(KV):
                for half in range(2):
                    pool.dma_start(k_both[half * DH:(half + 1) * DH, g, :], k_raw[g * DH:(g + 1) * DH, :])\
                        .then_inc(S.k_both_loaded, 16)
            pool.wait_ge(S.k_both_loaded, 16 * 4)
            pool.wait_ge(S.v_tok_ready, 1)
            pool.wait_ge(S.zeroB_set, 4)
            pool.tensor_copy(v_swap[0:DH], v_tok[0:DH]).then_inc(S.v_swap_ready, 1)
            pool.wait_ge(S.v_swap_ready, 1)
            pool.tensor_copy(v_swap[DH:P, 1:TB, :], v_tok[DH:P, 0:TB - 1, :]).then_inc(S.v_swap_ready, 1)
            pool.wait_ge(S.v_swap_ready, 2)

            def bands(g):
                keys = k_both[:, g].rearrange("p (n c) -> p n c", c=CHUNK)
                if g:
                    pool.wait_ge(S.logits_done, g * 8)
                pool.tensor_copy(k_band[:, 1:NCH:2, 0:CHUNK], keys[:, 0:NCH:2, :])
                pool.tensor_copy(k_band[:, 1:NCH:2, CHUNK:P], keys[:, 1:NCH:2, :])
                pool.tensor_copy(k_band[:, 0:NCH:2, 0:CHUNK], keys[:, 0:NCH:2, :])
                pool.tensor_copy(k_band[:, 2:NCH:2, CHUNK:P], keys[:, 1:NCH - 2:2, :])\
                    .then_inc(S.k_band_ready, 2)
                if g:
                    pool.wait_ge(S.pv_done, g * 8)
                cols = slice(g * DH, (g + 1) * DH)
                pool.tensor_copy(v_band[:, 1:NCH:2, :], v_tok[:, :, cols])
                pool.tensor_copy(v_band[:, 0:NCH:2, :], v_swap[:, :, cols]).then_inc(S.v_band_ready, 2)

            for g in range(KV):
                bands(g)

            low_weights(1, woB_raw, woB_hi, woB_lo)

            pool.wait_ge(S.resid_stored, 16 * TB)
            for slot in range(2):
                load_resid(x1_store, 1, slot, slot)
            with pool.Fori(1, TB // 2) as i:
                for slot in range(2):
                    load_resid(x1_store, 1, i * 2 + slot, slot)
                    store(out, 1, i * 2 + (slot - 2), S.out_stored)
            store(out, 1, TB - 2, S.out_stored)
            pool.wait_ge(S.out_stored, 16 * (TB - 1))

        @block.tensor
        def _(pe):
            def turn(src, dst):
                for k in range(KB):
                    last = pe.transpose(dst[:, k * P:(k + 1) * P], src[:, k * P:(k + 1) * P], ident[:])
                return last

            def three_pass(dst, w_hi, w_lo, v_hi, v_lo, start, stop):
                pe.matmul(dst, w_hi, v_hi, start=start, stop=False)
                pe.matmul(dst, w_lo, v_hi, start=False, stop=False)
                return pe.matmul(dst, w_hi, v_lo, start=False, stop=stop)

            def project(slot, half, h_hi, h_lo, rows=range(KB)):
                toks = slice(half * HALF, (half + 1) * HALF)
                for k in rows:
                    last = three_pass(proj_ps[slot][:, half, :], split_hi[:, slot, k, :], split_lo[:, slot, k, :],
                                      h_hi[:, k, toks], h_lo[:, k, toks], k == 0, k == KB - 1)
                return last

            pe.wait_ge(S.ident_loaded, 16)

            def turn_in(t):
                pe.wait_ge(S.in_scaled, t + 1)
                turn(x_scaled[:, t % 2], mix_flat[t % 2]).then_inc(S.in_turned, 1)

            for t in range(TB // 2 + 1):
                turn_in(t)
            for j in range(2):
                pe.wait_ge(S.lo_ready, j + 1)
                pe.wait_ge(S.in_lo_ready, TB // 2)
                project(j, 0, hA_hi, hA_lo, range(KB // 2))
                turn_in(TB // 2 + 1 + 2 * j)
                project(j, 0, hA_hi, hA_lo, range(KB // 2, KB))
                if j == 0:
                    turn_in(TB // 2 + 2)
            pe.wait_ge(S.in_lo_ready, TB)
            for j in range(2):
                project(j, 1, hA_hi, hA_lo).then_inc(S.block_done, 1)
            pe.wait_ge(S.ones_set, 1)
            pe.wait_ge(S.zeros_set, 2)

            def turn_values(p):
                pe.wait_ge(S.val_ready, p + 1)
                turn(val, mix_flat[0]).then_inc(S.val_turned, 1)

            def turn_keys(p):
                pe.wait_ge(S.k_dec_ready, p + 1)
                turn(k_dec, mix_flat[1]).then_inc(S.k_dec_turned, 1)

            def level(k, q, dst, done):
                for r in range(NPAIR):
                    last = pe.matmul(dst[:, r * P:(r + 1) * P], flat(k[:])[:, r * P:(r + 1) * P],
                                     flat(q[:])[:, r * P:(r + 1) * P], start=True, stop=True)
                last.then_inc(done, 1)

            def level3(p):
                pe.wait_ge(S.q3_ready, p + 1)
                pe.wait_ge(S.k3_ready, p + 1)
                pe.wait_ge(S.val_tok_ready, p + 1)
                level(k3, q3, mix_flat[0], S.level3_done)

            def updates(p):
                pe.wait_ge(S.val_tok_ready, p + 1)
                pe.wait_ge(S.k_dec_tok_ready, p + 1)
                for r in range(NPAIR - 1):
                    cols = slice(r * P, (r + 1) * P)
                    last = pe.matmul(mix_flat[1][:, cols], k_dec[:, cols], val[:, cols], start=True, stop=True)
                last.then_inc(S.update_done, 1)

            def level2(p):
                pe.wait_ge(S.k2_ready, p + 1)
                pe.wait_ge(S.level3_kept, p + 1)
                level(k2, q3, mix_flat[0], S.level2_done)

            def level1(p):
                pe.wait_ge(S.k1_ready, p + 1)
                pe.wait_ge(S.q1_ready, p + 1)
                pe.wait_ge(S.state_step, p * (NPAIR - 1) + (NPAIR - 1))
                for n in range(NCH):
                    row, col = n % 2 * CHUNK, n // 2 * HC
                    last = pe.matmul(mix_flat[1][row:row + HC, col:col + HC], k1[:, n, :], q1[:, n, :],
                                     start=True, stop=True)
                last.then_inc(S.level1_done, 1)

            def level0(p):
                pe.wait_ge(S.k_dec_a_ready, p + 1)
                pe.wait_ge(S.q_dec_b_ready, p + 1)
                pe.wait_ge(S.level2_kept, p + 1)
                for r in range(NPAIR):
                    last = pe.matmul(mix_ps[0][0:CHUNK, 0, r * CHUNK:(r + 1) * CHUNK], k_dec_a[:, r, :],
                                     q_dec_b[:, r, :], start=True, stop=True)
                last.then_inc(S.level0_done, 1)

            def outputs(p):
                pe.wait_ge(S.level1_kept, p + 1)
                pe.wait_ge(S.level0_kept, p + 1)
                pe.wait_ge(S.q_dec_ready, p + 1)
                for r in range(NPAIR):
                    cols = slice(r * P, (r + 1) * P)
                    last = pe.matmul(mix_flat[1][:, cols], val[:, cols], scores[:, r, :], start=True, stop=r == 0)
                    if r:
                        last = pe.matmul(mix_flat[1][:, cols], state[:, r - 1, :], q_dec[:, cols],
                                         start=False, stop=True)
                last.then_inc(S.o_done, 1)

            def means(p):
                pe.wait_ge(S.square_lo_ready, p + 1)
                for half in range(2):
                    toks = slice(half * HALF, (half + 1) * HALF)
                    pe.matmul(mix_ps[0][:, half, :], ones[:], square_hi[:, toks], start=True, stop=False)
                    last = pe.matmul(mix_ps[0][:, half, :], ones[:], square_lo[:, toks], start=False, stop=True)
                last.then_inc(S.mean_done, 1)

            def head_projections(h, between, first_block=0):
                free = ((S.gate_ready, 0), (S.val_ready, 0), (S.log_nf_ready, 1), (S.silu_q_ready, 1))
                for j in range(first_block, A_BLOCKS):
                    pe.wait_ge(S.lo_ready, h * A_BLOCKS + (j + 1))
                    sem, plus = free[j]
                    if plus or not first(h):
                        pe.wait_ge(sem, h + plus)
                    if j == 2:
                        pe.wait_ge(S.f_abs, h + 1)
                    for half in range(2):
                        last = project(j % 2, half, hA_hi, hA_lo)
                        if half == 1:
                            last.then_inc(S.block_done, 1)
                        elif j == A_BLOCKS - 1:
                            last.then_inc(S.last_half, 1)
                        for step in between[2 * j + half]:
                            step(h - 1)

            steps = ((turn_values, turn_keys), (level3, updates), (level2, level1), (level0,), (outputs,),
                     (means,), (), ())
            head_projections(0, ((),) * 8, 2)
            with pe.Fori(1, HEADS) as h:
                head_projections(h, steps)
            last_head = HEADS - 1

            def early(t, half, *rows):
                early_rows(0, t, half, range(*rows))

            def out_rows(layer, slot, half, rows):
                w_hi, w_lo = ((woA_hi, woA_lo), (woB_hi, woB_lo))[layer]
                cols = slice(half * HALF, (half + 1) * HALF)
                for k in rows:
                    last = three_pass(proj_ps[slot][:, half, :], split_hi[:, slot, k, :], split_lo[:, slot, k, :],
                                      w_hi[:, k, cols], w_lo[:, k, cols], k == 0, k == KB - 1)
                return last

            def early_rows(layer, t, half, rows):
                if rows[0] == 0 and half == 0:
                    pe.wait_ge(S.early_lo_ready, 2 * layer + t + 1)
                    banks = (((S.gate_ready, HEADS),), ((S.val_ready, HEADS),),
                             ((S.q_even_ready, 2 * NJ - 1), (S.q_odd_ready, 2 * NJ - 1)),
                             ((S.q_even_ready, 2 * NJ), (S.q_odd_ready, 2 * NJ)))[2 * layer + t]
                    for sem, value in banks:
                        pe.wait_ge(sem, value)
                for k in rows:
                    if t == 0 and k % 2 == 0:
                        pe.wait_ge(*low_part(layer, half * 4 + k // 2))
                    out_rows(layer, t, half, range(k, k + 1))

            def out_tile(layer, t, slot):
                pe.wait_ge(S.mix_lo_ready, t + (TB * layer + 1))
                pe.wait_ge(S.y_scaled, t + (TB * layer - 1))
                for half in range(2):
                    last = out_rows(layer, slot, half, range(KB))
                last.then_inc(S.out_tile_done, 1)

            def turn_h(t, slot):
                pe.wait_ge(S.h_scaled, t + 1)
                turn(y_norm[:, slot], mix_flat[slot]).then_inc(S.h_turned, 1)

            turn_values(last_head)
            turn_keys(last_head)
            early(0, 0, 0, 2)
            level3(last_head)
            updates(last_head)
            early(0, 0, 2, 5)
            level2(last_head)
            level1(last_head)
            early(0, 0, 5, EARLY[0])
            early(0, 1, 0, 2)
            level0(last_head)
            early(0, 1, 2, 4)
            outputs(last_head)
            early(0, 1, 4, EARLY[0])
            early(1, 0, 0, 3)
            means(last_head)
            early(1, 0, 3, EARLY[0])
            early(1, 1, 0, 4)
            pe.wait_ge(S.mix_lo_ready, 1)
            for half in range(2):
                last = out_rows(0, 0, half, range(EARLY[0], KB))
            last.then_inc(S.out_tile_done, 1)
            pe.wait_ge(S.mix_lo_ready, 2)
            out_rows(0, 1, 0, range(EARLY[0], KB))
            out_rows(0, 1, 1, range(4, KB)).then_inc(S.out_tile_done, 1)
            with pe.Fori(1, TB // 2) as i:
                for slot in range(2):
                    out_tile(0, i * 2 + slot, slot)
                    turn_h(i * 2 + (slot - 2), slot)
            turn_h(TB - 2, 0)

            pe.wait_ge(S.lo_ready, FIRST_B + 1)
            pe.wait_ge(S.y_scaled, TB - 1)
            pe.wait_ge(S.h_lo_ready, TB // 2)
            project(0, 0, hB_hi, hB_lo)
            pe.wait_ge(S.lo_ready, FIRST_B + 2)
            pe.wait_ge(S.y_scaled, TB)
            project(1, 0, hB_hi, hB_lo, range(KB // 2))
            turn_h(TB - 1, 1)
            project(1, 0, hB_hi, hB_lo, range(KB // 2, KB))
            pe.wait_ge(S.h_lo_ready, TB)
            for slot in range(2):
                project(slot, 1, hB_hi, hB_lo).then_inc(S.block_done, 1)

            def logits_of(p, c):
                if c == 0:
                    pe.wait_ge(S.q_even_ready, p * 2 + 2)
                    pe.wait_ge(S.q_odd_ready, p * 2 + 2)
                    pe.wait_ge(S.k_band_ready, p + 1)
                else:
                    pe.wait_ge(S.biased, p * 4 + c)
                for n in range(4):
                    for e, q in enumerate((q_even, q_odd)):
                        col = (2 * n + e) * P
                        last = pe.matmul(mix_flat[0][:, col:col + P], q[:, 4 * c + n].rearrange("p b q -> p (b q)"),
                                         k_band[:, 4 * c + n, :],
                                         start=True, stop=True)
                last.then_inc(S.logits_done, 1)

            def turn_probs(p, c):
                pe.wait_ge(S.probs_ready, p * 4 + (c + 1))
                if c:
                    pe.wait_ge(S.o_ready, p * 4 + c)
                src = logits[:, c % 2].rearrange("p n e k -> p (n e k)")
                turn(src, mix_flat[1]).then_inc(S.probs_turned, 1)

            def values_of(p, c):
                pe.wait_ge(S.probs_t_ready, p * 4 + (c + 1))
                if c == 0:
                    pe.wait_ge(S.v_band_ready, p + 1)
                for n in range(4):
                    for e in range(2):
                        last = pe.matmul(mix_ps[1][e * DH:(e + 1) * DH, 0, n * P:(n + 1) * P],
                                         v_band[:, 4 * c + n, :], probs_t[:, n, e, :], start=True, stop=True)
                last.then_inc(S.pv_done, 1)

            def turn_v(p):
                pe.wait_ge(S.v_raw_ready, 1)
                turn(v_raw, mix_flat[1]).then_inc(S.v_turned, 1)

            def attn(*steps):
                return tuple((lambda p, f=f, c=c: f(p, c)) for f, c in steps)

            L, Tr, V = logits_of, turn_probs, values_of
            attention = ((), attn((L, 0)), (), attn((L, 1)), (), attn((Tr, 0), (L, 2)), attn((V, 0)), (),
                         attn((Tr, 1), (L, 3)), attn((V, 1)), (), attn((Tr, 2)), attn((V, 2)), (), attn((Tr, 3)),
                         attn((V, 3)))

            def step_projections(i, between):
                for j in range(4):
                    pe.wait_ge(S.lo_ready, i * 4 + (FIRST_B + 3 + j))
                    if j < 2:
                        if first(i):
                            pe.wait_ge((S.k_raw_ready, S.v_raw_ready)[j], 1)
                        else:
                            pe.wait_ge(S.q_even_ready, i * 2 + (j - 1))
                            pe.wait_ge(S.q_odd_ready, i * 2 + (j - 1))
                    else:
                        pe.wait_ge(S.gate_ready, i * 2 + (HEADS + j - 1))
                    for quarter in range(4):
                        rows = range(quarter % 2 * (KB // 2), (quarter % 2 + 1) * (KB // 2))
                        last = project(j % 2, quarter // 2, hB_hi, hB_lo, rows)
                        if quarter == 3:
                            last.then_inc(S.block_done, 1)
                        elif quarter == 1 and j == 3:
                            last.then_inc(S.last_half, 1)
                        for step in between[4 * j + quarter]:
                            step(i - 1)

            step_projections(0, ((turn_v,),) + ((),) * 15)
            with pe.Fori(1, NJ) as i:
                step_projections(i, attention)

            p = NJ - 1
            logits_of(p, 0)
            early_rows(1, 0, 0, range(2))
            logits_of(p, 1)
            early_rows(1, 0, 0, range(2, EARLY[1]))
            early_rows(1, 0, 1, range(2))
            turn_probs(p, 0)
            logits_of(p, 2)
            early_rows(1, 0, 1, range(2, EARLY[1] - 1))
            values_of(p, 0)
            early_rows(1, 0, 1, range(EARLY[1] - 1, EARLY[1]))
            turn_probs(p, 1)
            logits_of(p, 3)
            early_rows(1, 1, 0, range(EARLY[1]))
            values_of(p, 1)
            pe.wait_ge(S.mix_lo_ready, TB + 1)
            for half in range(2):
                pe.wait_ge(*low_part(1, half * 4 + 3))
                last = out_rows(1, 0, half, range(EARLY[1], KB))
            last.then_inc(S.out_tile_done, 1)
            turn_probs(p, 2)
            pe.wait_ge(S.mix_lo_ready, TB + 2)
            out_rows(1, 1, 0, range(EARLY[1], KB))
            values_of(p, 2)
            out_rows(1, 1, 1, range(KB // 2))
            turn_probs(p, 3)
            out_rows(1, 1, 1, range(KB // 2, KB)).then_inc(S.out_tile_done, 1)
            values_of(p, 3)
            with pe.Fori(1, TB // 2) as i:
                out_tile(1, i * 2, 0)
                out_tile(1, i * 2 + 1, 1)

        @block.scalar
        def _(act):
            def exp_and_log():
                nc.scalar.preload_act_table_set("natural_log_exp_and_others")

            def inverse_rms(source, junk, col, squared, logged, ready, n, loaded):
                act.wait_ge(S.cols_set, 2)
                for sem, value in loaded:
                    act.wait_ge(sem, value)
                nc.scalar.activation(junk, source, ACT.Square, accum_out=ssq[:, col:col + 1]).then_inc(squared, 1)
                act.wait_ge(squared, n)
                nc.scalar.activation(rms[:, col:col + 1], ssq[:, col:col + 1], ACT.Ln, scale=1.0 / D,
                                     bias=eps_col[:]).then_inc(logged, 1)
                act.wait_ge(logged, n)
                nc.scalar.activation(rms[:, col:col + 1], rms[:, col:col + 1], ACT.Exp, scale=-0.5)\
                    .then_inc(ready, 1)

            def split_block(n, slot, free):
                act.wait_ge(raw_loaded[slot], (n - slot) * 8 + 16)
                if free is not None:
                    act.wait_ge(*free)
                nc.scalar.copy(split_hi[:, slot], w_raw[:, slot]).then_inc(S.hi_ready, 1)

            def split_out_weights(layer, m, raw, w_hi):
                act.wait_ge(out_w_loaded[m], 16 * layer + 16)
                nc.scalar.copy(out_part(w_hi, m), out_part(raw, m)).then_inc(S.out_w_hi, 1)

            def norm_in(t):
                loaded = [(x_in_loaded[t], 16)]
                if t >= 2:
                    loaded.append((S.in_turned, t - 1))
                inverse_rms(x_in[:, t % X_SLOTS], x_scaled[:, t % 2], t % 2, S.in_squared, S.in_logged,
                            S.in_rms_ready, t + 1, loaded)

            def high_in(t):
                act.wait_ge(S.in_turned, t + 1)
                nc.scalar.copy(hA_hi[:, :, ds(t * P, P)], mix_flat[t % 2].rearrange("p (k n) -> p k n", k=KB))\
                    .then_inc(S.in_hi_ready, 1)

            exp_and_log()
            for t in range(TB):
                norm_in(t)
                if t in (1, 3):
                    split_block(t // 2, t // 2, None)
                if t:
                    high_in(t - 1)
            high_in(TB - 1)

            act.wait_ge(S.bound_shifted, 1)
            nc.scalar.activation(lb_tmp[:], lb_tmp[:], ACT.Exp).then_inc(S.bound_exped, 1)
            act.wait_ge(S.bound_ready, 1)
            act.wait_ge(S.cols_set, 2)
            nc.scalar.activation(log1mlb_col[:], lb_col[:], ACT.Ln, scale=-1.0, bias=one_col[:])\
                .then_inc(S.bound_logged, 1)

            def value_buffer(p):
                act.wait_ge(S.block_done, p * A_BLOCKS + A_BLOCKS)
                nc.scalar.copy(val[:], flat(proj_ps[1])).then_inc(S.val_ready, 1)

            def values_by_token(p):
                act.wait_ge(S.val_turned, p + 1)
                nc.scalar.copy(val[:], mix_flat[0]).then_inc(S.val_tok_ready, 1)

            def keys_by_token(p):
                act.wait_ge(S.k_dec_turned, p + 1)
                nc.scalar.copy(k_dec[:], mix_flat[1]).then_inc(S.k_dec_tok_ready, 1)

            def forget_gate(h):
                act.wait_ge(S.block_done, h * A_BLOCKS + 1)
                if not first(h):
                    act.wait_ge(S.q1_ready, h)
                nc.scalar.activation(tmp1[:], flat(proj_ps[0]), ACT.Abs).then_inc(S.f_abs, 1)
                act.wait_ge(S.f_abs, h + 1)
                nc.scalar.activation(tmp1[:], tmp1[:], ACT.Exp, scale=-1.0).then_inc(S.f_exp, 1)
                act.wait_ge(S.f_exp, h + 1)
                nc.scalar.activation(tmp1[:], tmp1[:], ACT.Ln, bias=one_col[:]).then_inc(S.f_log, 1)
                act.wait_ge(S.f_neg_ready, h + 1)
                nc.scalar.activation(tmp3[:], tmp3[:], ACT.Exp).then_inc(S.f_neg_exp, 1)
                act.wait_ge(S.f_neg_exp, h + 1)
                nc.scalar.activation(tmp3[:], tmp3[:], ACT.Ln, scale=lb_col[:, ds(h, 1)], bias=one_col[:])\
                    .then_inc(S.f_neg_log, 1)
                act.wait_ge(S.log_nf_ready, h + 1)
                if not first(h):
                    act.wait_ge(S.k_dec_ready, h)
                nc.scalar.activation(k_gate[:], tmp2[:], ACT.Exp, bias=log1mlb_col[:, ds(h, 1)])\
                    .then_inc(S.k_gate_ready, 1)

            def silu_query(h):
                act.wait_ge(S.block_done, h * A_BLOCKS + 2)
                if not first(h):
                    act.wait_ge(S.q_dec_ready, h)
                nc.scalar.activation(silu_q[:], flat(proj_ps[1]), ACT.Silu).then_inc(S.silu_q_ready, 1)

            def silu_gate(h):
                act.wait_ge(S.block_done, h * A_BLOCKS + 3)
                nc.scalar.activation(mixed[:, ds(h, 1), :].rearrange("p a n -> p (a n)"), flat(proj_ps[0]),
                                     ACT.Silu).then_inc(S.gate_ready, 1)

            def decays_near(h):
                act.wait_ge(S.d3_ready, h + 1)
                act.wait_ge(S.k_gate_ready, h + 1)
                nc.scalar.activation(tmp2[:], tmp1[:], ACT.Exp).then_inc(S.e3q_ready, 1)
                nc.scalar.activation(tmp1[:], tmp1[:], ACT.Exp, scale=-1.0).then_inc(S.e3k_ready, 1)
                act.wait_ge(S.d21_ready, h + 1)
                nc.scalar.activation(tmp3[:], tmp3[:], ACT.Exp).then_inc(S.e21_ready, 1)

            def decays_far(h):
                act.wait_ge(S.b_ready, h + 1)
                if not first(h):
                    act.wait_ge(S.k_dec_ready, h)
                nc.scalar.activation(chunk_decay[:], halves(b_cum)[:, :, :, CHUNK - 1], ACT.Exp)\
                    .then_inc(S.decay_ready, 1)
                act.wait_ge(S.q3_ready, h + 1)
                nc.scalar.activation(tmp2[:], b_cum[:], ACT.Exp).then_inc(S.eb_ready, 1)
                act.wait_ge(S.dq1_ready, h + 1)
                nc.scalar.activation(tmp1[:, 0:HALF], tmp1[:, 0:HALF], ACT.Exp).then_inc(S.eq1_ready, 1)
                act.wait_ge(S.dkd_ready, h + 1)
                nc.scalar.activation(tmp3[:], tmp3[:], ACT.Exp).then_inc(S.ekd_ready, 1)

            def keep_level0(p):
                act.wait_ge(S.level1_kept, p + 1)
                act.wait_ge(S.level0_done, p + 1)
                nc.scalar.copy(scores[0:CHUNK, :, CHUNK:P],
                               mix_ps[0][0:CHUNK, 0, :].rearrange("p (r c) -> p r c", c=CHUNK))\
                    .then_inc(S.level0_kept, 1)

            def square_output(p):
                act.wait_ge(S.o_done, p + 1)
                nc.scalar.activation(rstd[:], mix_flat[1], ACT.Square).then_inc(S.o_squared, 1)
                act.wait_ge(S.o_squared, p + 1)
                nc.scalar.copy(square_hi[:], rstd[:]).then_inc(S.square_hi_ready, 1)

            def inverse_head_rms(p):
                act.wait_ge(S.mean_done, p + 1)
                nc.scalar.activation(rstd[:], mix_flat[0], ACT.Ln, bias=eps_col[:]).then_inc(S.mean_logged, 1)
                act.wait_ge(S.mean_logged, p + 1)
                nc.scalar.activation(rstd[:], rstd[:], ACT.Exp, scale=-0.5).then_inc(S.rstd_ready, 1)

            def split_early(layer, t, free):
                for sem, value in free:
                    act.wait_ge(sem, value)
                rows = slice(0, EARLY[layer])
                nc.scalar.copy(split_hi[:, t, rows], mixed_tile(t)[:, rows]).then_inc(S.early_hi_ready, 1)

            def head(h, previous, following):
                def next_block(j):
                    n = h * A_BLOCKS + j
                    split_block(n, j % 2, (S.block_done, n - 1) if not (first(h) and j < 2) else None)

                if previous:
                    next_block(1)
                    value_buffer(h - 1)
                    values_by_token(h - 1)
                    keys_by_token(h - 1)
                next_block(2)
                forget_gate(h)
                next_block(3)
                if previous:
                    keep_level0(h - 1)
                silu_query(h)
                exp_and_log()
                if previous:
                    square_output(h - 1)
                decays_near(h)
                if previous:
                    inverse_head_rms(h - 1)
                if following:
                    next_block(4)
                silu_gate(h)
                exp_and_log()
                decays_far(h)

            head(0, False, True)
            with act.Fori(1, HEADS - 1) as h:
                head(h, True, True)
            head(HEADS - 1, True, False)
            last = HEADS - 1

            def weights_a(*ms):
                for m in ms:
                    split_out_weights(0, m, woA_raw, woA_hi)

            def split_late(layer, t, done):
                act.wait_ge(*done)
                rows = slice(EARLY[layer], KB)
                nc.scalar.copy(split_hi[:, t, rows], mixed_tile(t)[:, rows]).then_inc(S.mix_hi_ready, 1)

            split_early(0, 0, ((S.mixed_ready, HEADS - 1), (S.block_done, BLK_B - 1)))
            weights_a(0)
            value_buffer(last)
            weights_a(1)
            values_by_token(last)
            keys_by_token(last)
            weights_a(2, 3, 4)
            split_early(0, 1, ((S.block_done, BLK_B),))
            weights_a(5, 6)
            keep_level0(last)
            weights_a(7)
            square_output(last)
            inverse_head_rms(last)

            def split_mixed(layer, t, slot, free):
                for sem, value in free:
                    act.wait_ge(sem, value)
                nc.scalar.copy(split_hi[:, slot], mixed_tile(t)).then_inc(S.mix_hi_ready, 1)

            def norm_y(layer, t, slot, buffer):
                loaded = [(S.out_tile_done, t + (TB * layer + 1))]
                if not (isinstance(t, int) and t < 2):
                    loaded.append((S.h_turned, t - 1) if layer == 0 else (S.x1_ready, t + (TB - 1)))
                inverse_rms(flat(proj_ps[slot]), buffer[:, slot], slot, S.y_squared, S.y_logged, S.y_rms,
                            t + (TB * layer + 1), loaded)

            def high_h(t, slot):
                act.wait_ge(S.h_turned, t + 1)
                nc.scalar.copy(hB_hi[:, :, ds(t * P, P)], mix_flat[slot].rearrange("p (k n) -> p k n", k=KB))\
                    .then_inc(S.h_hi_ready, 1)

            def norm_x1(t, slot):
                inverse_rms(mixed_tile(t), y_norm[:, slot].rearrange("p (k n) -> p k n", k=KB), 2 + slot,
                            S.x1_squared, S.x1_logged, S.x1_rms, t + 1, [(S.x1_ready, t + 1)])

            split_late(0, 0, (S.mixed_ready, HEADS))
            split_late(0, 1, (S.mixed_ready, HEADS))
            split_mixed(0, 2, 0, ((S.out_tile_done, 1),))
            norm_y(0, 0, 0, y_norm)
            norm_x1(0, 0)
            norm_y(0, 1, 1, y_norm)
            norm_x1(1, 1)
            with act.Fori(1, TB // 2 - 1) as i:
                for slot in range(2):
                    t = i * 2 + slot
                    split_mixed(0, t + 1, 1 - slot, ((S.out_tile_done, t),))
                    norm_y(0, t, slot, y_norm)
                    high_h(t - 2, slot)
                    norm_x1(t, slot)
            split_mixed(0, TB - 1, 1, ((S.out_tile_done, TB - 2),))
            norm_y(0, TB - 2, 0, y_norm)
            high_h(TB - 4, 0)
            norm_x1(TB - 2, 0)
            split_block(FIRST_B, 0, (S.out_tile_done, TB - 1))
            norm_y(0, TB - 1, 1, y_norm)
            split_block(FIRST_B + 1, 1, (S.out_tile_done, TB))
            high_h(TB - 3, 1)
            norm_x1(TB - 1, 1)
            high_h(TB - 2, 0)
            high_h(TB - 1, 1)

            split_block(FIRST_B + 2, 0, (S.block_done, BLK_B + 1))
            nc.scalar.copy(k_raw[:], flat(proj_ps[0])).then_inc(S.k_raw_ready, 1)
            split_block(FIRST_B + 3, 1, (S.block_done, BLK_B + 2))
            nc.scalar.copy(v_raw[:], flat(proj_ps[1])).then_inc(S.v_raw_ready, 1)

            def next_blk(i, j):
                split_block(i * 4 + (FIRST_B + 2 + j), j % 2, (S.block_done, i * 4 + (BLK_B + j + 1)))

            def gate(i, blk):
                act.wait_ge(S.block_done, i * 4 + (BLK_B + 3 + blk))
                if first(i) and blk == 0:
                    act.wait_ge(S.resid_stored, 16 * TB)
                nc.scalar.activation(mixed[:, ds(i * 2 + blk, 1), :].rearrange("p a n -> p (a n)"),
                                     flat(proj_ps[blk]), ACT.Silu).then_inc(S.gate_ready, 1)

            def even_queries(i, blk):
                act.wait_ge(S.zeroB_set, 4)
                act.wait_ge(S.block_done, i * 4 + (BLK_B + 5 + blk))
                if blk == 0 and not first(i):
                    act.wait_ge(S.logits_done, i * 4)
                nc.scalar.activation(q_even[0:DH, :, blk, :], by_chunk(proj_ps[blk])[0:DH], ACT.Copy, scale=DH ** -0.5)\
                    .then_inc(S.q_even_ready, 1)

            def exp_logits(p, c):
                act.wait_ge(S.sink_shifted, p * 4 + (c + 1))
                buf = c % 2
                nc.scalar.activation(sink_exp[:, buf], sink_exp[:, buf], ACT.Exp)
                for n in range(4):
                    for e in range(2):
                        row = n * 2 + e
                        last = nc.scalar.activation(logits[:, buf, n, e, :], logits[:, buf, n, e, :], ACT.Exp,
                                                    bias=neg_max[:, buf, row:row + 1],
                                                    accum_out=row_sum[:, buf, row:row + 1])
                last.then_inc(S.exped, 1)

            def probs_by_key(p, c):
                act.wait_ge(S.probs_turned, p * 4 + (c + 1))
                nc.scalar.copy(probs_t[:].rearrange("p n e k -> p (n e k)"), mix_flat[1])\
                    .then_inc(S.probs_t_ready, 1)

            X, C = exp_logits, probs_by_key

            def step(i, previous, following):
                def attend(*steps):
                    for f, c in steps if previous else ():
                        f(i - 1, c)

                if previous:
                    next_blk(i, 1)
                    even_queries(i - 1, 1)
                attend((X, 0))
                next_blk(i, 2)
                attend((X, 1))
                gate(i, 0)
                exp_and_log()
                attend((C, 0), (X, 2))
                next_blk(i, 3)
                gate(i, 1)
                exp_and_log()
                attend((C, 1), (X, 3), (C, 2))
                if following:
                    next_blk(i, 4)
                even_queries(i, 0)
                attend((C, 3))

            def values_by_token_b():
                act.wait_ge(S.v_turned, 1)
                nc.scalar.copy(v_tok[:].rearrange("p t d -> p (t d)"), mix_flat[1]).then_inc(S.v_tok_ready, 1)

            values_by_token_b()
            step(0, False, True)
            with act.Fori(1, NJ - 1) as i:
                step(i, True, True)
            step(NJ - 1, True, False)
            last = NJ - 1

            def weights_b(*ms):
                for m in ms:
                    split_out_weights(1, m, woB_raw, woB_hi)

            weights_b(0, 1)
            even_queries(last, 1)
            split_early(1, 0, ((S.o_ready, 4 * (NJ - 1)), (S.block_done, BLK_END - 1)))
            weights_b(2, 3, 4, 5, 6)
            exp_logits(last, 0)
            exp_logits(last, 1)
            probs_by_key(last, 0)
            weights_b(7)
            split_early(1, 1, ((S.block_done, BLK_END),))
            exp_logits(last, 2)

            split_late(1, 0, (S.o_ready, 4 * NJ - 3))
            split_late(1, 1, (S.o_ready, 4 * NJ - 3))
            probs_by_key(last, 1)
            exp_logits(last, 3)
            probs_by_key(last, 2)
            norm_y(1, 0, 0, y_last)
            split_mixed(1, 2, 0, ((S.out_tile_done, TB + 1), (S.o_ready, 4 * NJ - 2)))
            probs_by_key(last, 3)
            norm_y(1, 1, 1, y_last)
            split_mixed(1, 3, 1, ((S.out_tile_done, TB + 2),))
            norm_y(1, 2, 0, y_last)
            act.wait_ge(S.o_ready, 4 * NJ)
            with act.Fori(2, TB // 2) as i:
                split_mixed(1, i * 2, 0, ((S.out_tile_done, i * 2 + (TB - 1)),))
                norm_y(1, i * 2 - 1, 1, y_last)
                split_mixed(1, i * 2 + 1, 1, ((S.out_tile_done, i * 2 + TB),))
                norm_y(1, i * 2, 0, y_last)
            norm_y(1, TB - 1, 1, y_last)

        @block.vector
        def _(dve):
            v = nc.vector

            def split_block(n, slot):
                dve.wait_ge(S.hi_ready, n + 1)
                v.tensor_tensor(split_lo[:, slot], w_raw[:, slot], split_hi[:, slot].bitcast(F32), ALU.subtract)\
                    .then_inc(S.lo_ready, 1)

            def split_out_weights(layer, m, raw, w_hi, w_lo):
                dve.wait_ge(S.out_w_hi, KB * layer + m + 1)
                v.tensor_tensor(out_part(w_lo, m), out_part(raw, m), out_part(w_hi, m).bitcast(F32), ALU.subtract)\
                    .then_inc(S.out_w_odd_lo, 1)

            v.memset(eps_col[:], EPS).then_inc(S.cols_set, 1)
            v.memset(one_col[:], 1.0).then_inc(S.cols_set, 1)
            v.memset(scan_keep[:], 1.0).then_inc(S.keep_ones, 1)
            dve.wait_ge(S.keep_ones, 1)
            v.memset(chunks(scan_keep)[:, :, 0:1], 0.0).then_inc(S.keep_set, 1)

            dve.wait_ge(S.gain_in_loaded, 16)

            def scale_in(t):
                slot = t % 2
                dve.wait_ge(S.in_rms_ready, t + 1)
                v.scalar_tensor_tensor(x_scaled[:, slot], x_in[:, t % X_SLOTS], rms[:, slot:slot + 1], gain_in[:],
                                       ALU.mult, ALU.mult).then_inc(S.in_scaled, 1)

            def low_in(t):
                dve.wait_ge(S.in_hi_ready, t + 1)
                cols = slice(t * P, (t + 1) * P)
                v.tensor_tensor(hA_lo[:, :, cols], mix_flat[t % 2].rearrange("p (k n) -> p k n", k=KB),
                                hA_hi[:, :, cols].bitcast(F32), ALU.subtract).then_inc(S.in_lo_ready, 1)

            for t in range(TB):
                scale_in(t)
                if t in (1, 3):
                    split_block(t // 2, t // 2)
                if t:
                    low_in(t - 1)
            low_in(TB - 1)
            dve.wait_ge(S.const_loaded, 16 * 5)
            v.tensor_tensor(lb_tmp[:], lb_tmp[:], lb_tmp[:], ALU.subtract).then_inc(S.bound_shifted, 1)
            dve.wait_ge(S.bound_exped, 1)
            v.reciprocal(lb_col[:], lb_tmp[:]).then_inc(S.bound_inverse, 1)
            dve.wait_ge(S.bound_inverse, 1)
            v.tensor_tensor(lb_tmp[:], lb_tmp[:], lb_col[:], ALU.mult).then_inc(S.bound_prob, 1)
            dve.wait_ge(S.bound_prob, 1)
            v.tensor_tensor(lb_col[:], lb_tmp[:], lb_tmp[:], ALU.subtract).then_inc(S.bound_prob, 1)
            dve.wait_ge(S.bound_prob, 2)
            v.tensor_scalar(lb_col[:], lb_col[:], 0.0, None, ALU.max).then_inc(S.bound_ready, 1)
            v.tensor_scalar(sink[:], sink[:], -1.0, None, ALU.mult).then_inc(S.sinks_negated, 1)

            dve.wait_ge(S.zeros_set, 2)

            def keep(n, done, kept, p):
                dve.wait_ge(S.zeros_set, 2)
                if n:
                    dve.wait_ge(S.level3_kept, p + 1)
                dve.wait_ge(done, p + 1)
                mask = masks[:, n:n + 1, :].broadcast_to([P, NPAIR, P])
                v.copy_predicated(scores[:], mask, mix_flat[0].rearrange("p (r c) -> p r c", c=P)).then_inc(kept, 1)

            def keep_level1(p):
                dve.wait_ge(S.level2_kept, p + 1)
                dve.wait_ge(S.level1_done, p + 1)
                for row in (0, CHUNK):
                    last = v.tensor_copy(scores[row:row + HC, :, row + HC:row + CHUNK],
                                         mix_flat[1][row:row + HC, 0:NPAIR * HC].rearrange("p (r c) -> p r c", c=HC))
                last.then_inc(S.level1_kept, 1)

            def states(p):
                dve.wait_ge(S.update_done, p + 1)
                for r in range(NPAIR - 1):
                    update = mix_flat[1][:, r * P:(r + 1) * P]
                    if r == 0:
                        v.tensor_copy(state[:, 0, :], update).then_inc(S.state_step, 1)
                    else:
                        dve.wait_ge(S.state_step, p * (NPAIR - 1) + r)
                        v.scalar_tensor_tensor(state[:, r, :], state[:, r - 1, :], pair_decay[:, r:r + 1], update,
                                               ALU.mult, ALU.add).then_inc(S.state_step, 1)

            def forget_gate(h):
                f = flat(proj_ps[0])
                dve.wait_ge(S.block_done, h * A_BLOCKS + 1)
                dve.wait_ge(S.f_abs, h + 1)
                v.tensor_scalar(tmp3[:], f, -1.0, 40.0, ALU.mult, ALU.min).then_inc(S.f_neg_ready, 1)
                dve.wait_ge(S.f_log, h + 1)
                v.scalar_tensor_tensor(b_cum[:], f, 0.0, tmp1[:], ALU.min, ALU.subtract)\
                    .then_inc(S.log_f_ready, 1)
                dve.wait_ge(S.log_f_ready, h + 1)
                v.tensor_tensor(tmp2[:], b_cum[:], f, ALU.subtract).then_inc(S.log_nf_ready, 1)

            def cumulate(h):
                dve.wait_ge(S.f_neg_log, h + 1)
                v.tensor_tensor(b_cum[:], b_cum[:], tmp3[:], ALU.add).then_inc(S.log_f_full, 1)
                dve.wait_ge(S.log_f_full, h + 1)
                v.tensor_tensor_scan(b_cum[:], scan_keep[:], b_cum[:], 0.0, ALU.mult, ALU.add)\
                    .then_inc(S.b_ready, 1)

            b_subs, b_chunks, b_halves = subs(b_cum), chunks(b_cum), halves(b_cum)
            b_quads = b_cum[:].rearrange("p (n s c) -> p n s c", s=2, c=SUB)

            def distances(h):
                dve.wait_ge(S.b_ready, h + 1)
                v.tensor_tensor(subs(tmp1), b_subs, b_subs[:, :, 0:1].broadcast_to([P, T // SUB, SUB]),
                                ALU.subtract).then_inc(S.d3_ready, 1)
                v.tensor_tensor(tmp3[:, 0:HALF].rearrange("p (n c) -> p n c", c=SUB),
                                b_quads[:, :, 1, 0:1].broadcast_to([P, T // SUB // 2, SUB]), b_quads[:, :, 0, :],
                                ALU.subtract)
                v.tensor_tensor(tmp3[:, HALF:T].rearrange("p (n c) -> p n c", c=HC),
                                b_chunks[:, :, HC:HC + 1].broadcast_to([P, NCH, HC]), b_chunks[:, :, 0:HC],
                                ALU.subtract).then_inc(S.d21_ready, 1)

            def near_operands(h):
                dve.wait_ge(S.silu_q_ready, h + 1)
                dve.wait_ge(S.e3q_ready, h + 1)
                if not first(h):
                    dve.wait_ge(S.level2_done, h)
                v.tensor_tensor(flat(q3[:]), silu_q[:], tmp2[:], ALU.mult).then_inc(S.q3_ready, 1)
                dve.wait_ge(S.e3k_ready, h + 1)
                v.tensor_tensor(flat(k3[:]), k_gate[:], tmp1[:], ALU.mult).then_inc(S.k3_ready, 1)
                dve.wait_ge(S.k3_ready, h + 1)
                v.tensor_tensor(tmp1[:, 0:HALF].rearrange("p (n c) -> p n c", c=HC), b_chunks[:, :, HC:CHUNK],
                                b_chunks[:, :, HC:HC + 1].broadcast_to([P, NCH, HC]), ALU.subtract)\
                    .then_inc(S.dq1_ready, 1)
                dve.wait_ge(S.e21_ready, h + 1)
                even = "p (n s c) -> p n s c"
                v.tensor_tensor(flat(k2[:]).rearrange(even, s=2, c=SUB)[:, :, 0, :],
                                k_gate[:].rearrange(even, s=2, c=SUB)[:, :, 0, :],
                                tmp3[:, 0:HALF].rearrange("p (n c) -> p n c", c=SUB), ALU.mult)\
                    .then_inc(S.k2_ready, 1)
                if not first(h):
                    dve.wait_ge(S.level1_done, h)
                v.tensor_tensor(k1[:], chunks(k_gate)[:, :, 0:HC],
                                tmp3[:, HALF:T].rearrange("p (n c) -> p n c", c=HC), ALU.mult)\
                    .then_inc(S.k1_ready, 1)
                dve.wait_ge(S.k1_ready, h + 1)
                v.tensor_tensor(chunks(tmp3), b_chunks[:, :, CHUNK - 1:CHUNK].broadcast_to([P, NCH, CHUNK]), b_chunks,
                                ALU.subtract).then_inc(S.dkd_ready, 1)

            def far_operands(h):
                dve.wait_ge(S.eq1_ready, h + 1)
                v.tensor_tensor(q1[:], chunks(silu_q)[:, :, HC:CHUNK],
                                tmp1[:, 0:HALF].rearrange("p (n c) -> p n c", c=HC), ALU.mult)\
                    .then_inc(S.q1_ready, 1)
                dve.wait_ge(S.decay_ready, h + 1)
                v.tensor_tensor(pair_decay[:], chunk_decay[:, :, 0], chunk_decay[:, :, 1], ALU.mult)\
                    .then_inc(S.pair_decay_ready, 1)
                dve.wait_ge(S.eb_ready, h + 1)
                if not first(h):
                    dve.wait_ge(S.level0_done, h)
                sq, eb, kg, ekd = halves(silu_q), halves(tmp2), halves(k_gate), halves(tmp3)
                v.tensor_tensor(q_dec_b[:], sq[:, :, 1, :], eb[:, :, 1, :], ALU.mult).then_inc(S.q_dec_b_ready, 1)
                dve.wait_ge(S.ekd_ready, h + 1)
                v.tensor_tensor(k_dec_a[:], kg[:, :, 0, :], ekd[:, :, 0, :], ALU.mult).then_inc(S.k_dec_a_ready, 1)
                if not first(h):
                    dve.wait_ge(S.mean_done, h)
                v.tensor_tensor(halves(q_dec)[:, :, 0, :], sq[:, :, 0, :], eb[:, :, 0, :], ALU.mult)
                dve.wait_ge(S.q_dec_b_ready, h + 1)
                v.tensor_tensor(halves(q_dec)[:, :, 1, :], q_dec_b[:],
                                chunk_decay[:, :, 0:1].broadcast_to([P, NPAIR, CHUNK]), ALU.mult)\
                    .then_inc(S.q_dec_ready, 1)
                v.tensor_tensor(halves(k_dec)[:, :, 1, :], kg[:, :, 1, :], ekd[:, :, 1, :], ALU.mult)
                dve.wait_ge(S.k_dec_a_ready, h + 1)
                v.tensor_tensor(halves(k_dec)[:, :, 0, :], k_dec_a[:],
                                chunk_decay[:, :, 1:2].broadcast_to([P, NPAIR, CHUNK]), ALU.mult)\
                    .then_inc(S.k_dec_ready, 1)

            def square_low(p):
                dve.wait_ge(S.square_hi_ready, p + 1)
                v.tensor_tensor(square_lo[:], rstd[:], square_hi[:].bitcast(F32), ALU.subtract)\
                    .then_inc(S.square_lo_ready, 1)

            def norm_and_gate(p):
                dve.wait_ge(S.rstd_ready, p + 1)
                v.tensor_tensor(rstd[:], mix_flat[1], rstd[:], ALU.mult).then_inc(S.o_scaled, 1)
                dve.wait_ge(S.o_scaled, p + 1)
                dve.wait_ge(S.gate_ready, p + 1)
                row = mixed[:, ds(p, 1), :].rearrange("p a n -> p (a n)")
                v.scalar_tensor_tensor(row, rstd[:], gn_col[:, ds(p, 1)], row, ALU.mult, ALU.mult)\
                    .then_inc(S.mixed_ready, 1)

            def split_early(layer, t):
                dve.wait_ge(S.early_hi_ready, 2 * layer + t + 1)
                rows = slice(0, EARLY[layer])
                v.tensor_tensor(split_lo[:, t, rows], mixed_tile(t)[:, rows], split_hi[:, t, rows].bitcast(F32),
                                ALU.subtract).then_inc(S.early_lo_ready, 1)

            def head(h, previous, following):
                n = h * A_BLOCKS
                if previous:
                    split_block(n + 1, 1)
                    keep(0, S.level3_done, S.level3_kept, h - 1)
                    states(h - 1)
                split_block(n + 2, 0)
                forget_gate(h)
                if previous:
                    keep(1, S.level2_done, S.level2_kept, h - 1)
                    keep_level1(h - 1)
                cumulate(h)
                split_block(n + 3, 1)
                distances(h)
                if previous:
                    square_low(h - 1)
                near_operands(h)
                if previous:
                    norm_and_gate(h - 1)
                if following:
                    split_block(n + 4, 0)
                far_operands(h)

            head(0, False, True)
            with dve.Fori(1, HEADS - 1) as h:
                head(h, True, True)
            head(HEADS - 1, True, False)
            last = HEADS - 1

            def split_late(layer, t):
                dve.wait_ge(S.mix_hi_ready, TB * layer + t + 1)
                rows = slice(EARLY[layer], KB)
                v.tensor_tensor(split_lo[:, t, rows], mixed_tile(t)[:, rows], split_hi[:, t, rows].bitcast(F32),
                                ALU.subtract).then_inc(S.mix_lo_ready, 1)

            def weights_a(m):
                split_out_weights(0, m, woA_raw, woA_hi, woA_lo)

            split_early(0, 0)
            weights_a(1)
            keep(0, S.level3_done, S.level3_kept, last)
            states(last)
            weights_a(3)
            keep(1, S.level2_done, S.level2_kept, last)
            weights_a(5)
            keep_level1(last)
            split_early(0, 1)
            weights_a(7)
            square_low(last)
            norm_and_gate(last)

            def split_mixed(layer, t, slot):
                dve.wait_ge(S.mix_hi_ready, t + (TB * layer + 1))
                v.tensor_tensor(split_lo[:, slot], mixed_tile(t), split_hi[:, slot].bitcast(F32), ALU.subtract)\
                    .then_inc(S.mix_lo_ready, 1)

            def add_y(layer, t, slot, buffer, gain):
                n = t + (TB * layer + 1)
                dve.wait_ge(S.y_rms, n)
                v.scalar_tensor_tensor(buffer[:, slot], flat(proj_ps[slot]), rms[:, slot:slot + 1], gain[:],
                                       ALU.mult, ALU.mult).then_inc(S.y_scaled, 1)
                dve.wait_ge(S.y_scaled, n)
                dve.wait_ge(resid_loaded[slot], (t - slot) * 8 + (64 * layer + 16))
                scaled = buffer[:, slot].rearrange("p (k n) -> p k n", k=KB)
                parts = 2 if isinstance(t, int) and t + TB * layer == 2 * TB - 1 else 1
                for part in range(parts):
                    k = slice(part * KB // parts, (part + 1) * KB // parts)
                    v.tensor_tensor(mixed_tile(t)[:, k], scaled[:, k], mixed_tile(t)[:, k], ALU.add)\
                        .then_inc(S.x1_ready, 1)

            def low_h(t, slot):
                dve.wait_ge(S.h_hi_ready, t + 1)
                cols = ds(t * P, P)
                v.tensor_tensor(hB_lo[:, :, cols], mix_flat[slot].rearrange("p (k n) -> p k n", k=KB),
                                hB_hi[:, :, cols].bitcast(F32), ALU.subtract).then_inc(S.h_lo_ready, 1)

            def scale_h(t, slot):
                dve.wait_ge(S.x1_rms, t + 1)
                v.scalar_tensor_tensor(y_norm[:, slot].rearrange("p (k n) -> p k n", k=KB), mixed_tile(t),
                                       rms[:, 2 + slot:3 + slot], gain_pre[:].rearrange("p (k n) -> p k n", k=KB),
                                       ALU.mult, ALU.mult).then_inc(S.h_scaled, 1)

            split_late(0, 0)
            split_late(0, 1)
            dve.wait_ge(S.gains_loaded, 32)
            split_mixed(0, 2, 0)
            add_y(0, 0, 0, y_norm, gain_post)
            scale_h(0, 0)
            add_y(0, 1, 1, y_norm, gain_post)
            scale_h(1, 1)
            with dve.Fori(1, TB // 2 - 1) as i:
                for slot in range(2):
                    t = i * 2 + slot
                    split_mixed(0, t + 1, 1 - slot)
                    add_y(0, t, slot, y_norm, gain_post)
                    low_h(t - 2, slot)
                    scale_h(t, slot)
            split_mixed(0, TB - 1, 1)
            add_y(0, TB - 2, 0, y_norm, gain_post)
            low_h(TB - 4, 0)
            scale_h(TB - 2, 0)
            split_block(FIRST_B, 0)
            add_y(0, TB - 1, 1, y_norm, gain_post)
            split_block(FIRST_B + 1, 1)
            low_h(TB - 3, 1)
            scale_h(TB - 1, 1)
            low_h(TB - 2, 0)
            low_h(TB - 1, 1)

            split_block(FIRST_B + 2, 0)
            split_block(FIRST_B + 3, 1)
            dve.wait_ge(S.bias_loaded, 16)
            dve.wait_ge(S.sinks_negated, 1)

            def odd_queries(i, blk):
                dve.wait_ge(S.zeroB_set, 4)
                dve.wait_ge(S.block_done, i * 4 + (BLK_B + 5 + blk))
                if blk == 0 and not first(i):
                    dve.wait_ge(S.logits_done, i * 4)
                v.tensor_scalar(q_odd[DH:P, :, blk, :], by_chunk(proj_ps[blk])[DH:P], DH ** -0.5, None, ALU.mult)\
                    .then_inc(S.q_odd_ready, 1)

            def shift(p, c):
                n, buf = p * 4 + (c + 1), c % 2
                dve.wait_ge(S.logits_done, n)
                lg = logits[:, buf].rearrange("p (r n) e k -> p r (n e k)", r=2)
                table = bias[:, ds(p, 1), :].broadcast_to([P, 2, 4 * P])
                v.tensor_tensor(lg, mix_flat[0].rearrange("p (r m) -> p r m", r=2), table, ALU.add)\
                    .then_inc(S.biased, 1)
                dve.wait_ge(S.biased, n)
                if c == 0:
                    v.memset(logits[:, buf, 0, :, CHUNK:P], MASKED).then_inc(S.edge_masked, 1)
                    dve.wait_ge(S.edge_masked, p + 1)
                by_row = logits[:, buf].rearrange("p n e k -> p (n e) k")
                v.tensor_reduce(neg_max[:, buf], by_row, AX_X, ALU.max).then_inc(S.max_part, 1)
                dve.wait_ge(S.max_part, n)
                rows = neg_max[:, buf].rearrange("p (n e) -> p n e", e=2)
                neg_sinks = sink[:, ds(p, 1), :].broadcast_to([P, 4, 2])
                v.scalar_tensor_tensor(rows, rows, -1.0, neg_sinks, ALU.mult, ALU.min).then_inc(S.max_ready, 1)
                dve.wait_ge(S.max_ready, n)
                v.tensor_tensor(sink_exp[:, buf].rearrange("p (n e) -> p n e", e=2), rows, neg_sinks, ALU.subtract)\
                    .then_inc(S.sink_shifted, 1)

            def normalise(p, c):
                n, buf = p * 4 + (c + 1), c % 2
                by_row = logits[:, buf].rearrange("p n e k -> p (n e) k")
                dve.wait_ge(S.exped, n)
                v.tensor_tensor(row_sum[:, buf], row_sum[:, buf], sink_exp[:, buf], ALU.add).then_inc(S.sum_ready, 1)
                dve.wait_ge(S.sum_ready, n)
                v.reciprocal(row_sum[:, buf], row_sum[:, buf]).then_inc(S.inverse_ready, 1)
                dve.wait_ge(S.inverse_ready, n)
                v.tensor_tensor(by_row, by_row, row_sum[:, buf].unsqueeze(2).broadcast_to([P, 8, P]), ALU.mult)\
                    .then_inc(S.probs_ready, 1)

            def gate_output(p, c):
                dve.wait_ge(S.pv_done, p * 4 + (c + 1))
                dve.wait_ge(S.gate_ready, p * 2 + (HEADS + 2))
                for blk in range(2):
                    dst = mixed[:, ds(p * 2 + blk, 1), 4 * CHUNK * c:4 * CHUNK * (c + 1)]\
                        .rearrange("p a (n q) -> p (a n) q", q=CHUNK)
                    src = mix_ps[1][:, 0, :].rearrange("p (n b q) -> p n b q", b=2, q=CHUNK)[:, :, blk, :]
                    last = v.tensor_tensor(dst, src, dst, ALU.mult)
                last.then_inc(S.o_ready, 1)

            M, N, G = shift, normalise, gate_output

            def step(i, previous, following):
                def attend(*steps):
                    for f, c in steps if previous else ():
                        f(i - 1, c)

                n = i * 4 + (FIRST_B + 2)
                if previous:
                    split_block(n + 1, 1)
                    odd_queries(i - 1, 1)
                attend((M, 0), (M, 1), (N, 0))
                split_block(n + 2, 0)
                attend((M, 2), (N, 1), (G, 0))
                split_block(n + 3, 1)
                attend((M, 3), (G, 1), (N, 2), (N, 3), (G, 2))
                if following:
                    split_block(n + 4, 0)
                odd_queries(i, 0)
                if following:
                    attend((G, 3))

            step(0, False, True)
            with dve.Fori(1, NJ - 1) as i:
                step(i, True, True)
            step(NJ - 1, True, False)
            last = NJ - 1

            def weights_b(m):
                split_out_weights(1, m, woB_raw, woB_hi, woB_lo)

            odd_queries(last, 1)
            gate_output(last - 1, 3)
            split_early(1, 0)
            shift(last, 0)
            weights_b(1)
            weights_b(3)
            weights_b(5)
            normalise(last, 0)
            shift(last, 1)
            shift(last, 2)
            normalise(last, 1)
            gate_output(last, 0)
            split_early(1, 1)
            weights_b(7)

            split_late(1, 0)
            split_late(1, 1)
            normalise(last, 2)
            shift(last, 3)
            gate_output(last, 1)
            normalise(last, 3)
            gate_output(last, 2)
            dve.wait_ge(S.gain_last_loaded, 16)
            add_y(1, 0, 0, y_last, gain_last)
            split_mixed(1, 2, 0)
            gate_output(last, 3)
            add_y(1, 1, 1, y_last, gain_last)
            split_mixed(1, 3, 1)
            add_y(1, 2, 0, y_last, gain_last)
            with dve.Fori(2, TB // 2) as i:
                split_mixed(1, i * 2, 0)
                add_y(1, i * 2 - 1, 1, y_last, gain_last)
                split_mixed(1, i * 2 + 1, 1)
                add_y(1, i * 2, 0, y_last, gain_last)
            add_y(1, TB - 1, 1, y_last, gain_last)


def shape_constants():
    c = np.arange(P)[:, None]
    q = np.arange(P)[None, :]
    same = c // CHUNK == q // CHUNK
    c_sub, q_sub = c % CHUNK // SUB, q % CHUNK // SUB
    near = same & (c_sub == q_sub) & (c <= q)
    middle = same & (q_sub % 2 == 1) & (c_sub == q_sub - 1)
    score_masks = np.stack([near, middle], axis=1).astype(np.int32)
    heads = KV * 8
    slopes = (2.0 ** (-8.0 * np.arange(1, heads + 1, dtype=np.float32) / heads)).astype(np.float32)
    alibi = np.zeros((2, CHUNK, NJ, 2, 2, 2, CHUNK), np.float32)
    query = np.arange(CHUNK)[:, None]
    key = np.arange(CHUNK)[None, :]
    for odd_chunk in range(2):
        for half in range(2):
            own = half == odd_chunk
            dist = np.abs(query + (0 if own else CHUNK) - key).astype(np.float32)
            for blk in range(2):
                for j in range(NJ):
                    for e in range(2):
                        alibi[blk, :, j, odd_chunk, e, half, :] = -slopes[4 * j + 2 * blk + e] * dist
    return np.eye(P, dtype=np.float32), score_masks, alibi.reshape(P, NJ, 4 * P)


def kernel(**inputs):
    import concourse.bacc as bacc
    from concourse.bass_utils import run_bass_kernel_spmd

    nc = bacc.Bacc("TRN2", target_bir_lowering=False, num_devices=1)
    names = ("x", "norm_pre", "norm_post", "a_w_in", "a_lb_logits", "a_norm", "a_w_out", "b_w_in", "b_sinks",
             "b_w_out")
    arrays = {n: np.ascontiguousarray(inputs[n]) for n in names}
    arrays["identity"], arrays["score_masks"], arrays["alibi"] = shape_constants()
    handles = [nc.dram_tensor(f"in_{n}", a.shape, mybir.dt.from_np(a.dtype), kind="ExternalInput").ap()
               for n, a in arrays.items()]
    out = nc.dram_tensor("out", (1, T, D), F32, kind="ExternalOutput").ap()
    x1_store = nc.dram_tensor("x1_store", (1, T, D), F32).ap()
    build(nc, *handles, out, x1_store)
    result = run_bass_kernel_spmd(nc, [{f"in_{n}": a for n, a in arrays.items()}], core_ids=[0])
    return result.results[0]["out"]
```
